# Optimizing a Trainium2 kernel written in Bass

```python
import jax, jax.numpy as jnp
from jax import lax
import numpy as np

D_MODEL = 1024
BATCH = 1
SEQ = 128
DEPTH = 2
DEC_BATCH = 1
DEC_SEQ = 512
PAST_LEN = 128

GRID_W = 64
EPS = 1e-6
F_MIN = 1e-20
CHUNK = 64
H_A = 8
DK_A = 128
DV_A = D_MODEL // H_A
F_A = H_A * DK_A
DVT_A = H_A * DV_A
HGRN_IN = F_A + DVT_A + F_A + F_A + DVT_A
H_B = 4
DK_B = D_MODEL // 2 // H_B
DV_B = D_MODEL // H_B
KT_B = H_B * DK_B
DVT_B = H_B * DV_B
QKV_B = 2 * KT_B + DVT_B
GLA_RANK = 16
GATE_NORM = 16.0
CONV_K = 3
GLA_IN = QKV_B + DVT_B + 2 * GLA_RANK
P_HEADS = 8
N_KEYS = 128
N_EXPERTS = N_KEYS * N_KEYS
P_TOPK = 16
P_QDIM = 256
P_HALF = P_QDIM // 2
PEER_CHUNK = 128

N_A = (DEPTH + 1) // 2
N_B = DEPTH // 2

kernel_name = "hybrid_hgrn2_gla_peer_diffusion_step"

f32 = jnp.float32

def _rms_norm(x, w):
    xf = x.astype(f32)
    y = xf * lax.rsqrt(jnp.mean(xf * xf, axis=-1, keepdims=True) + EPS)
    return (y * w.astype(f32)).astype(x.dtype)

def _adaln(cvec, w, b):
    mod = jax.nn.silu(cvec) @ w + b
    return jnp.split(mod, 6, axis=-1)

def _modulate(h, shift, scale):
    return h * (1.0 + scale[:, None, :]) + shift[:, None, :]

def _chunk_scan(q, k, v, g, s0):
    b_, L, H, DK = q.shape
    DV = v.shape[-1]
    n = L // CHUNK

    def to_chunks(a):
        return a.astype(f32).reshape(b_, n, CHUNK, H, a.shape[-1]).transpose(1, 0, 3, 2, 4)

    qc, kc, vc, gc = to_chunks(q), to_chunks(k), to_chunks(v), to_chunks(g)
    causal = jnp.tril(jnp.ones((CHUNK, CHUNK), bool))[:, :, None]

    def step(S, inp):
        qi, ki, vi, gi = inp
        bcum = jnp.cumsum(gi, axis=2)
        b_last = bcum[:, :, -1:, :]
        o_inter = jnp.einsum('bhtd,bhde->bhte', qi * jnp.exp(bcum), S)
        diff = bcum[:, :, :, None, :] - bcum[:, :, None, :, :]
        decay = jnp.where(causal, jnp.exp(jnp.minimum(diff, 0.0)), 0.0)
        att = jnp.einsum('bhtd,bhtsd,bhsd->bhts', qi, decay, ki)
        o = o_inter + jnp.einsum('bhts,bhse->bhte', att, vi)
        S = jnp.exp(b_last[:, :, 0, :])[..., None] * S + jnp.einsum(
            'bhsd,bhse->bhde', ki * jnp.exp(b_last - bcum), vi)
        return S, o

    S, o = lax.scan(step, s0.astype(f32), (qc, kc, vc, gc))
    o = o.transpose(1, 0, 3, 2, 4).reshape(b_, L, H, DV)
    return o, S

def _bidirectional_scan(q, v, fwd, bwd):
    k_f, g_f, s_f = fwd
    k_b, g_b, s_b = bwd
    o_f, S_f = _chunk_scan(q, k_f, v, g_f, s_f)
    rev = lambda a: jnp.flip(a, axis=1)
    o_b, S_b = _chunk_scan(rev(q), rev(k_b), rev(v), rev(g_b), s_b)
    return o_f + rev(o_b), S_f, S_b

def _gated_head_norm(o, gate, w):
    of = o.astype(f32)
    y = of * lax.rsqrt(jnp.mean(of * of, axis=-1, keepdims=True) + EPS)
    return y * w.astype(f32) * jax.nn.silu(gate.astype(f32))

def _hgrn2_mixer(h, w_in, lb, gnorm_w, w_out, s_f, s_b):
    b_, L, _ = h.shape
    z = h @ w_in
    q, iv, f_f, f_b, og = jnp.split(
        z, [F_A, F_A + DVT_A, 2 * F_A + DVT_A, 3 * F_A + DVT_A], axis=-1)
    q = jax.nn.silu(q).reshape(b_, L, H_A, DK_A)
    iv = iv.reshape(b_, L, H_A, DV_A)

    def gate(f_pre, lb_d):
        f_pre = f_pre.astype(f32)
        f = lb_d + (1.0 - lb_d) * jax.nn.sigmoid(f_pre)
        log_f = jnp.log(jnp.maximum(f, F_MIN))
        k = (1.0 - lb_d) * jax.nn.sigmoid(-f_pre)
        return k.reshape(b_, L, H_A, DK_A), log_f.reshape(b_, L, H_A, DK_A)

    k_f, g_f = gate(f_f, lb[0])
    k_b, g_b = gate(f_b, lb[1])
    o, S_f, S_b = _bidirectional_scan(q, iv, (k_f, g_f, s_f), (k_b, g_b, s_b))
    o = _gated_head_norm(o, og.reshape(b_, L, H_A, DV_A), gnorm_w)
    return o.reshape(b_, L, DVT_A).astype(h.dtype) @ w_out, S_f, S_b

def _depthwise_conv2d(x, w, rows):
    b_, L, C = x.shape
    xg = x.reshape(b_, rows, L // rows, C)
    y = lax.conv_general_dilated(
        xg, w[:, :, None, :].astype(x.dtype), (1, 1), 'SAME',
        dimension_numbers=('NHWC', 'HWIO', 'NHWC'), feature_group_count=C)
    return y.reshape(b_, L, C)

def _gla_mixer(h, rows, w_in, conv_w, w_gate, b_gate, gnorm_w, w_out, s_f, s_b):
    b_, L, _ = h.shape
    z = h @ w_in
    qkv, og, low = jnp.split(z, [QKV_B, QKV_B + DVT_B], axis=-1)
    qkv = jax.nn.silu(_depthwise_conv2d(qkv, conv_w, rows))
    q, k, v = jnp.split(qkv, [KT_B, 2 * KT_B], axis=-1)
    q = (q * (DK_B ** -0.5)).reshape(b_, L, H_B, DK_B)
    k = k.reshape(b_, L, H_B, DK_B)
    v = v.reshape(b_, L, H_B, DV_B)
    low = low.reshape(b_, L, 2, GLA_RANK)
    gk = jnp.einsum('blnr,nrk->blnk', low, w_gate) + b_gate
    log_g = jax.nn.log_sigmoid(gk.astype(f32)) / GATE_NORM
    g_f = log_g[:, :, 0].reshape(b_, L, H_B, DK_B)
    g_b = log_g[:, :, 1].reshape(b_, L, H_B, DK_B)
    o, S_f, S_b = _bidirectional_scan(q, v, (k, g_f, s_f), (k, g_b, s_b))
    o = _gated_head_norm(o, og.reshape(b_, L, H_B, DV_B), gnorm_w)
    return o.reshape(b_, L, DVT_B).astype(h.dtype) @ w_out, S_f, S_b

def _peer(h, w_q, sub_keys, u_tab, v_tab):
    b_, L, D = h.shape
    blocks = h.reshape(-1, PEER_CHUNK, D)

    def one(hc):
        q = (hc @ w_q).reshape(PEER_CHUNK, P_HEADS, 2, P_HALF)
        s = jnp.einsum('thpk,hpnk->thpn', q, sub_keys).astype(f32)
        s_top, i_top = lax.top_k(s, P_TOPK)
        comb = (s_top[:, :, 0, :, None] + s_top[:, :, 1, None, :]).reshape(
            PEER_CHUNK, P_HEADS, P_TOPK * P_TOPK)
        c_top, c_pos = lax.top_k(comb, P_TOPK)
        idx = (jnp.take_along_axis(i_top[:, :, 0], c_pos // P_TOPK, axis=-1) * N_KEYS
               + jnp.take_along_axis(i_top[:, :, 1], c_pos % P_TOPK, axis=-1))
        gates = jax.nn.softmax(c_top, axis=-1).reshape(PEER_CHUNK, P_HEADS * P_TOPK)
        idx = idx.reshape(PEER_CHUNK, P_HEADS * P_TOPK)
        u = jnp.take(u_tab, idx, axis=0)
        act = jax.nn.gelu(jnp.einsum('td,ted->te', hc, u), approximate=False)
        coef = gates.astype(hc.dtype) * act
        vv = jnp.take(v_tab, idx, axis=0)
        return jnp.einsum('te,ted->td', coef, vv)

    return lax.map(one, blocks).reshape(b_, L, D)

def setup_inputs(seed: int = 0) -> dict:
    key = jax.random.key(seed)
    ks = jax.random.split(key, 26)
    nrm = lambda k, shape, s: jax.random.normal(k, shape, jnp.float32) * s
    return {
        "x_prompt": nrm(ks[0], (BATCH, SEQ, D_MODEL), 1.0),
        "x_sample": nrm(ks[1], (DEC_BATCH, DEC_SEQ, D_MODEL), 1.0),
        "state_hgrn": nrm(ks[2], (DEC_BATCH, N_A, 2, H_A, DK_A, DV_A), 0.5),
        "state_gla": nrm(ks[3], (DEC_BATCH, N_B, 2, H_B, DK_B, DV_B), 1.0),
        "c": nrm(ks[4], (DEC_BATCH, D_MODEL), 1.0),
        "c_ctx": nrm(ks[5], (D_MODEL,), 1.0),
        "ada_w": nrm(ks[6], (DEPTH, D_MODEL, 6 * D_MODEL), 0.5 * D_MODEL ** -0.5),
        "ada_b": nrm(ks[7], (DEPTH, 6 * D_MODEL), 0.02),
        "norm1_w": 1.0 + nrm(ks[8], (DEPTH, D_MODEL), 0.02),
        "norm2_w": 1.0 + nrm(ks[9], (DEPTH, D_MODEL), 0.02),
        "final_norm_w": 1.0 + nrm(ks[10], (D_MODEL,), 0.02),
        "hgrn_w_in": nrm(ks[11], (N_A, D_MODEL, HGRN_IN), D_MODEL ** -0.5),
        "hgrn_lb": nrm(ks[12], (N_A, 2, F_A), 0.5),
        "hgrn_gnorm_w": 1.0 + nrm(ks[13], (N_A, DV_A), 0.02),
        "hgrn_w_out": nrm(ks[14], (N_A, DVT_A, D_MODEL), DVT_A ** -0.5),
        "gla_w_in": nrm(ks[15], (N_B, D_MODEL, GLA_IN), D_MODEL ** -0.5),
        "gla_conv_w": nrm(ks[16], (N_B, CONV_K, CONV_K, QKV_B), 1.0 / CONV_K),
        "gla_w_gate": nrm(ks[17], (N_B, 2, GLA_RANK, KT_B), GLA_RANK ** -0.5),
        "gla_b_gate": nrm(ks[18], (N_B, 2, KT_B), 0.1),
        "gla_gnorm_w": 1.0 + nrm(ks[19], (N_B, DV_B), 0.02),
        "gla_w_out": nrm(ks[20], (N_B, DVT_B, D_MODEL), DVT_B ** -0.5),
        "peer_w_q": nrm(ks[21], (DEPTH, D_MODEL, P_HEADS * P_QDIM), D_MODEL ** -0.5),
        "peer_keys": nrm(ks[22], (DEPTH, P_HEADS, 2, N_KEYS, P_HALF), P_HALF ** -0.5),
        "peer_u": nrm(ks[23], (DEPTH, N_EXPERTS, D_MODEL), D_MODEL ** -0.5),
        "peer_v": nrm(ks[24], (DEPTH, N_EXPERTS, D_MODEL), 0.5),
    }

def reference(x_prompt, x_sample, state_hgrn, state_gla, c, c_ctx, ada_w, ada_b,
              norm1_w, norm2_w, final_norm_w, hgrn_w_in, hgrn_lb, hgrn_gnorm_w,
              hgrn_w_out, gla_w_in, gla_conv_w, gla_w_gate, gla_b_gate, gla_gnorm_w,
              gla_w_out, peer_w_q, peer_keys, peer_u, peer_v):
    rows = x_sample.shape[1] // GRID_W
    bp = x_prompt.shape[0]
    p = jax.nn.softmax(hgrn_lb.astype(f32), axis=0)
    lower_bounds = jnp.cumsum(p, axis=0) - p[0:1]

    xp, xs = x_prompt, x_sample
    new_hgrn, new_gla = [], []
    for l in range(DEPTH):
        j = l // 2
        sh1p, sc1p, g1p, sh2p, sc2p, g2p = _adaln(c_ctx[None, :], ada_w[l], ada_b[l])
        sh1s, sc1s, g1s, sh2s, sc2s, g2s = _adaln(c, ada_w[l], ada_b[l])
        hp = _modulate(_rms_norm(xp, norm1_w[l]), sh1p, sc1p)
        hs = _modulate(_rms_norm(xs, norm1_w[l]), sh1s, sc1s)
        if l % 2 == 0:
            z0 = jnp.zeros((bp, H_A, DK_A, DV_A), f32)
            mp, sf, sb = _hgrn2_mixer(hp, hgrn_w_in[j], lower_bounds[j], hgrn_gnorm_w[j],
                                      hgrn_w_out[j], z0, z0)
            ms, _, _ = _hgrn2_mixer(hs, hgrn_w_in[j], lower_bounds[j], hgrn_gnorm_w[j],
                                    hgrn_w_out[j], state_hgrn[:, j, 0], state_hgrn[:, j, 1])
            new_hgrn.append(jnp.stack([sf, sb], axis=1))
        else:
            z0 = jnp.zeros((bp, H_B, DK_B, DV_B), f32)
            mp, sf, sb = _gla_mixer(hp, 1, gla_w_in[j], gla_conv_w[j], gla_w_gate[j],
                                    gla_b_gate[j], gla_gnorm_w[j], gla_w_out[j], z0, z0)
            ms, _, _ = _gla_mixer(hs, rows, gla_w_in[j], gla_conv_w[j], gla_w_gate[j],
                                  gla_b_gate[j], gla_gnorm_w[j], gla_w_out[j],
                                  state_gla[:, j, 0], state_gla[:, j, 1])
            new_gla.append(jnp.stack([sf, sb], axis=1))
        xp = xp + g1p[:, None, :] * mp
        xs = xs + g1s[:, None, :] * ms
        hp = _modulate(_rms_norm(xp, norm2_w[l]), sh2p, sc2p)
        hs = _modulate(_rms_norm(xs, norm2_w[l]), sh2s, sc2s)
        xp = xp + g2p[:, None, :] * _peer(hp, peer_w_q[l], peer_keys[l], peer_u[l], peer_v[l])
        xs = xs + g2s[:, None, :] * _peer(hs, peer_w_q[l], peer_keys[l], peer_u[l], peer_v[l])

    y_prompt = _rms_norm(xp, final_norm_w)
    y_sample = _rms_norm(xs, final_norm_w)
    new_state_hgrn = jnp.stack(new_hgrn, axis=1).astype(x_prompt.dtype)
    new_state_gla = jnp.stack(new_gla, axis=1).astype(x_prompt.dtype)
    return (y_prompt, y_sample, new_state_hgrn, new_state_gla)


_drawn_inputs = setup_inputs


def setup_inputs(seed=0):
    import zlib

    import numpy as np

    out = dict(_drawn_inputs(seed))
    spreads = {}
    factors = {'state_hgrn': 8.0,
     'state_gla': 5.08,
     'norm2_w': 3.202,
     'final_norm_w': 2.923,
     'hgrn_gnorm_w': 5.205,
     'gla_gnorm_w': 8.0}
    for name, (base, spread) in spreads.items():
        noise = np.random.default_rng([zlib.crc32(name.encode()), seed]).standard_normal(out[name].shape)
        drawn = base * np.exp(spread * noise) if base else spread * noise
        out[name] = __import__('jax').numpy.asarray(drawn.astype(out[name].dtype))
    for name, factor in factors.items():
        out[name] = (out[name] * factor).astype(out[name].dtype)
    return out
```

```python
import numpy as np
from contextlib import ExitStack

import concourse.bass as bass
from concourse import mybir

F32 = mybir.dt.float32
F32R = mybir.dt.float32r
BF16 = mybir.dt.bfloat16
U32 = mybir.dt.uint32
I32 = mybir.dt.int32
ALU = mybir.AluOpType
ACT = mybir.ActivationFunctionType
AX = mybir.AxisListType

P = 128
D = 1024
DC = D // P
TS, TC = 512, 128
T = TS + TC
NT = T // P
HALF = T // 2
GRID_W = 64
ROWS = TS // GRID_W
EPS = 1e-6
F_MIN = 1e-20
LEVELS = [64, 32, 16, 8, 4, 2, 1]
NL = len(LEVELS)
DEPTH = 2
KEYS = 128
TOPK = 16
PH = 8
LN2 = float(np.log(2.0))
LN_LOW = 2.0 ** -40
LN_UP = 2.0 ** 40 - 1.0
LN_FIX = -40.0 * LN2 / LN_UP

VEC = {}


def stage_semaphores(nc, stack, suffix):
    made = []

    def sem(name):
        made.append(nc.alloc_semaphore(f"{name}{suffix}"))
        return made[-1]

    def leave():
        nc.clear_and_free_semaphores(made)
        nc.all_engine_barrier()

    stack.callback(leave)
    return sem


def alone(eng, passed):
    eng.sem_inc(passed, 1)


def halves():
    return [(0, slice(0, HALF)), (1, slice(HALF, T))]


def parts():
    return [(0, slice(0, TS)), (1, slice(TS, T))]


class Mixer:

    def __init__(self, kind):
        self.gla = kind == "gla"
        self.heads = 4 if self.gla else 8
        self.dv = D // self.heads
        self.nv = self.dv // P
        if self.gla:
            self.chunks = [("k", 512, P), ("q", 0, P), ("v0", 1024, 2 * P), ("v1", 1024 + P, 2 * P),
                           ("og0", 2048, 2 * P), ("og1", 2048 + P, 2 * P)]
            self.extra = 2
        else:
            self.chunks = [("ff", 2048, P), ("fb", 3072, P), ("q", 0, P), ("v0", 1024, P), ("og0", 4096, P)]
            self.extra = 0
        self.nch = len(self.chunks)
        self.turns = self.nch + self.extra


def build_program(nc, a, out, upto=99):
    x_sp = nc.dram_tensor("xT_spill", [P, DC, T], F32, kind="Internal").ap()
    og_sp = nc.dram_tensor("og_spill", [DC, P, T], F32, kind="Internal").ap()
    gates_dram = nc.dram_tensor("gates", [KEYS, KEYS, T], F32, kind="Internal").ap()

    ctx = ExitStack()
    with ctx:
        c = {}
        for name, shape, dt in [
            ("ident", [P, P], F32), ("ones_d", [P, P], F32), ("ones_h", [P, P], F32),
            ("level_mask", [P, (NL + 1), P], BF16), ("scan_f", [P, T], BF16), ("scan_b", [P, T], BF16),
            ("vec", [P, 3 * P], F32), ("mod", [P, DEPTH, 48, 2], F32), ("one", [P, 1], F32),
            ("scale_w", [P, DC, 2], F32), ("lb", [P, 16], F32), ("oml", [P, 16], F32),
        ]:
            c[name] = ctx.enter_context(nc.sbuf_tensor(name, shape, dt))
        with nc.sbuf_tensor("xT", [P, DC, T], F32) as xT:
            setup(nc, a, c, xT, x_sp)
        if upto < 1:
            return
        for layer in range(DEPTH):
            mx = Mixer("gla" if layer % 2 else "hgrn")
            with nc.sbuf_tensor(f"h_hi{layer}", [P, DC, T], F32R) as h_hi, \
                    nc.sbuf_tensor(f"h_lo{layer}", [P, DC, T], F32R) as h_lo:
                norm(nc, c, h_hi, h_lo, x_sp, layer, 0)
                with nc.sbuf_tensor(f"oT{layer}", [P, DC, T], F32) as oT:
                    mixer(nc, a, c, mx, h_hi, h_lo, oT, og_sp, out, layer)
                    mix_out(nc, a, c, mx, h_hi, h_lo, oT, og_sp, x_sp, layer)
                if upto < 2 + 2 * layer:
                    return
                norm(nc, c, h_hi, h_lo, x_sp, layer, 1)
                with nc.sbuf_tensor(f"chosen{layer}", [P, 4, PH, NT, TOPK], F32) as chosen:
                    retrieve(nc, a, c, h_hi, h_lo, chosen, layer)
                    route(nc, c, chosen, gates_dram, layer)
                experts(nc, a, c, h_hi, h_lo, x_sp, gates_dram, layer)
                if upto < 3 + 2 * layer:
                    return
        finish(nc, c, x_sp, out)



def vec_rows(a):
    r = lambda ap: ap.rearrange("(n p) -> n p", p=P)
    return [
        ("norm1", a["norm1_w"].rearrange("l (n p) -> (l n) p", p=P), 16),
        ("norm2", a["norm2_w"].rearrange("l (n p) -> (l n) p", p=P), 16),
        ("final", r(a["final_norm_w"]), 8),
        ("lb", a["hgrn_lb"].rearrange("o d (n p) -> (o d n) p", p=P), 16),
        ("hgrn_g", a["hgrn_gnorm_w"].rearrange("o (n p) -> (o n) p", p=P), 1),
        ("gla_g", a["gla_gnorm_w"].rearrange("o (n p) -> (o n) p", p=P), 2),
        ("b_gate", a["gla_b_gate"].rearrange("o d (n p) -> (o d n) p", p=P), 8),
        ("c", a["c"].rearrange("o (n p) -> (o n) p", p=P), 8),
        ("c_ctx", r(a["c_ctx"]), 8),
        ("pad", None, P - 83),
        ("ada_b", a["ada_b"].rearrange("l (n p) -> (l n) p", p=P), 96),
        ("conv8", a["gla_conv_w"].rearrange("o y x (n p) -> (o y x n) p", p=P)[P:P + 16, :], 16),
        ("pad2", None, 16),
        ("conv", a["gla_conv_w"].rearrange("o y x (n p) -> (o y x n) p", p=P)[0:P, :], P),
    ]


def setup(nc, a, c, xT, x_sp):
    NB = 512
    NBL = 6 * D // NB
    with ExitStack() as s:
        sb = lambda n, sh, dt=F32: s.enter_context(nc.sbuf_tensor(n, sh, dt))
        sem = stage_semaphores(nc, s, "")
        rows = sb("param_rows", [P, 3, P])
        xin = sb("xin", [P, NT, D])
        ada = [sb(f"ada{i}", [P, DC, NB]) for i in range(2)]
        cs = sb("cs", [P, 2, DC])
        sg = sb("sg", [P, 2, DC])
        it_p = sb("it_p", [P, P], I32)
        it_f = sb("it_f", [P, P], I32)
        xorf = sb("xorf", [P, P])
        low = sb("low", [P, P])
        l0 = sb("l0", [P, 16])
        l1 = sb("l1", [P, 16])
        pt = [s.enter_context(nc.psum_tensor(f"pt{i}", [P, 4, P], F32)) for i in range(2)]
        pa = [s.enter_context(nc.psum_tensor(f"pa{i}", [P, 512], F32)) for i in range(2)]
        rows_in, x_in, consts, tr, ev, vecs, cready = (sem(n) for n in
            ("rows_in", "x_in", "consts", "tr", "ev", "vecs", "cready"))
        ada_in = [sem(f"ada_in{i}") for i in range(2)]
        ada_mm, mod_done, x_out, iot, sig, rows_z = (sem(n) for n in
            ("ada_mm", "mod_done", "x_out", "iot", "sig", "rows_z"))
        col = 0
        loads = []
        for name, view, n in vec_rows(a):
            VEC[name] = col
            if view is not None:
                loads.append((view, col, n))
            col += n
        block = s.enter_context(nc.Block())
        nload = len(loads)

        @block.sync
        def _(sp):
            sp.wait_ge(rows_z, 1)
            for view, col0, n in loads:
                sp.dma_start(rows[col0 % P:col0 % P + n, col0 // P, :], view).then_inc(rows_in, 16)
            for l in range(DEPTH):
                w = a["ada_w"][l].rearrange("(k p) n -> p k n", p=P)
                with sp.Fori(0, NBL // 2) as i:
                    for b in range(2):
                        sp.wait_ge(ada_mm, i * 2 + (l * NBL + b + 1))
                        sp.dma_start(ada[b][:, :, :], w[:, :, bass.ds(i * (2 * NB) + b * NB, NB)]) \
                            .then_inc(ada_in[b], 16)
            sp.wait_ge(ev, 3 + 40 // 4)
            sp.dma_start(x_sp, xT[:, :, :]).then_inc(x_out, 16)
            sp.wait_ge(x_out, 16)

        @block.gpsimd
        def _(pool):
            pool.memset(rows[:, :, :], 0.0)
            pool.drain().then_inc(rows_z, 1)
            pool.iota(it_p[:, :], [[0, P]], base=0, channel_multiplier=1)
            pool.iota(it_f[:, :], [[1, P]], base=0, channel_multiplier=0)
            pool.memset(c["ident"][:, :], 0.0)
            pool.memset(c["ones_d"][:, :], 1.0 / D)
            pool.memset(c["one"][:, :], 1.0)
            pool.memset(c["scan_f"][:, :], 1.0)
            pool.memset(c["scan_b"][:, :], 1.0)
            pool.drain()
            pool.affine_select(out=c["ident"][:, :], in_=c["ident"][:, :], compare_op=ALU.not_equal,
                               fill=1.0, base=0, pattern=[[-1, P]], channel_multiplier=1)
            pool.memset(c["scan_f"][:, :].rearrange("p (n t) -> p n t", t=P)[:, :, 0:1], 0.0)
            pool.memset(c["scan_b"][:, :].rearrange("p (n t) -> p n t", t=P)[:, :, P - 1:P], 0.0)
            pool.drain().then_inc(iot, 1)

        @block.scalar
        def _(act):
            act.dma_start(xin[:, 0:NT - 1, :], a["x_sample"].rearrange("o (n p) d -> p (o n) d", p=P)) \
                .then_inc(x_in, 16)
            act.dma_start(xin[:, NT - 1, :], a["x_prompt"].rearrange("o p d -> (o p) d")).then_inc(x_in, 16)
            for g in range(3 + 10):
                act.wait_ge(tr, g + 1)
                if g < 3:
                    act.activation(c["vec"][:, g * P:(g + 1) * P], pt[g % 2][:, 0, :], ACT.Copy).then_inc(ev, 1)
                else:
                    q = g - 3
                    t, k = q // 2, 4 * (q % 2)
                    act.activation(xT[:, k:k + 4, t * P:(t + 1) * P], pt[g % 2][:, :, :], ACT.Copy).then_inc(ev, 1)
            act.wait_ge(ev, 3)
            for v, name in ((0, "c"), (1, "c_ctx")):
                act.activation(sg[:, v, :], c["vec"][:, VEC[name]:VEC[name] + DC], ACT.Sigmoid)
            act.drain().then_inc(sig, 1)

        @block.vector
        def _(dve):
            dve.wait_ge(iot, 1)
            nc.vector.tensor_tensor(it_p[:, :], it_p[:, :], it_f[:, :], ALU.bitwise_xor)
            dve.drain()
            nc.vector.tensor_copy(xorf[:, :], it_p[:, :])
            dve.drain()
            for l, m in enumerate(LEVELS):
                nc.vector.tensor_scalar(low[:, :], xorf[:, :], float(m), None, ALU.is_ge)
                dve.drain()
                nc.vector.scalar_tensor_tensor(c["level_mask"][:, l, :], xorf[:, :], float(2 * m), low[:, :],
                                               ALU.is_lt, ALU.mult)
                dve.drain()
            nc.vector.tensor_scalar(c["level_mask"][:, NL, :], xorf[:, :], 0.0, None, ALU.is_equal)
            dve.wait_ge(ev, 3)
            lbr = c["vec"][:, VEC["lb"]:VEC["lb"] + 16]
            nc.vector.tensor_sub(l0[:, :], lbr, lbr)
            dve.drain().then_inc(vecs, 1)
            dve.wait_ge(vecs, 2)
            nc.vector.reciprocal(l1[:, :], l0[:, :])
            dve.drain()
            nc.vector.tensor_mul(l1[:, :], l0[:, :], l1[:, :])
            dve.drain()
            nc.vector.tensor_sub(c["lb"][:, :], l1[:, :], l1[:, :])
            dve.drain()
            nc.vector.tensor_scalar(c["oml"][:, :], c["lb"][:, :], -1.0, 1.0, ALU.mult, ALU.add)
            dve.wait_ge(sig, 1)
            for v, name in ((0, "c"), (1, "c_ctx")):
                nc.vector.tensor_mul(cs[:, v, :], sg[:, v, :], c["vec"][:, VEC[name]:VEC[name] + DC])
            dve.drain().then_inc(cready, 1)
            for l in range(DEPTH):
                bias = c["vec"][:, VEC["ada_b"] + 48 * l:VEC["ada_b"] + 48 * l + 48]
                for v in range(2):
                    dve.wait_ge(ada_mm, 2 + NBL * (l + 1))
                    nc.vector.tensor_add(c["mod"][:, l, :, v], pa[l][:, 0:96].rearrange("p (n v) -> p n v", v=2)[:, :, v],
                                         bias)
            dve.drain().then_inc(mod_done, 1)

        @block.scalar
        def _(act):
            act.wait_ge(vecs, 1)
            act.activation(l0[:, :], l0[:, :], ACT.Exp)
            act.drain().then_inc(vecs, 1)

        @block.tensor
        def _(pe):
            pe.sem_inc(ada_mm, 2)
            pe.wait_ge(iot, 1)
            pe.wait_ge(rows_in, 16 * nload)
            for g in range(3 + 10):
                if g >= 2:
                    pe.wait_ge(ev, g - 1)
                if g < 3:
                    last = nc.tensor.transpose(pt[g % 2][:, 0, :], rows[:, g, :], c["ident"][:, :])
                else:
                    if g == 3:
                        pe.wait_ge(x_in, 32)
                    q = g - 3
                    for k in range(4):
                        kk = 4 * (q % 2) + k
                        last = nc.tensor.transpose(pt[g % 2][:, k, :], xin[:, q // 2, kk * P:(kk + 1) * P],
                                                   c["ident"][:, :])
                last.then_inc(tr, 1)
            pe.wait_ge(cready, 1)
            for l in range(DEPTH):
                with pe.Fori(0, NBL // 2) as i:
                    for b in range(2):
                        pe.wait_ge(ada_in[b], i * 16 + (16 * (l * NBL // 2) + 16))
                        for n in range(NB // P):
                            for k in range(DC):
                                dst = pa[l][:, bass.ds(i * (4 * NB // P) + (2 * (b * NB // P + n)), 2)]
                                last = nc.tensor.matmul(dst, ada[b][:, k, n * P:(n + 1) * P], cs[:, :, k],
                                                        start=(k == 0), stop=(k == DC - 1))
                        last.then_inc(ada_mm, 1)


def norm(nc, c, h_hi, h_lo, x_sp, layer, which):
    with ExitStack() as s:
        sb = lambda n, sh, dt=F32: s.enter_context(nc.sbuf_tensor(f"{n}_n{layer}{which}", sh, dt))
        sem = stage_semaphores(nc, s, f"_n{layer}{which}")
        xT = sb("x", [P, DC, T])
        sq = [sb(f"sq{i}", [P, T]) for i in range(2)]
        rs = sb("rs", [P, T])
        y = [sb(f"y{i}", [P, T]) for i in range(2)]
        ms = [s.enter_context(nc.psum_tensor(f"ms{i}_n{layer}{which}", [P, 512], F32)) for i in range(2)]
        x_in, sq_done, summed, inv, rooted, hi_done, y_done, lo_done = (sem(n) for n in
            ("x_in", "sq_done", "summed", "inv", "rooted", "hi_done", "y_done", "lo_done"))
        block = s.enter_context(nc.Block())
        w0 = VEC["norm2" if which else "norm1"] + 8 * layer
        sh, sc = 24 * which, 24 * which + 8

        @block.sync
        def _(sp):
            sp.dma_start(xT[:, :, :], x_sp).then_inc(x_in, 16)

        @block.scalar
        def _(act):
            act.wait_ge(x_in, 16)
            for k in range(DC):
                if k >= 2:
                    act.wait_ge(summed, k - 1)
                act.activation(sq[k % 2][:, :], xT[:, k, :], ACT.Square).then_inc(sq_done, 1)
            act.wait_ge(inv, 1)
            act.activation(rs[:, :], rs[:, :], ACT.Sqrt).then_inc(rooted, 1)
            for k in range(DC):
                act.wait_ge(y_done, k + 1)
                act.activation(h_hi[:, k, :], y[k % 2][:, :], ACT.Copy).then_inc(hi_done, 1)

        @block.tensor
        def _(pe):
            for k in range(DC):
                pe.wait_ge(sq_done, k + 1)
                for i, cols in halves():
                    last = nc.tensor.matmul(ms[i][:, 0:HALF], c["ones_d"][:, :], sq[k % 2][:, cols],
                                            start=(k == 0), stop=(k == DC - 1))
                last.then_inc(summed, 1)

        @block.vector
        def _(dve):
            for v in range(2):
                nc.vector.scalar_tensor_tensor(c["scale_w"][:, :, v], c["mod"][:, layer, sc:sc + DC, v], 1.0,
                                               c["vec"][:, w0:w0 + DC], ALU.add, ALU.mult)
            dve.wait_ge(summed, DC)
            for i, cols in halves():
                nc.vector.tensor_scalar(rs[:, cols], ms[i][:, 0:HALF], EPS, None, ALU.add)
            dve.drain()
            nc.vector.reciprocal(rs[:, :], rs[:, :])
            dve.drain().then_inc(inv, 1)
            dve.wait_ge(rooted, 1)

            def modulate(k):
                nc.vector.tensor_mul(y[k % 2][:, :], xT[:, k, :], rs[:, :])
                dve.drain()
                for v, cols in parts():
                    nc.vector.tensor_scalar(y[k % 2][:, cols], y[k % 2][:, cols], c["scale_w"][:, k, v:v + 1],
                                            c["mod"][:, layer, sh + k, v:v + 1], ALU.mult, ALU.add)
                dve.drain().then_inc(y_done, 1)

            modulate(0)
            for k in range(DC):
                if k + 1 < DC:
                    modulate(k + 1)
                dve.wait_ge(hi_done, k + 1)
                nc.vector.tensor_sub(h_lo[:, k, :], y[k % 2][:, :], h_hi[:, k, :].bitcast(F32))
                dve.drain()


def split_product(nc, psum, w_hi, w_lo, x_hi, x_lo, cols):
    for k in range(DC):
        for w, x in ((w_hi, x_hi), (w_hi, x_lo), (w_lo, x_hi)):
            last = nc.tensor.matmul(psum, w[:, k, :], x[:, k, cols], start=(k == 0 and w is w_hi and x is x_hi),
                                    stop=(k == DC - 1 and w is w_lo))
    return last


def mixer(nc, a, c, mx, h_hi, h_lo, oT, og_sp, out, layer):
    NV, DV, NCH, TURNS, H = mx.nv, mx.dv, mx.nch, mx.turns, mx.heads
    w_in = a["gla_w_in" if mx.gla else "hgrn_w_in"][0].rearrange("(k p) n -> p k n", p=P)
    s0 = a["state_gla" if mx.gla else "state_hgrn"][0, 0]
    s_new = out[3 if mx.gla else 2][0, 0]
    NTR = 10 + NT * NV
    NG = (NTR + 3) // 4
    KVR = 4 // NV
    WITH_STATE = [(0, 0), (0, 1), (0, 2), (0, 4), (1, 3), (1, 2), (1, 1), (1, 4)]
    tag = "gla" if mx.gla else "hgrn"
    with ExitStack() as s:
        sb = lambda n, sh, dt=F32: s.enter_context(nc.sbuf_tensor(f"{n}_{tag}", sh, dt))
        sem = stage_semaphores(nc, s, f"_{tag}")
        ps = lambda n, sh: s.enter_context(nc.psum_tensor(f"{n}_{tag}", sh, F32))
        w_raw = [sb(f"w_raw{i}", [P, DC, P]) for i in range(2)]
        w_hi = [sb(f"w_hi{i}", [P, DC, P], F32R) for i in range(2)]
        w_lo = [sb(f"w_lo{i}", [P, DC, P], F32R) for i in range(2)]
        zc = sb("zc", [P, 2, T])
        q = sb("q", [P, T])
        k2 = sb("k2", [P, 2, T])
        g2 = sb("g2", [P, 2, T])
        t2 = sb("t2", [P, 2, T])
        b2 = sb("b2", [P, 2, T])
        e2 = sb("e2", [P, 2, T])
        kd = sb("kdiag", [P, T])
        v = sb("v", [P, NV, T])
        og = sb("og", [P, NV, T])
        ex = sb("ex", [P, 2, NL, T])
        am = [sb(f"am{i}", [P, NL + 1, P]) for i in range(2)]
        tt = sb("tt", [P, NG * 4, P])
        S = sb("S", [P, 2, NT, DV])
        ebl = sb("ebl", [P, 2, NT])
        pp = [ps(f"pp{i}", [P, 512]) for i in range(2)]
        pA = [ps(f"pA{i}", [P, NL + 1, P]) for i in range(2)]
        pX = ps("pX", [P, 4, P])
        pO = ps("pO", [P, 4, P])
        (w_hi_done, w_lo_done, proj, copied, f_ready, ln_done, b_ready, diff_done, e_ready, exp_done, qk_ready,
         ex_ready, turned, turned_out, kv, s_done, att, masked, o_done, o_out, s_in, s_out, og_done, og_out) = (
            sem(n) for n in ("w_hi_done", "w_lo_done", "proj", "copied", "f_ready", "ln_done", "b_ready",
                             "diff_done", "e_ready", "exp_done", "qk_ready", "ex_ready", "turned", "turned_out",
                             "kv", "s_done", "att", "masked", "o_done", "o_out", "s_in", "s_out", "og_done",
                             "og_out"))
        weighted, sp_passed, act_passed = sem("weighted"), sem("sp_passed"), sem("act_passed")
        w_loaded = [sem(f"w_loaded{i}") for i in range(2)]
        if mx.gla:
            wg = sb("wg", [P, 2, P])
            lowT = sb("lowT", [P, T])
            wg_in, wg_zero, conv_done, sig_done, low_done, silu_done = (sem(n) for n in
                ("wg_in", "wg_zero", "conv_done", "sig_done", "low_done", "silu_done"))
        block = s.enter_context(nc.Block())
        PRE = 1 if mx.gla else 0
        per_buf = [len([j for j in range(NCH) if j % 2 == b]) for b in range(2)]

        def loaded_value(h, j):
            return h * (16 * per_buf[j % 2]) + (16 * (j // 2 + 1) + (16 * PRE if j % 2 == 0 else 0))

        def split_free(h, j):
            return h * NCH + (2 + PRE + (j - 1 if j >= 2 else 0))

        @block.sync
        def _(sp):
            sp.sem_inc(s_out, 32)
            sp.sem_inc(og_out, 16)
            if mx.gla:
                sp.dma_start(w_raw[0][:, :, :], w_in[:, :, 3104 - P:3104]).then_inc(w_loaded[0], 16)
            with sp.Fori(0, H) as h:
                sp.wait_ge(o_done, h * NT + 1)
                if mx.gla:
                    sp.wait_ge(wg_zero, 1)
                    for d in range(2):
                        sp.dma_start(wg[96 + 16 * d:112 + 16 * d, d, :],
                                     a["gla_w_gate"][0, d][:, bass.ds(h * P, P)]).then_inc(wg_in, 16)
                alone(sp, sp_passed)
                sp.wait_ge(s_out, h * 32 + 32)
                sp.dma_start(S[:, 0, 0, :], s0[0][bass.ds(h, 1)].rearrange("o p v -> p (o v)")).then_inc(s_in, 16)
                sp.dma_start(S[:, 1, 3, :], s0[1][bass.ds(h, 1)].rearrange("o p v -> p (o v)")).then_inc(s_in, 16)
                for j, (_, col0, step) in enumerate(mx.chunks):
                    sp.wait_ge(w_lo_done, split_free(h, j))
                    alone(sp, sp_passed)
                    sp.dma_start(w_raw[j % 2][:, :, :], w_in[:, :, bass.ds(h * step + col0, P)]) \
                        .then_inc(w_loaded[j % 2], 16)
                sp.wait_ge(og_done, h + 1)
                sp.dma_start(og_sp[bass.ds(h * NV, NV)].rearrange("n p t -> p n t"), og[:, :, :]).then_inc(og_out, 16)
                sp.wait_ge(s_done, h * 8 + 8)
                for d in range(2):
                    sp.dma_start(s_new[d][bass.ds(h, 1)].rearrange("o p v -> p (o v)"), S[:, d, 4, :]) \
                        .then_inc(s_out, 16)
            sp.wait_ge(s_out, 32 * H + 32)
            sp.wait_ge(og_out, 16 * H + 16)

        @block.gpsimd
        def _(pool):
            pool.sem_inc(w_lo_done, 2)

            def lo(h, j):
                pool.wait_ge(w_hi_done, h * NCH + (j + 1 + PRE))
                b = j % 2
                pool.tensor_tensor(w_lo[b][:, :, :], w_raw[b][:, :, :], w_hi[b][:, :, :].bitcast(F32),
                                   ALU.subtract).then_inc(w_lo_done, 1)

            if mx.gla:
                pool.memset(wg[:, :, :], 0.0)
                pool.drain().then_inc(wg_zero, 1)
                pool.wait_ge(w_hi_done, 1)
                pool.tensor_tensor(w_lo[0][:, :, :], w_raw[0][:, :, :], w_hi[0][:, :, :].bitcast(F32),
                                   ALU.subtract).then_inc(w_lo_done, 1)
            with pool.Fori(0, H) as h:
                for j in range(NCH):
                    lo(h, j)
                pool.wait_ge(b_ready, h + 1)
                for l, m in enumerate(LEVELS):
                    nb = T // (2 * m)
                    bf, bb, qs, ks = (x.rearrange("p (n h m) -> p n h m", h=2, m=m) for x in
                                      (b2[:, 0, :], b2[:, 1, :], ex[:, 0, l, :], ex[:, 1, l, :]))
                    rf = bf[:, :, 0, m - 1:m].to_broadcast([P, nb, m])
                    rb = bb[:, :, 1, 0:1].to_broadcast([P, nb, m])
                    pool.tensor_tensor(qs[:, :, 1, :], bf[:, :, 1, :], rf, ALU.subtract)
                    pool.tensor_tensor(ks[:, :, 0, :], rf, bf[:, :, 0, :], ALU.subtract)
                    pool.tensor_tensor(qs[:, :, 0, :], bb[:, :, 0, :], rb, ALU.subtract)
                    pool.tensor_tensor(ks[:, :, 1, :], rb, bb[:, :, 1, :], ALU.subtract)
                    pool.drain().then_inc(diff_done, 1)

        @block.scalar
        def _(act):
            act.sem_inc(copied, 2)
            act.sem_inc(o_out, 1)

            def hi(b, loaded, used):
                act.wait_ge(w_loaded[b], loaded)
                act.wait_ge(proj, used)
                act.activation(w_hi[b][:, :, :], w_raw[b][:, :, :], ACT.Copy).then_inc(w_hi_done, 1)

            def used(h, j):
                if j >= 2:
                    t = turn_of(j - 2) + 1
                    return h * (2 * TURNS) + (2 + 2 * (t + PRE))
                return h * (2 * TURNS) + (2 + 2 * PRE)

            def turn_of(j):
                return j + (2 if mx.gla and j >= 4 else 0)

            def copy(dst, turn, h, func=ACT.Copy, scale=1.0, also=None, bias=None):
                for i, cols in halves():
                    act.wait_ge(proj, h * (2 * TURNS) + (2 + 2 * (turn + PRE) + i + 1))
                    if bias is not None:
                        alone(act, act_passed)
                    kw = {"bias": bias} if bias is not None else {}
                    if also is not None:
                        act.activation(also[0][:, cols], pp[i][:, 0:HALF], also[1], scale=also[2])
                    act.activation(dst[:, cols], pp[i][:, 0:HALF], func, scale=scale, **kw).then_inc(copied, 1)

            if mx.gla:
                hi(0, 16, 2)
                for i, cols in halves():
                    act.wait_ge(proj, 2 + i + 1)
                    act.activation(lowT[:, cols], pp[i][:, 0:HALF], ACT.Copy).then_inc(copied, 1)
            with act.Fori(0, H) as h:
                hi(0, loaded_value(h, 0), used(h, 0))
                hi(1, loaded_value(h, 1), used(h, 1))
                act.wait_ge(o_done, h * NT + 1)
                act.wait_ge(og_out, h * 16 + 16)
                if mx.gla:
                    dests = [k2[:, 0, :], q[:, :], v[:, 0, :], v[:, 1, :]]

                    def sig(j):
                        act.wait_ge(conv_done, h * 4 + (j + 1))
                        act.activation(t2[:, j % 2, :], dests[j], ACT.Sigmoid).then_inc(sig_done, 1)

                    for j in range(4):
                        copy(zc[:, j % 2, :], j, h)
                        if j + 2 < NCH:
                            hi(j % 2, loaded_value(h, j + 2), used(h, j + 2))
                        if j >= 1:
                            sig(j - 1)
                    sig(3)
                    for d in range(2):
                        bg = VEC["b_gate"] + 4 * d
                        copy(g2[:, d, :], 4 + d, h, ACT.Identity,
                             bias=c["vec"][:, bass.ds(h + bg, 1)])
                    for j in (4, 5):
                        copy(og[:, j - 4, :], j + 2, h)
                    act.drain().then_inc(og_done, 1)
                    act.wait_ge(silu_done, h + 1)
                    act.activation(t2[:, :, :], g2[:, :, :], ACT.Abs)
                    act.drain()
                    act.activation(t2[:, :, :], t2[:, :, :], ACT.Exp, scale=-1.0)
                    act.drain()
                    act.activation(t2[:, :, :], t2[:, :, :], ACT.Ln, bias=c["one"][:, 0:1])
                    act.drain().then_inc(ln_done, 1)
                else:
                    for j in range(2):
                        copy(g2[:, j, :], j, h, ACT.Sigmoid, also=(k2[:, j, :], ACT.Sigmoid, -1.0))
                        hi(j % 2, loaded_value(h, j + 2), used(h, j + 2))
                    copy(zc[:, 0, :], 2, h, also=(zc[:, 1, :], ACT.Sigmoid, 1.0))
                    hi(0, loaded_value(h, 4), used(h, 4))
                    copy(v[:, 0, :], 3, h)
                    copy(og[:, 0, :], 4, h)
                    act.drain().then_inc(og_done, 1)
                    act.wait_ge(f_ready, h + 1)
                    act.activation(t2[:, :, :], t2[:, :, :], ACT.Ln).then_inc(ln_done, 1)
                act.wait_ge(e_ready, h + 1)
                act.activation(e2[:, :, :], b2[:, :, :], ACT.Exp)
                act.activation(t2[:, :, :], t2[:, :, :], ACT.Exp)
                act.drain().then_inc(exp_done, 1)
                for g in range(NG):
                    n = min(4, NTR - 4 * g)
                    act.wait_ge(turned, h * NG + (g + 1))
                    act.activation(tt[:, 4 * g:4 * g + n, :], pX[:, 0:n, :], ACT.Copy).then_inc(turned_out, 1)
                for l in range(NL):
                    act.wait_ge(diff_done, h * NL + (l + 1))
                    act.activation(ex[:, :, l, :], ex[:, :, l, :], ACT.Exp).then_inc(ex_ready, 1)
                for t in range(NT):
                    act.wait_ge(o_done, h * NT + (1 + t + 1))
                    act.activation(oT[:, bass.ds(h * NV, NV), t * P:(t + 1) * P],
                                   pO[:, 0:NV, :], ACT.Copy).then_inc(o_out, 1)

        @block.vector
        def _(dve):
            def conv(h, j, dst, tap0, zsl):
                nc.vector.tensor_scalar(dst, zsl, tap_ap(h, 1, 1, tap0), None, ALU.mult)
                dve.drain()
                gz = zsl[:, 0:TS].rearrange("p (r w) -> p r w", w=GRID_W)
                gd = dst[:, 0:TS].rearrange("p (r w) -> p r w", w=GRID_W)
                for y in range(3):
                    for x in range(3):
                        if (y, x) == (1, 1):
                            continue
                        r0, r1 = max(0, 1 - y), min(ROWS, ROWS + 1 - y)
                        w0, w1 = max(0, 1 - x), min(GRID_W, GRID_W + 1 - x)
                        if y == 1:
                            u0, u1 = TS + max(0, 1 - x), TS + min(TC, TC + 1 - x)
                            nc.vector.scalar_tensor_tensor(dst[:, u0:u1], zsl[:, u0 + x - 1:u1 + x - 1],
                                                           tap_ap(h, y, x, tap0), dst[:, u0:u1], ALU.mult, ALU.add)
                        nc.vector.scalar_tensor_tensor(
                            gd[:, r0:r1, w0:w1], gz[:, r0 + y - 1:r1 + y - 1, w0 + x - 1:w1 + x - 1],
                            tap_ap(h, y, x, tap0), gd[:, r0:r1, w0:w1], ALU.mult, ALU.add)
                        dve.drain()

            def tap_ap(h, y, x, tap0):
                n = 3 * y + x
                first = (VEC["conv"] + 16 * n if n < 8 else VEC["conv8"]) + tap0[0]
                return c["vec"][:, bass.ds(h * tap0[1] + first, 1)]

            dve.sem_inc(masked, 1)
            with dve.Fori(0, H) as h:
                if mx.gla:
                    dests = [k2[:, 0, :], q[:, :], v[:, 0, :], v[:, 1, :]]
                    where = [(4, 1), (0, 1), (8, 2), (9, 2)]
                    scales = [1.0, float(P) ** -0.5, 1.0, 1.0]

                    def silu(j):
                        dve.wait_ge(sig_done, h * 4 + (j + 1))
                        nc.vector.scalar_tensor_tensor(dests[j], dests[j], scales[j], t2[:, j % 2, :],
                                                       ALU.mult, ALU.mult)

                    for j in range(4):
                        dve.wait_ge(copied, h * (2 * TURNS) + (2 + 2 * (j + 1 + PRE)))
                        conv(h, j, dests[j], where[j], zc[:, j % 2, :])
                        dve.drain().then_inc(conv_done, 1)
                        if j >= 1:
                            silu(j - 1)
                            dve.drain()
                    silu(3)
                    dve.drain().then_inc(silu_done, 1)
                    dve.wait_ge(ln_done, h + 1)
                    nc.vector.scalar_tensor_tensor(g2[:, :, :], g2[:, :, :], 0.0, t2[:, :, :], ALU.min, ALU.subtract)
                    dve.drain()
                    nc.vector.tensor_scalar(g2[:, :, :], g2[:, :, :], 1.0 / 16.0, None, ALU.mult)
                    nc.vector.tensor_scalar(kd[:, :], k2[:, 0, :], 2.0, None, ALU.mult)
                    nc.vector.tensor_copy(k2[:, 1, :], k2[:, 0, :])
                    dve.drain()
                else:
                    dve.wait_ge(copied, h * (2 * TURNS) + (2 + 4))
                    for d in range(2):
                        oml = c["oml"][:, bass.ds(h + 8 * d, 1)]
                        nc.vector.tensor_scalar(t2[:, d, :], g2[:, d, :], oml, c["lb"][:, bass.ds(h + 8 * d, 1)],
                                                ALU.mult, ALU.add)
                        nc.vector.tensor_scalar(k2[:, d, :], k2[:, d, :], oml, None, ALU.mult)
                    dve.drain()
                    nc.vector.tensor_scalar(t2[:, :, :], t2[:, :, :], F_MIN, None, ALU.max)
                    dve.drain()
                    nc.vector.tensor_scalar(g2[:, :, :], t2[:, :, :], LN_LOW, LN_UP, ALU.is_lt, ALU.mult)
                    dve.drain()
                    nc.vector.scalar_tensor_tensor(t2[:, :, :], g2[:, :, :], 1.0, t2[:, :, :], ALU.add, ALU.mult)
                    dve.drain().then_inc(f_ready, 1)
                    nc.vector.tensor_add(kd[:, :], k2[:, 0, :], k2[:, 1, :])
                    dve.wait_ge(copied, h * (2 * TURNS) + (2 + 6))
                    nc.vector.tensor_mul(q[:, :], zc[:, 0, :], zc[:, 1, :])
                    dve.wait_ge(ln_done, h + 1)
                    nc.vector.scalar_tensor_tensor(g2[:, :, :], g2[:, :, :], LN_FIX, t2[:, :, :], ALU.mult, ALU.add)
                    dve.drain()
                nc.vector.tensor_tensor_scan(b2[:, 0, :], c["scan_f"][:, :], g2[:, 0, :], 0.0, ALU.mult, ALU.add)
                nc.vector.tensor_tensor_scan(b2[:, 1, ::-1], c["scan_b"][:, ::-1], g2[:, 1, ::-1], 0.0,
                                             ALU.mult, ALU.add)
                dve.drain().then_inc(b_ready, 1)
                for d, e in ((0, P - 1), (1, 0)):
                    bv = b2[:, d, :].rearrange("p (n t) -> p n t", t=P)
                    nc.vector.tensor_tensor(t2[:, d, :].rearrange("p (n t) -> p n t", t=P),
                                            bv[:, :, e:e + 1].to_broadcast([P, NT, P]), bv, ALU.subtract)
                dve.drain().then_inc(e_ready, 1)
                dve.wait_ge(exp_done, h + 1)
                for d, e in ((0, P - 1), (1, 0)):
                    nc.vector.tensor_copy(ebl[:, d, :], e2[:, d, :].rearrange("p (n t) -> p n t", t=P)[:, :, e])
                dve.drain()
                for d in range(2):
                    nc.vector.tensor_mul(e2[:, d, :], e2[:, d, :], q[:, :])
                    nc.vector.tensor_mul(t2[:, d, :], t2[:, d, :], k2[:, d, :])
                dve.drain().then_inc(qk_ready, 1)
                dve.wait_ge(s_in, h * 32 + 32)
                for i, (d, t) in enumerate(WITH_STATE):
                    dve.wait_ge(kv, h * 8 + (i // KVR + 1) * KVR)
                    r = (i % KVR) * NV
                    if t == NT - 1:
                        nc.vector.tensor_copy(S[:, d, t, :], pX[:, r:r + NV, :].rearrange("p a b -> p (a b)"))
                    else:
                        nxt = t + 1 if d == 0 else t - 1
                        nc.vector.scalar_tensor_tensor(S[:, d, nxt, :], S[:, d, t, :], ebl[:, d, t:t + 1],
                                                       pX[:, r:r + NV, :].rearrange("p a b -> p (a b)"),
                                                       ALU.mult, ALU.add)
                    dve.drain().then_inc(s_done, 1)
                for l, m in enumerate(LEVELS):
                    dve.wait_ge(ex_ready, h * NL + (l + 1))
                    nc.vector.tensor_mul(ex[:, 0, l, :], ex[:, 0, l, :], q[:, :])
                    for d in range(2):
                        kv_ = k2[:, d, :].rearrange("p (n h m) -> p n h m", h=2, m=m)[:, :, d, :]
                        ks = ex[:, 1, l, :].rearrange("p (n h m) -> p n h m", h=2, m=m)[:, :, d, :]
                        nc.vector.tensor_mul(ks, ks, kv_)
                dve.drain().then_inc(weighted, 1)
                for t in range(NT):
                    dve.wait_ge(att, h * NT + (t + 1))
                    dve.wait_ge(o_done, h * NT + (1 + (t - 1 if t >= 2 else 0)))
                    nc.vector.tensor_mul(am[t % 2][:, :, :], pA[t % 2][:, :, :], c["level_mask"][:, :, :]) \
                        .then_inc(masked, 1)

        @block.tensor
        def _(pe):
            pe.sem_inc(proj, 2)
            pe.sem_inc(o_done, 1)
            if mx.gla:
                pe.wait_ge(w_lo_done, 2 + 1)
                for i, cols in halves():
                    split_product(nc, pp[i][:, 0:HALF], w_hi[0], w_lo[0], h_hi, h_lo, cols).then_inc(proj, 1)
            with pe.Fori(0, H) as h:
                def free(turn, i):
                    pe.wait_ge(copied, h * (2 * TURNS) + (2 + 2 * (turn + PRE) - (1 - i if turn else 0)))

                turn = 0
                for j in range(NCH):
                    if mx.gla and j == 4:
                        pe.wait_ge(wg_in, h * 32 + 32)
                        for d in range(2):
                            for i, cols in halves():
                                free(turn, i)
                                nc.tensor.matmul(pp[i][:, 0:HALF], wg[96:128, d, :], lowT[96:128, cols],
                                                 start=True, stop=True).then_inc(proj, 1)
                            turn += 1
                    pe.wait_ge(w_lo_done, h * NCH + (2 + j + 1 + PRE))
                    for i, cols in halves():
                        free(turn, i)
                        split_product(nc, pp[i][:, 0:HALF], w_hi[j % 2], w_lo[j % 2], h_hi, h_lo, cols) \
                            .then_inc(proj, 1)
                    turn += 1
                pe.wait_ge(qk_ready, h + 1)
                for g in range(NG):
                    if g:
                        pe.wait_ge(turned_out, h * NG + g)
                    for r in range(min(4, NTR - 4 * g)):
                        n = 4 * g + r
                        if n < 10:
                            src = t2[:, n // NT, (n % NT) * P:(n % NT + 1) * P]
                        else:
                            t, vv = (n - 10) // NV, (n - 10) % NV
                            src = v[:, vv, t * P:(t + 1) * P]
                        last = nc.tensor.transpose(pX[:, r, :], src, c["ident"][:, :])
                    last.then_inc(turned, 1)
                pe.wait_ge(turned_out, h * NG + NG)
                for i, (d, t) in enumerate(WITH_STATE):
                    if i >= KVR and i % KVR == 0:
                        pe.wait_ge(s_done, h * 8 + i)
                    r = (i % KVR) * NV
                    nc.tensor.matmul(pX[:, r:r + NV, :], tt[:, d * NT + t, :],
                                     tt[:, 10 + t * NV:10 + t * NV + NV, :], start=True, stop=True).then_inc(kv, 1)
                pe.wait_ge(weighted, h + 1)
                pe.wait_ge(s_done, h * 8 + 8)

                def scores(t):
                    pe.wait_ge(masked, h * NT + (1 + (t - 1 if t >= 2 else 0)))
                    tok = slice(t * P, (t + 1) * P)
                    for l in range(NL):
                        nc.tensor.matmul(pA[t % 2][:, l, :], ex[:, 1, l, tok], ex[:, 0, l, tok], start=True, stop=True)
                    nc.tensor.matmul(pA[t % 2][:, NL, :], kd[:, tok], q[:, tok], start=True, stop=True) \
                        .then_inc(att, 1)

                scores(0)
                for t in range(NT):
                    if t + 1 < NT:
                        scores(t + 1)
                    pe.wait_ge(masked, h * NT + (1 + t + 1))
                    pe.wait_ge(o_out, h * NT + (1 + t))
                    tok = slice(t * P, (t + 1) * P)
                    for vv in range(NV):
                        dst = pO[:, vv, :]
                        terms = [(tt[:, 10 + t * NV + vv, :], am[t % 2][:, l, :]) for l in range(NL + 1)]
                        if t < NT - 1:
                            terms += [(S[:, d, t, vv * P:(vv + 1) * P], e2[:, d, tok]) for d in range(2)]
                        for n, (lhsT, rhs) in enumerate(terms):
                            last = nc.tensor.matmul(dst, lhsT, rhs, start=(n == 0), stop=(n == len(terms) - 1))
                    last.then_inc(o_done, 1)


def mix_out(nc, a, c, mx, h_hi, h_lo, oT, og_sp, x_sp, layer):
    NV, H = mx.nv, mx.heads
    w_out = a["gla_w_out" if mx.gla else "hgrn_w_out"][0].rearrange("(k p) n -> p k n", p=P)
    gw = VEC["gla_g" if mx.gla else "hgrn_g"]
    with ExitStack() as s:
        sb = lambda n, sh, dt=F32: s.enter_context(nc.sbuf_tensor(f"{n}_mo{layer}", sh, dt))
        sem = stage_semaphores(nc, s, f"_mo{layer}")
        ps = lambda n, sh: s.enter_context(nc.psum_tensor(f"{n}_mo{layer}", sh, F32))
        xT = sb("x", [P, DC, T])
        og = sb("og", [P, DC, T])
        sg = [sb(f"sg{i}", [P, T]) for i in range(2)]
        sq = [sb(f"sq{i}", [P, T]) for i in range(2)]
        rs = sb("rs", [P, T])
        y = [sb(f"y{i}", [P, T]) for i in range(2)]
        w_raw = [sb(f"w_raw{i}", [P, DC, P]) for i in range(2)]
        w_hi = [sb(f"w_hi{i}", [P, DC, P], F32R) for i in range(2)]
        w_lo = [sb(f"w_lo{i}", [P, DC, P], F32R) for i in range(2)]
        ms = [ps(f"ms{i}", [P, 512]) for i in range(2)]
        pp = [ps(f"pp{i}", [P, 512]) for i in range(4)]
        (x_in, og_in, sig_done, silu_done, sq_done, summed, ms_out, inv, rooted, y_done, hi_done, lo_done,
         w_hi_done, w_lo_done, proj, added, x_out) = (sem(n) for n in (
            "x_in", "og_in", "sig_done", "silu_done", "sq_done", "summed", "ms_out", "inv", "rooted", "y_done",
            "hi_done", "lo_done", "w_hi_done", "w_lo_done", "proj", "added", "x_out"))
        w_loaded = [sem(f"w_loaded{i}") for i in range(2)]
        block = s.enter_context(nc.Block())

        @block.sync
        def _(sp):
            sp.dma_start(og[:, :, :], og_sp.rearrange("k p t -> p k t")).then_inc(og_in, 16)
            sp.dma_start(xT[:, :, :], x_sp).then_inc(x_in, 16)
            with sp.Fori(0, DC // 2) as i:
                for b in range(2):
                    sp.wait_ge(w_lo_done, i * 2 + (b + 1))
                    sp.dma_start(w_raw[b][:, :, :], w_out[:, :, bass.ds(i * (2 * P) + b * P, P)]) \
                        .then_inc(w_loaded[b], 16)
            sp.wait_ge(added, 4 + 2 * DC)
            sp.dma_start(x_sp, xT[:, :, :]).then_inc(x_out, 16)
            sp.wait_ge(x_out, 16)

        @block.gpsimd
        def _(pool):
            pool.sem_inc(w_lo_done, 2)
            with pool.Fori(0, DC // 2) as i:
                for b in range(2):
                    pool.wait_ge(w_hi_done, i * 2 + (b + 1))
                    pool.tensor_tensor(w_lo[b][:, :, :], w_raw[b][:, :, :], w_hi[b][:, :, :].bitcast(F32),
                                       ALU.subtract).then_inc(w_lo_done, 1)

        @block.scalar
        def _(act):
            def hi(b, i):
                act.wait_ge(w_loaded[b], i * 16 + 16)
                act.wait_ge(proj, i * 4 + (2 * b + 2))
                act.activation(w_hi[b][:, :, :], w_raw[b][:, :, :], ACT.Copy).then_inc(w_hi_done, 1)

            act.wait_ge(og_in, 16)
            for k in range(DC):
                if k >= 2:
                    act.wait_ge(silu_done, k - 1)
                act.activation(sg[k % 2][:, :], og[:, k, :], ACT.Sigmoid).then_inc(sig_done, 1)
            for g in range(H):
                for k in range(g * NV, (g + 1) * NV):
                    if k >= 2:
                        act.wait_ge(summed, k - 1)
                    act.activation(sq[k % 2][:, :], oT[:, k, :], ACT.Square).then_inc(sq_done, 1)
                act.wait_ge(inv, g + 1)
                act.activation(rs[:, :], rs[:, :], ACT.Sqrt).then_inc(rooted, 1)
                for k in range(g * NV, (g + 1) * NV):
                    act.wait_ge(y_done, k + 1)
                    act.activation(h_hi[:, k, :], y[k % 2][:, :], ACT.Copy).then_inc(hi_done, 1)
            with act.Fori(0, DC // 2) as i:
                hi(0, i)
                hi(1, i)

        @block.tensor
        def _(pe):
            pe.sem_inc(proj, 4)
            for k in range(DC):
                pe.wait_ge(sq_done, k + 1)
                if k % NV == 0 and k:
                    pe.wait_ge(ms_out, k // NV)
                for i, cols in halves():
                    last = nc.tensor.matmul(ms[i][:, 0:HALF], c["ones_d"][:, :], sq[k % 2][:, cols],
                                            start=(k % NV == 0), stop=(k % NV == NV - 1))
                last.then_inc(summed, 1)
            pe.wait_ge(lo_done, DC)
            with pe.Fori(0, DC // 2) as n:
                for b in range(2):
                    pe.wait_ge(w_lo_done, n * 2 + (2 + b + 1))
                    for i, cols in halves():
                        pe.wait_ge(added, n * 4 + (2 * b + i + 1))
                        split_product(nc, pp[2 * b + i][:, 0:HALF], w_hi[b], w_lo[b], h_hi, h_lo, cols) \
                            .then_inc(proj, 1)

        @block.vector
        def _(dve):
            dve.sem_inc(added, 4)
            for k in range(DC):
                dve.wait_ge(sig_done, k + 1)
                nc.vector.tensor_mul(og[:, k, :], og[:, k, :], sg[k % 2][:, :]).then_inc(silu_done, 1)

            for g in range(H):
                dve.wait_ge(summed, (g + 1) * NV)
                for i, cols in halves():
                    nc.vector.tensor_scalar(rs[:, cols], ms[i][:, 0:HALF], float(D / mx.dv), EPS, ALU.mult, ALU.add)
                dve.drain().then_inc(ms_out, 1)
                nc.vector.reciprocal(rs[:, :], rs[:, :])
                dve.drain().then_inc(inv, 1)
                dve.wait_ge(rooted, g + 1)
                for k in range(g * NV, (g + 1) * NV):
                    nc.vector.scalar_tensor_tensor(y[k % 2][:, :], oT[:, k, :],
                                                   c["vec"][:, gw + k % NV:gw + k % NV + 1], rs[:, :],
                                                   ALU.mult, ALU.mult)
                    dve.drain()
                    nc.vector.tensor_mul(y[k % 2][:, :], y[k % 2][:, :], og[:, k, :])
                    dve.drain().then_inc(y_done, 1)
                    dve.wait_ge(hi_done, k + 1)
                    nc.vector.tensor_sub(h_lo[:, k, :], y[k % 2][:, :], h_hi[:, k, :].bitcast(F32)) \
                        .then_inc(lo_done, 1)
            dve.wait_ge(x_in, 16)
            with dve.Fori(0, DC // 2) as n:
                for b in range(2):
                    for i in range(2):
                        dve.wait_ge(proj, n * 4 + (4 + 2 * b + i + 1))
                        src = pp[2 * b + i]
                        k = n * 2 + b
                        for vec, c0, c1 in ((0, 0, HALF),) if i == 0 else ((0, HALF, TS), (1, TS, T)):
                            xs = xT[:, bass.ds(k, 1), c0:c1].rearrange("p o t -> p (o t)")
                            nc.vector.scalar_tensor_tensor(
                                xs, src[:, c0 - i * HALF:c1 - i * HALF],
                                c["mod"][:, layer, bass.ds(k + 16, 1), vec], xs, ALU.mult, ALU.add)
                        dve.drain().then_inc(added, 1)


def retrieve(nc, a, c, h_hi, h_lo, chosen, layer):
    w_q = a["peer_w_q"][layer].rearrange("(k p) n -> p k n", p=P)
    keys = a["peer_keys"][layer]
    NCAND = 88
    LOWEST = -3.0e38
    with ExitStack() as s:
        sb = lambda n, sh, dt=F32: s.enter_context(nc.sbuf_tensor(f"{n}_re{layer}", sh, dt))
        sem = stage_semaphores(nc, s, f"_re{layer}")
        ps = lambda n, sh: s.enter_context(nc.psum_tensor(f"{n}_re{layer}", sh, F32))
        w_raw = [sb(f"w_raw{i}", [P, DC, P]) for i in range(2)]
        w_hi = [sb(f"w_hi{i}", [P, DC, P], F32R) for i in range(2)]
        w_lo = [sb(f"w_lo{i}", [P, DC, P], F32R) for i in range(2)]
        kraw = [sb(f"kraw{i}", [P, P]) for i in range(2)]
        kT = [sb(f"kT{i}", [P, P]) for i in range(2)]
        qT = [sb(f"qT{i}", [P, T]) for i in range(2)]
        top = sb("top", [P, 2, NT, TOPK])
        idx = sb("idx", [P, 2, NT, TOPK], U32)
        rest = sb("rest", [P, NT, P])
        cand = sb("cand", [P, NT, NCAND])
        crest = sb("crest", [P, NT, NCAND])
        ctop = sb("ctop", [P, NT, TOPK])
        cpos = sb("cpos", [P, NT, TOPK], U32)
        pq = [ps(f"pq{i}", [P, 512]) for i in range(2)]
        pk = ps("pk", [P, P])
        pS = [ps(f"pS{i}", [P, 8, P]) for i in range(2)]
        w_hi_done, w_lo_done, proj, q_out, k_turned, k_out, scored, read = (sem(n) for n in
            ("w_hi_done", "w_lo_done", "proj", "q_out", "k_turned", "k_out", "scored", "read"))
        w_loaded = [sem(f"w_loaded{i}") for i in range(2)]
        k_loaded = [sem(f"k_loaded{i}") for i in range(2)]
        dve_passed = sem("dve_passed")
        block = s.enter_context(nc.Block())

        @block.sync
        def _(sp):
            with sp.Fori(0, PH) as h:
                for b in range(2):
                    sp.wait_ge(w_lo_done, h * 2 + (b + 1))
                    sp.dma_start(w_raw[b][:, :, :], w_q[:, :, bass.ds(h * (2 * P) + b * P, P)]) \
                        .then_inc(w_loaded[b], 16)
                    sp.wait_ge(k_turned, h * 2 + (b + 1))
                    sp.dma_start(kraw[b][:, :], keys[bass.ds(h, 1), b].rearrange("o n k -> (o n) k")) \
                        .then_inc(k_loaded[b], 16)

        @block.gpsimd
        def _(pool):
            pool.sem_inc(w_lo_done, 2)
            with pool.Fori(0, PH) as h:
                for b in range(2):
                    pool.wait_ge(w_hi_done, h * 2 + (b + 1))
                    pool.tensor_tensor(w_lo[b][:, :, :], w_raw[b][:, :, :], w_hi[b][:, :, :].bitcast(F32),
                                       ALU.subtract).then_inc(w_lo_done, 1)

        @block.scalar
        def _(act):
            act.sem_inc(k_out, 1)
            act.sem_inc(q_out, 1)
            with act.Fori(0, PH) as h:
                for b in range(2):
                    act.wait_ge(w_loaded[b], h * 16 + 16)
                    act.wait_ge(proj, h * 4 + (2 * b + 2))
                    act.activation(w_hi[b][:, :, :], w_raw[b][:, :, :], ACT.Copy).then_inc(w_hi_done, 1)
                for b in range(2):
                    act.wait_ge(scored, h * 2 + (b + 1))
                    act.wait_ge(k_turned, h * 2 + (2 + b + 1))
                    act.activation(kT[b][:, :], pk[:, :], ACT.Copy).then_inc(k_out, 1)
                    for i, cols in halves():
                        act.wait_ge(proj, h * 4 + (4 + 2 * b + i + 1))
                        act.activation(qT[b][:, cols], pq[i][:, 0:HALF], ACT.Copy).then_inc(q_out, 1)

        @block.tensor
        def _(pe):
            pe.sem_inc(proj, 4)
            pe.sem_inc(k_turned, 2)
            pe.sem_inc(scored, 2)
            with pe.Fori(0, PH) as h:
                for b in range(2):
                    pe.wait_ge(k_loaded[b], h * 16 + 16)
                    pe.wait_ge(k_out, h * 2 + (1 + b))
                    nc.tensor.transpose(pk[:, :], kraw[b][:, :], c["ident"][:, :]).then_inc(k_turned, 1)
                    pe.wait_ge(w_lo_done, h * 2 + (2 + b + 1))
                    for i, cols in halves():
                        pe.wait_ge(q_out, h * 4 + (1 + (2 * b - 1 + i if b else 0)))
                        split_product(nc, pq[i][:, 0:HALF], w_hi[b], w_lo[b], h_hi, h_lo, cols).then_inc(proj, 1)
                    pe.wait_ge(q_out, h * 4 + (1 + 2 * b + 2))
                    pe.wait_ge(k_out, h * 2 + (1 + b + 1))
                    pe.wait_ge(read, h * 2 + (b + 1))
                    for t in range(NT):
                        last = nc.tensor.matmul(pS[b][:, t, :], qT[b][:, t * P:(t + 1) * P], kT[b][:, :],
                                                start=True, stop=True)
                    last.then_inc(scored, 1)

        @block.vector
        def _(dve):
            def best16(values, left, top_, idx_):
                for t in range(NT):
                    nc.vector.max(top_[:, t, 0:8], values(t))
                dve.drain()
                for t in range(NT):
                    nc.vector.max_index(idx_[:, t, 0:8], top_[:, t, 0:8], values(t))
                    nc.vector.match_replace(left[:, t, :], top_[:, t, 0:8], values(t), LOWEST)
                dve.drain()
                for t in range(NT):
                    nc.vector.max(top_[:, t, 8:16], left[:, t, :])
                dve.drain()
                for t in range(NT):
                    nc.vector.max_index(idx_[:, t, 8:16], top_[:, t, 8:16], left[:, t, :])

            dve.sem_inc(read, 2)
            with dve.Fori(0, PH) as h:
                for b in range(2):
                    dve.wait_ge(scored, h * 2 + (2 + b + 1))
                    alone(dve, dve_passed)
                    best16(lambda t: pS[b][:, t, :], rest, top[:, b], idx[:, b])
                    dve.drain().then_inc(read, 1)
                for rows, n, at in ((slice(0, 4), 16, 0), (slice(4, 8), 4, 64), (slice(8, 16), 1, 80)):
                    r = rows.stop - rows.start
                    first = top[:, 0, :, rows].unsqueeze(3).to_broadcast([P, NT, r, n])
                    second = top[:, 1, :, 0:n].unsqueeze(2).to_broadcast([P, NT, r, n])
                    nc.vector.tensor_tensor(cand[:, :, at:at + r * n].rearrange("p t (r n) -> p t r n", n=n),
                                            first, second, ALU.add)
                for f, b in ((2, 0), (3, 1)):
                    nc.vector.tensor_copy(chosen[:, f, bass.ds(h, 1)].rearrange("p o t k -> p (o t k)"),
                                          idx[:, b].rearrange("p t k -> p (t k)"))
                dve.drain()
                best16(lambda t: cand[:, t, :], crest, ctop, cpos)
                dve.drain()
                nc.vector.tensor_copy(chosen[:, 0, bass.ds(h, 1)].rearrange("p o t k -> p (o t k)"),
                                      ctop[:, :, :].rearrange("p t k -> p (t k)"))
                nc.vector.tensor_copy(chosen[:, 1, bass.ds(h, 1)].rearrange("p o t k -> p (o t k)").bitcast(U32),
                                      cpos[:, :, :].rearrange("p t k -> p (t k)"))


def route(nc, c, chosen, gates_dram, layer):
    NCH_ = PH * TOPK
    GROUP = 4
    RING = 4
    PER = GROUP * RING
    with ExitStack() as s:
        sb = lambda n, sh, dt=F32: s.enter_context(nc.sbuf_tensor(f"{n}_ro{layer}", sh, dt))
        sem = stage_semaphores(nc, s, f"_ro{layer}")
        ps = lambda n, sh: s.enter_context(nc.psum_tensor(f"{n}_ro{layer}", sh, F32))
        ALLC = [P, PH, NT, TOPK]
        e = sb("e", ALLC)
        esum = sb("esum", [P, PH, NT])
        s4 = sb("s4", ALLC, U32)
        s2 = sb("s2", ALLC, U32)
        posf = sb("posf", ALLC)
        m = sb("m", ALLC)
        rank = [sb(f"rank{i}", [P, NT, PH, TOPK]) for i in range(2)]
        gt = sb("gt", [P, NT, PH, TOPK])
        found = [sb(f"found{i}", [P, NT, NCH_]) for i in range(2)]
        iota16 = sb("iota16", [P, TOPK])
        iota128 = sb("iota128", [P, P])
        eq = [sb(f"eq{i}", [P, NCH_, TOPK]) for i in range(2)]
        turned = sb("turned", [P, 3, T])
        first = sb("first", [P, PER, P])
        second = sb("second", [P, PER, P])
        stage = sb("stage", [P, KEYS, P])
        pt = ps("pt", [P, 4, P])
        pg = [ps(f"pg{i}", [P, GROUP, P]) for i in range(RING)]
        iot, sub_done, exp_done, compared, eqd, summed, gated, tr, tr_out, hot, mm, staged, stored = (sem(n) for n in
            ("iot", "sub_done", "exp_done", "compared", "eqd", "summed", "gated", "tr", "tr_out", "hot", "mm",
             "staged", "stored"))
        block = s.enter_context(nc.Block())

        @block.gpsimd
        def _(pool):
            pool.iota(iota16[:, :], [[1, TOPK]], base=0, channel_multiplier=0, allow_small_or_imprecise_dtypes=True)
            pool.iota(iota128[:, :], [[1, P]], base=0, channel_multiplier=0, allow_small_or_imprecise_dtypes=True)
            pool.drain().then_inc(iot, 1)
            for t in range(NT):
                for b in range(2):
                    n = 2 * t + b
                    pool.wait_ge(compared, n + 1)
                    ev = eq[b][:, :, :].rearrange("p (h k) r -> p h k r", k=TOPK)
                    pool.tensor_tensor(ev, ev, chosen[:, 2 + b, :, t, :].unsqueeze(2).to_broadcast([P, PH, TOPK, TOPK]),
                                       ALU.mult)
                    pool.drain().then_inc(eqd, 1)

        @block.vector
        def _(dve):
            pos = chosen[:, 1].bitcast(U32)
            nc.vector.tensor_tensor(e[:, :, :, :], chosen[:, 0], chosen[:, 0, :, :, 0:1].to_broadcast(ALLC), ALU.subtract)
            dve.drain().then_inc(sub_done, 1)
            nc.vector.tensor_scalar(s4[:, :, :, :], pos, 4, None, ALU.logical_shift_right)
            nc.vector.tensor_scalar(s2[:, :, :, :], pos, 2, None, ALU.logical_shift_right)
            nc.vector.tensor_copy(posf[:, :, :, :], pos)
            dve.drain()
            f = lambda x: x[:, :, :, :].rearrange("p h t k -> p (h t k)")
            nc.vector.scalar_tensor_tensor(f(m), f(s2), 12.0, f(s4), ALU.subtract, ALU.max)
            dve.drain()
            nc.vector.scalar_tensor_tensor(f(m), f(posf), 72.0, f(m), ALU.subtract, ALU.max)
            dve.drain()
            for t in range(NT):
                nc.vector.tensor_copy(rank[0][:, t], m[:, :, t, :])
            nc.vector.tensor_scalar(e2v(s4), f(m), 4.0, 48.0, ALU.mult, ALU.add)
            dve.drain()
            nc.vector.scalar_tensor_tensor(e2v(s4), f(m), 16.0, e2v(s4), ALU.mult, ALU.min)
            dve.drain()
            nc.vector.scalar_tensor_tensor(e2v(s4), f(m), 72.0, e2v(s4), ALU.add, ALU.min)
            dve.drain()
            nc.vector.tensor_sub(f(posf), f(posf), e2v(s4))
            dve.drain()
            for t in range(NT):
                nc.vector.tensor_copy(rank[1][:, t], posf[:, :, t, :])
            dve.wait_ge(iot, 1)
            dve.drain()
            dve.wait_ge(exp_done, 1)
            nc.vector.tensor_reduce(esum[:, :, :], e[:, :, :, :], AX.X, ALU.add)
            dve.drain()
            nc.vector.reciprocal(esum[:, :, :], esum[:, :, :])
            dve.drain()
            for t in range(NT):
                nc.vector.tensor_mul(gt[:, t], e[:, :, t, :], esum[:, :, t:t + 1].to_broadcast([P, PH, TOPK]))
            dve.drain().then_inc(gated, 1)

            def compare(t):
                for b in range(2):
                    r = rank[b][:, t].rearrange("p h k -> p (h k)").unsqueeze(2).to_broadcast([P, NCH_, TOPK])
                    nc.vector.tensor_tensor(eq[b][:, :, :], r,
                                            iota16[:, :].unsqueeze(1).to_broadcast([P, NCH_, TOPK]), ALU.is_equal) \
                        .then_inc(compared, 1)

            def sums(t):
                for b in range(2):
                    dve.wait_ge(eqd, 2 * t + b + 1)
                    nc.vector.tensor_reduce(found[b][:, t, :], eq[b][:, :, :], AX.X, ALU.add).then_inc(summed, 1)

            compare(0)
            sums(0)
            for t in range(NT):
                if t + 1 < NT:
                    dve.drain()
                    compare(t + 1)
                dve.wait_ge(tr_out, t + 1)
                with dve.Fori(0, P // PER) as i:
                    for g in range(RING):
                        dve.wait_ge(mm, i * RING + (t * (P // GROUP) + g + 1))
                        for u in range(GROUP):
                            slot = g * GROUP + u
                            col = i * PER + (t * P + slot)
                            nc.vector.tensor_scalar(first[:, slot, :], iota128[:, :], turned[:, 0, bass.ds(col, 1)],
                                                    turned[:, 2, bass.ds(col, 1)], ALU.is_equal, ALU.mult)
                            last = nc.vector.tensor_scalar(second[:, slot, :], iota128[:, :],
                                                           turned[:, 1, bass.ds(col, 1)], None, ALU.is_equal)
                        last.then_inc(hot, 1)
                if t + 1 < NT:
                    sums(t + 1)

        @block.tensor
        def _(pe):
            pe.sem_inc(mm, RING)

            def turn(t):
                pe.wait_ge(summed, 2 * t + 2)
                pe.wait_ge(gated, 1)
                if t:
                    pe.wait_ge(tr_out, t)
                for n, src in enumerate((found[0][:, t, :], found[1][:, t, :], gt[:, t].rearrange("p h k -> p (h k)"))):
                    last = nc.tensor.transpose(pt[:, n, :], src, c["ident"][:, :])
                last.then_inc(tr, 1)

            for t in range(NT):
                turn(t)
                with pe.Fori(0, P // PER) as i:
                    for g in range(RING):
                        pe.wait_ge(hot, i * RING + (t * (P // GROUP) + g + 1))
                        pe.wait_ge(staged, i * RING + (t * (P // GROUP) + g + 1))
                        for u in range(GROUP):
                            last = nc.tensor.matmul(pg[g][:, u, :], second[:, g * GROUP + u, :],
                                                    first[:, g * GROUP + u, :], start=True, stop=True)
                        last.then_inc(mm, 1)

        @block.scalar
        def _(act):
            act.sem_inc(staged, RING)
            act.wait_ge(sub_done, 1)
            act.activation(e[:, :, :, :], e[:, :, :, :], ACT.Exp).then_inc(exp_done, 1)

            def turn_out(t):
                act.wait_ge(tr, t + 1)
                act.activation(turned[:, :, t * P:(t + 1) * P], pt[:, 0:3, :], ACT.Copy).then_inc(tr_out, 1)

            for t in range(NT):
                turn_out(t)
                if t:
                    act.wait_ge(stored, 16 * t)
                with act.Fori(0, P // PER) as i:
                    for g in range(RING):
                        act.wait_ge(mm, i * RING + (RING + t * (P // GROUP) + g + 1))
                        act.activation(stage[:, :, bass.ds(i * PER + g * GROUP, GROUP)],
                                       pg[g][:, :, :].rearrange("p t i -> p i t"), ACT.Copy).then_inc(staged, 1)

        @block.sync
        def _(sp):
            for t in range(NT):
                sp.wait_ge(staged, RING + (t + 1) * (P // GROUP))
                sp.dma_start(gates_dram[:, :, t * P:(t + 1) * P].rearrange("i j t -> j i t"), stage[:, :, :]) \
                    .then_inc(stored, 16)
            sp.wait_ge(stored, 16 * NT)


def e2v(x):
    return x[:, :, :, :].rearrange("p h t k -> p (h t k)").bitcast(F32)


def experts(nc, a, c, h_hi, h_lo, x_sp, gates_dram, layer):
    NE = KEYS
    K = 2
    u_tab = a["peer_u"][layer].rearrange("(n p) d -> n p d", p=P)
    v_tab = a["peer_v"][layer].rearrange("(n p) d -> n p d", p=P)
    with ExitStack() as s:
        sb = lambda n, sh, dt=F32: s.enter_context(nc.sbuf_tensor(f"{n}_ex{layer}", sh, dt))
        sem = stage_semaphores(nc, s, f"_ex{layer}")
        ps = lambda n, sh: s.enter_context(nc.psum_tensor(f"{n}_ex{layer}", sh, F32))
        acc = sb("acc", [P, DC, T])
        u_raw = [sb(f"u_raw{i}", [P, D]) for i in range(2)]
        v_raw = [sb(f"v_raw{i}", [P, D]) for i in range(2)]
        g_raw = [sb(f"g_raw{i}", [P, T]) for i in range(2)]
        uT_hi = [sb(f"uT_hi{i}", [P, DC, P], F32R) for i in range(2)]
        uT_lo = [sb(f"uT_lo{i}", [P, DC, P], F32R) for i in range(2)]
        v_hi = [sb(f"v_hi{i}", [P, D], F32R) for i in range(4)]
        v_lo = [sb(f"v_lo{i}", [P, D], F32R) for i in range(4)]
        c_hi = [sb(f"c_hi{i}", [P, T], F32R) for i in range(4)]
        c_lo = [sb(f"c_lo{i}", [P, T], F32R) for i in range(4)]
        coef = [sb(f"coef{i}", [P, T]) for i in range(2)]
        pT = [ps(f"pT{i}", [P, 4, P]) for i in range(2)]
        pu = [ps(f"pu{i}", [P, 512]) for i in range(2)]
        pv = [ps(f"pv{i}", [P, 512]) for i in range(4)]
        (turned, u_hi_done, u_lo_done, dotted, gelu_done, coef_done, c_hi_done, c_lo_done, v_hi_done, v_lo_done,
         v_mm, added, x_in, x_out, x_added) = (sem(n) for n in (
            "turned", "u_hi_done", "u_lo_done", "dotted", "gelu_done", "coef_done", "c_hi_done", "c_lo_done",
            "v_hi_done", "v_lo_done", "v_mm", "added", "x_in", "x_out", "x_added"))
        u_in, v_in, g_in = ([sem(f"{n}{i}") for i in range(2)] for n in ("u_in", "v_in", "g_in"))
        block = s.enter_context(nc.Block())
        xT = [buf[:, 0:T] for buf in (*u_raw, *v_raw, *g_raw, *coef)]
        REG = 2 * DC
        BANKS = 4

        def half16(n, r):
            if isinstance(n, int):
                return 16 * (n // 2 + 1)
            return n * 8 + (16 - 8 * (r % 2))

        def chunk_of(n, r, scale):
            if isinstance(n, int):
                return scale * (n // 2)
            return n * (scale // 2) - (scale // 2) * (r % 2)

        def schedule(eng, first, step, last):
            first(0)
            step(0, 0, None)
            step(1, 1, None)
            with eng.Fori(0, (NE - 4) // 4) as i:
                for r in range(4):
                    n = i * 4 + (2 + r)
                    step(n, 2 + r, i * 2 + (r // 2) if r % 2 else None)
            step(NE - 2, 2, None)
            step(NE - 1, 3, NE // 2 - 2)
            last(NE // 2 - 1)

        @block.sync
        def _(sp):
            with sp.Fori(0, NE // 2) as i:
                for b in range(2):
                    n = i * 2 + b
                    sp.wait_ge(turned, n + 1)
                    sp.dma_start(u_raw[b][:, :], u_tab[bass.ds(n, 1)].rearrange("o p d -> (o p) d")).then_inc(u_in[b], 16)
                    sp.wait_ge(v_lo_done, n + 1)
                    sp.dma_start(v_raw[b][:, :], v_tab[bass.ds(n, 1)].rearrange("o p d -> (o p) d")).then_inc(v_in[b], 16)
                    sp.wait_ge(coef_done, n + 1)
                    sp.dma_start(g_raw[b][:, :], gates_dram[bass.ds(n, 1)].rearrange("o p t -> (o p) t")) \
                        .then_inc(g_in[b], 16)
            sp.wait_ge(added, BANKS + REG * NE // K)
            for k in range(DC):
                sp.dma_start(xT[k], x_sp[:, k, :]).then_inc(x_in, 16)
            sp.wait_ge(x_added, 1)
            for k in range(DC):
                sp.dma_start(x_sp[:, k, :], xT[k]).then_inc(x_out, 16)
            sp.wait_ge(x_out, 16 * DC)

        @block.gpsimd
        def _(pool):
            pool.sem_inc(v_lo_done, 2)
            with pool.Fori(0, NE // 4) as i:
                for r in range(4):
                    n = i * 4 + r
                    pool.wait_ge(v_hi_done, n + 1)
                    pool.tensor_tensor(v_lo[r][:, :], v_raw[r % 2][:, :], v_hi[r][:, :].bitcast(F32), ALU.subtract) \
                        .then_inc(v_lo_done, 1)

        @block.scalar
        def _(act):
            def turn_hi(n, r):
                act.wait_ge(turned, n + 3)
                act.wait_ge(dotted, n * 2 + 2)
                for i in range(2):
                    last_ = act.activation(uT_hi[r % 2][:, 4 * i:4 * i + 4, :], pT[i][:, :, :], ACT.Copy)
                last_.then_inc(u_hi_done, 1)

            def step(n, r, chunk):
                b = r % 2
                if not (isinstance(n, int) and n == NE - 1):
                    turn_hi(n + 1, r + 1)
                act.wait_ge(v_in[b], half16(n, r))
                act.wait_ge(v_mm, chunk_of(n, r, REG) + REG)
                act.activation(v_hi[r % 4][:, :], v_raw[b][:, :], ACT.Copy).then_inc(v_hi_done, 1)
                for i, cols in halves():
                    act.wait_ge(dotted, n * 2 + (4 + i + 1))
                    if i == 0:
                        act.wait_ge(c_lo_done, n + 1)
                    act.activation(coef[b][:, cols], pu[i][:, 0:HALF], ACT.Gelu).then_inc(gelu_done, 1)
                act.wait_ge(coef_done, n + 3)
                act.activation(c_hi[r % 4][:, :], coef[b][:, :], ACT.Copy).then_inc(c_hi_done, 1)

            schedule(act, lambda n: turn_hi(0, 0), step, lambda ch: None)

        @block.vector
        def _(dve):
            dve.sem_inc(coef_done, 2)
            dve.sem_inc(c_lo_done, 2)
            dve.sem_inc(added, BANKS)
            nc.vector.memset(acc[:, :, :], 0.0)
            dve.drain()

            def turn_lo(n, r):
                dve.wait_ge(u_hi_done, n + 1)
                for i in range(2):
                    last_ = nc.vector.tensor_sub(uT_lo[r % 2][:, 4 * i:4 * i + 4, :], pT[i][:, :, :],
                                                 uT_hi[r % 2][:, 4 * i:4 * i + 4, :].bitcast(F32))
                last_.then_inc(u_lo_done, 1)

            def accumulate(chunk):
                for g in range(REG):
                    k, i = g // 2, g % 2
                    dve.wait_ge(v_mm, chunk * REG + (2 * REG + g + 1))
                    dst = acc[:, k, i * HALF:(i + 1) * HALF]
                    nc.vector.tensor_add(dst, dst, pv[g % BANKS][:, 0:HALF]).then_inc(added, 1)

            def step(n, r, chunk):
                b = r % 2
                if not (isinstance(n, int) and n == NE - 1):
                    turn_lo(n + 1, r + 1)
                dve.wait_ge(g_in[b], half16(n, r))
                dve.wait_ge(gelu_done, n * 2 + 2)
                nc.vector.tensor_mul(coef[b][:, :], coef[b][:, :], g_raw[b][:, :]).then_inc(coef_done, 1)
                dve.wait_ge(c_hi_done, n + 1)
                nc.vector.tensor_sub(c_lo[r % 4][:, :], coef[b][:, :], c_hi[r % 4][:, :].bitcast(F32)) \
                    .then_inc(c_lo_done, 1)
                if chunk is not None:
                    accumulate(chunk)

            schedule(dve, lambda n: turn_lo(0, 0), step, accumulate)
            dve.drain()
            dve.wait_ge(x_in, 16 * DC)
            for k in range(DC):
                for v, cols in parts():
                    nc.vector.scalar_tensor_tensor(xT[k][:, cols], acc[:, k, cols],
                                                   c["mod"][:, layer, 40 + k, v:v + 1], xT[k][:, cols],
                                                   ALU.mult, ALU.add)
            dve.drain().then_inc(x_added, 1)

        @block.tensor
        def _(pe):
            pe.sem_inc(turned, 2)
            pe.sem_inc(dotted, 4)
            pe.sem_inc(v_mm, 2 * REG)

            def turn(n, r):
                pe.wait_ge(u_in[r % 2], half16(n, r))
                if not (isinstance(n, int) and n == 0):
                    pe.wait_ge(u_lo_done, n)
                for k in range(DC):
                    last_ = nc.tensor.transpose(pT[k // 4][:, k % 4, :], u_raw[r % 2][:, k * P:(k + 1) * P],
                                                c["ident"][:, :])
                last_.then_inc(turned, 1)

            def products(chunk, odd):
                for g in range(REG):
                    k, i = g // 2, g % 2
                    pe.wait_ge(added, chunk * REG + (g + 1))
                    terms = []
                    for t in range(K):
                        slot = 2 * odd + t
                        for w, x in ((v_hi, c_hi), (v_hi, c_lo), (v_lo, c_hi)):
                            terms.append((w[slot][:, k * P:(k + 1) * P], x[slot][:, i * HALF:(i + 1) * HALF]))
                    for m, (w, x) in enumerate(terms):
                        last_ = nc.tensor.matmul(pv[g % BANKS][:, 0:HALF], w, x, start=(m == 0),
                                                 stop=(m == len(terms) - 1))
                    last_.then_inc(v_mm, 1)

            def step(n, r, chunk):
                b = r % 2
                if not (isinstance(n, int) and n == NE - 1):
                    turn(n + 1, r + 1)
                pe.wait_ge(u_lo_done, n + 1)
                pe.wait_ge(gelu_done, n * 2)
                for i, cols in halves():
                    split_product(nc, pu[i][:, 0:HALF], uT_hi[b], uT_lo[b], h_hi, h_lo, cols).then_inc(dotted, 1)
                if chunk is not None:
                    pe.wait_ge(v_lo_done, chunk * 2 + 4)
                    pe.wait_ge(c_lo_done, chunk * 2 + 4)
                    products(chunk, slot_pair(r))

            def slot_pair(r):
                return 0 if r % 4 == 3 else 1

            def last(chunk):
                pe.wait_ge(v_lo_done, chunk * 2 + 4)
                pe.wait_ge(c_lo_done, chunk * 2 + 4)
                products(chunk, 1)

            schedule(pe, lambda n: turn(0, 0), step, last)


def finish(nc, c, x_sp, out):
    with ExitStack() as s:
        sb = lambda n, sh, dt=F32: s.enter_context(nc.sbuf_tensor(f"{n}_fi", sh, dt))
        sem = stage_semaphores(nc, s, f"_fi")
        ps = lambda n, sh: s.enter_context(nc.psum_tensor(f"{n}_fi", sh, F32))
        xT = sb("x", [P, DC, T])
        sq = [sb(f"sq{i}", [P, T]) for i in range(2)]
        rs = sb("rs", [P, T])
        y = sb("y", [P, NT, D])
        ms = [ps(f"ms{i}", [P, 512]) for i in range(2)]
        pt = [ps(f"pt{i}", [P, 4, P]) for i in range(2)]
        x_in, sq_done, summed, inv, rooted, scaled, tr, tr_out, stored = (sem(n) for n in
            ("x_in", "sq_done", "summed", "inv", "rooted", "scaled", "tr", "tr_out", "stored"))
        block = s.enter_context(nc.Block())

        @block.sync
        def _(sp):
            sp.dma_start(xT[:, :, :], x_sp).then_inc(x_in, 16)
            sp.wait_ge(tr_out, 2 * (NT - 1))
            sp.dma_start(out[1].rearrange("o (n p) d -> p (o n) d", p=P), y[:, 0:NT - 1, :]).then_inc(stored, 16)
            sp.wait_ge(tr_out, 2 * NT)
            sp.dma_start(out[0].rearrange("o p d -> (o p) d"), y[:, NT - 1, :]).then_inc(stored, 16)
            sp.wait_ge(stored, 32)

        @block.scalar
        def _(act):
            act.wait_ge(x_in, 16)
            for k in range(DC):
                if k >= 2:
                    act.wait_ge(summed, k - 1)
                act.activation(sq[k % 2][:, :], xT[:, k, :], ACT.Square).then_inc(sq_done, 1)
            act.wait_ge(inv, 1)
            act.activation(rs[:, :], rs[:, :], ACT.Sqrt).then_inc(rooted, 1)
            for n in range(2 * NT):
                act.wait_ge(tr, n + 1)
                act.activation(y[:, n // 2, (n % 2) * 512:(n % 2 + 1) * 512],
                               pt[n % 2][:, :, :].rearrange("p a b -> p (a b)"), ACT.Copy).then_inc(tr_out, 1)

        @block.tensor
        def _(pe):
            for k in range(DC):
                pe.wait_ge(sq_done, k + 1)
                for i, cols in halves():
                    last = nc.tensor.matmul(ms[i][:, 0:HALF], c["ones_d"][:, :], sq[k % 2][:, cols],
                                            start=(k == 0), stop=(k == DC - 1))
                last.then_inc(summed, 1)
            pe.wait_ge(scaled, 1)
            for n in range(2 * NT):
                if n >= 2:
                    pe.wait_ge(tr_out, n - 1)
                for k in range(4):
                    last = nc.tensor.transpose(pt[n % 2][:, k, :],
                                               xT[:, 4 * (n % 2) + k, (n // 2) * P:(n // 2 + 1) * P], c["ident"][:, :])
                last.then_inc(tr, 1)

        @block.vector
        def _(dve):
            dve.wait_ge(summed, DC)
            for i, cols in halves():
                nc.vector.tensor_scalar(rs[:, cols], ms[i][:, 0:HALF], EPS, None, ALU.add)
            dve.drain()
            nc.vector.reciprocal(rs[:, :], rs[:, :])
            dve.drain().then_inc(inv, 1)
            dve.wait_ge(rooted, 1)
            for k in range(DC):
                w = VEC["final"] + k
                nc.vector.scalar_tensor_tensor(xT[:, k, :], xT[:, k, :], c["vec"][:, w:w + 1], rs[:, :],
                                               ALU.mult, ALU.mult)
            dve.drain().then_inc(scaled, 1)


_INS = ["x_prompt", "x_sample", "state_hgrn", "state_gla", "c", "c_ctx", "ada_w", "ada_b", "norm1_w", "norm2_w",
        "final_norm_w", "hgrn_w_in", "hgrn_lb", "hgrn_gnorm_w", "hgrn_w_out", "gla_w_in", "gla_conv_w",
        "gla_w_gate", "gla_b_gate", "gla_gnorm_w", "gla_w_out", "peer_w_q", "peer_keys", "peer_u", "peer_v"]
_OUTS = [(1, TC, D), (1, TS, D), (1, 1, 2, 8, P, P), (1, 1, 2, 4, P, 2 * P)]


def kernel(**inputs):
    import concourse.bacc as bacc
    from concourse.bass_utils import run_bass_kernel_spmd

    nc = bacc.Bacc("TRN2", target_bir_lowering=False, num_devices=1)
    arrays, args = {}, {}
    for name in _INS:
        x = np.ascontiguousarray(inputs[name])
        arrays[f"in_{name}"] = x
        args[name] = nc.dram_tensor(f"in_{name}", x.shape, mybir.dt.from_np(x.dtype), kind="ExternalInput").ap()
    outs = [nc.dram_tensor(f"out_{i}", shape, F32, kind="ExternalOutput").ap() for i, shape in enumerate(_OUTS)]
    build_program(nc, args, outs)
    r = run_bass_kernel_spmd(nc, [arrays], core_ids=[0])
    return tuple(r.results[0][f"out_{i}"] for i in range(len(_OUTS)))
```

```python
import numpy as np
from contextlib import ExitStack

import concourse.bass as bass
from concourse import mybir

F32 = mybir.dt.float32
F32R = mybir.dt.float32r
BF16 = mybir.dt.bfloat16
U32 = mybir.dt.uint32
I32 = mybir.dt.int32
ALU = mybir.AluOpType
ACT = mybir.ActivationFunctionType
AX = mybir.AxisListType

P = 128
D = 1024
DC = D // P
TS, TC = 512, 128
T = TS + TC
NT = T // P
HALF = T // 2
GRID_W = 64
ROWS = TS // GRID_W
EPS = 1e-6
F_MIN = 1e-20
LEVELS = [64, 32, 16, 8, 4, 2, 1]
NL = len(LEVELS)
DEPTH = 2
KEYS = 128
TOPK = 16
PH = 8
STORE = 64
LN2 = float(np.log(2.0))
LN_LOW = 2.0 ** -40
LN_UP = 2.0 ** 40 - 1.0
LN_FIX = -40.0 * LN2 / LN_UP

VEC = {}


def stage_semaphores(nc, stack, suffix):
    made = []

    def sem(name):
        made.append(nc.alloc_semaphore(f"{name}{suffix}"))
        return made[-1]

    def leave():
        nc.clear_and_free_semaphores(made)
        nc.all_engine_barrier()

    stack.callback(leave)
    return sem


def alone(eng, passed):
    eng.sem_inc(passed, 1)


def halves():
    return [(0, slice(0, HALF)), (1, slice(HALF, T))]


def parts():
    return [(0, slice(0, TS)), (1, slice(TS, T))]


class Mixer:

    def __init__(self, kind):
        self.gla = kind == "gla"
        self.heads = 4 if self.gla else 8
        self.dv = D // self.heads
        self.nv = self.dv // P
        if self.gla:
            self.late = [("v0", 1024, 2 * P), ("v1", 1024 + P, 2 * P), ("og0", 2048, 2 * P), ("og1", 2048 + P, 2 * P)]
            self.early = [("k", 512, P), ("q", 0, P)]
            self.extra = 2
        else:
            self.late = [("v0", 1024, P), ("og0", 4096, P)]
            self.early = [("ff", 2048, P), ("fb", 3072, P), ("q", 0, P)]
            self.extra = 0
        self.chunks = self.late + self.early
        self.nch = len(self.chunks)
        self.turns = self.nch + self.extra


def build_program(nc, a, out, upto=99):
    x_sp = nc.dram_tensor("xT_spill", [P, DC, T], F32, kind="Internal").ap()
    og_sp = nc.dram_tensor("og_spill", [DC, P, T], F32, kind="Internal").ap()
    gates_dram = nc.dram_tensor("gates", [T // STORE, KEYS, KEYS, STORE], F32, kind="Internal").ap()

    ctx = ExitStack()
    with ctx:
        c = {}
        for name, shape, dt in [
            ("ident", [P, P], F32), ("ones_d", [P, P], F32), ("ones_h", [P, P], F32),
            ("level_mask", [P, (NL + 1), P], BF16), ("scan_f", [P, T], BF16), ("scan_b", [P, T], BF16),
            ("vec", [P, 3 * P], F32), ("mod", [P, DEPTH, 48, 2], F32), ("one", [P, 1], F32),
            ("scale_w", [P, DC, 2], F32), ("lb", [P, 16], F32), ("oml", [P, 16], F32),
        ]:
            c[name] = ctx.enter_context(nc.sbuf_tensor(name, shape, dt))
        with nc.sbuf_tensor("xT", [P, DC, T], F32) as xT:
            setup(nc, a, c, xT, x_sp)
        if upto < 1:
            return
        for layer in range(DEPTH):
            mx = Mixer("gla" if layer % 2 else "hgrn")
            with nc.sbuf_tensor(f"h_hi{layer}", [P, DC, T], F32R) as h_hi, \
                    nc.sbuf_tensor(f"h_lo{layer}", [P, DC, T], F32R) as h_lo:
                norm(nc, c, h_hi, h_lo, x_sp, layer, 0)
                with nc.sbuf_tensor(f"oT{layer}", [P, DC, T], F32) as oT:
                    mixer(nc, a, c, mx, h_hi, h_lo, oT, og_sp, out, layer)
                    mix_out(nc, a, c, mx, h_hi, h_lo, oT, og_sp, x_sp, layer)
                if upto < 2 + 2 * layer:
                    return
                norm(nc, c, h_hi, h_lo, x_sp, layer, 1)
                with nc.sbuf_tensor(f"chosen{layer}", [P, 4, PH, NT, TOPK], F32) as chosen:
                    retrieve(nc, a, c, h_hi, h_lo, chosen, layer)
                    route(nc, c, chosen, gates_dram, layer)
                experts(nc, a, c, h_hi, h_lo, x_sp, gates_dram, layer)
                if upto < 3 + 2 * layer:
                    return
        finish(nc, c, x_sp, out)



def vec_rows(a):
    r = lambda ap: ap.rearrange("(n p) -> n p", p=P)
    return [
        ("norm1", a["norm1_w"].rearrange("l (n p) -> (l n) p", p=P), 16),
        ("norm2", a["norm2_w"].rearrange("l (n p) -> (l n) p", p=P), 16),
        ("final", r(a["final_norm_w"]), 8),
        ("lb", a["hgrn_lb"].rearrange("o d (n p) -> (o d n) p", p=P), 16),
        ("hgrn_g", a["hgrn_gnorm_w"].rearrange("o (n p) -> (o n) p", p=P), 1),
        ("gla_g", a["gla_gnorm_w"].rearrange("o (n p) -> (o n) p", p=P), 2),
        ("b_gate", a["gla_b_gate"].rearrange("o d (n p) -> (o d n) p", p=P), 8),
        ("c", a["c"].rearrange("o (n p) -> (o n) p", p=P), 8),
        ("c_ctx", r(a["c_ctx"]), 8),
        ("pad", None, P - 83),
        ("ada_b", a["ada_b"].rearrange("l (n p) -> (l n) p", p=P), 96),
        ("conv8", a["gla_conv_w"].rearrange("o y x (n p) -> (o y x n) p", p=P)[P:P + 16, :], 16),
        ("pad2", None, 16),
        ("conv", a["gla_conv_w"].rearrange("o y x (n p) -> (o y x n) p", p=P)[0:P, :], P),
    ]


def setup(nc, a, c, xT, x_sp):
    NB = 512
    NBL = 6 * D // NB
    with ExitStack() as s:
        sb = lambda n, sh, dt=F32: s.enter_context(nc.sbuf_tensor(n, sh, dt))
        sem = stage_semaphores(nc, s, "")
        rows = sb("param_rows", [P, 3, P])
        xin = sb("xin", [P, NT, D])
        ada = [sb(f"ada{i}", [P, DC, NB]) for i in range(2)]
        cs = sb("cs", [P, 2, DC])
        sg = sb("sg", [P, 2, DC])
        it_p = sb("it_p", [P, P], I32)
        it_f = sb("it_f", [P, P], I32)
        xorf = sb("xorf", [P, P])
        low = sb("low", [P, P])
        l0 = sb("l0", [P, 16])
        l1 = sb("l1", [P, 16])
        pt = [s.enter_context(nc.psum_tensor(f"pt{i}", [P, 4, P], F32)) for i in range(2)]
        pa = [s.enter_context(nc.psum_tensor(f"pa{i}", [P, 512], F32)) for i in range(2)]
        rows_in, x_in, consts, tr, ev, vecs, cready = (sem(n) for n in
            ("rows_in", "x_in", "consts", "tr", "ev", "vecs", "cready"))
        ada_in = [sem(f"ada_in{i}") for i in range(2)]
        ada_mm, mod_done, x_out, iot, sig, rows_z = (sem(n) for n in
            ("ada_mm", "mod_done", "x_out", "iot", "sig", "rows_z"))
        col = 0
        loads = []
        for name, view, n in vec_rows(a):
            VEC[name] = col
            if view is not None:
                loads.append((view, col, n))
            col += n
        block = s.enter_context(nc.Block())
        nload = len(loads)

        @block.sync
        def _(sp):
            sp.wait_ge(rows_z, 1)
            for view, col0, n in loads:
                sp.dma_start(rows[col0 % P:col0 % P + n, col0 // P, :], view).then_inc(rows_in, 16)
            for l in range(DEPTH):
                w = a["ada_w"][l].rearrange("(k p) n -> p k n", p=P)
                with sp.Fori(0, NBL // 2) as i:
                    for b in range(2):
                        sp.wait_ge(ada_mm, i * 2 + (l * NBL + b + 1))
                        sp.dma_start(ada[b][:, :, :], w[:, :, bass.ds(i * (2 * NB) + b * NB, NB)]) \
                            .then_inc(ada_in[b], 16)
            sp.wait_ge(ev, 3 + 40 // 4)
            sp.dma_start(x_sp, xT[:, :, :]).then_inc(x_out, 16)
            sp.wait_ge(x_out, 16)

        @block.gpsimd
        def _(pool):
            pool.memset(rows[:, :, :], 0.0)
            pool.drain().then_inc(rows_z, 1)
            pool.iota(it_p[:, :], [[0, P]], base=0, channel_multiplier=1)
            pool.iota(it_f[:, :], [[1, P]], base=0, channel_multiplier=0)
            pool.memset(c["ident"][:, :], 0.0)
            pool.memset(c["ones_d"][:, :], 1.0 / D)
            pool.memset(c["one"][:, :], 1.0)
            pool.memset(c["scan_f"][:, :], 1.0)
            pool.memset(c["scan_b"][:, :], 1.0)
            pool.drain()
            pool.affine_select(out=c["ident"][:, :], in_=c["ident"][:, :], compare_op=ALU.not_equal,
                               fill=1.0, base=0, pattern=[[-1, P]], channel_multiplier=1)
            pool.memset(c["scan_f"][:, :].rearrange("p (n t) -> p n t", t=P)[:, :, 0:1], 0.0)
            pool.memset(c["scan_b"][:, :].rearrange("p (n t) -> p n t", t=P)[:, :, P - 1:P], 0.0)
            pool.drain().then_inc(iot, 1)

        @block.scalar
        def _(act):
            act.dma_start(xin[:, 0:NT - 1, :], a["x_sample"].rearrange("o (n p) d -> p (o n) d", p=P)) \
                .then_inc(x_in, 16)
            act.dma_start(xin[:, NT - 1, :], a["x_prompt"].rearrange("o p d -> (o p) d")).then_inc(x_in, 16)
            for g in range(3 + 10):
                act.wait_ge(tr, g + 1)
                if g < 3:
                    act.activation(c["vec"][:, g * P:(g + 1) * P], pt[g % 2][:, 0, :], ACT.Copy).then_inc(ev, 1)
                else:
                    q = g - 3
                    t, k = q // 2, 4 * (q % 2)
                    act.activation(xT[:, k:k + 4, t * P:(t + 1) * P], pt[g % 2][:, :, :], ACT.Copy).then_inc(ev, 1)
            act.wait_ge(ev, 3)
            for v, name in ((0, "c"), (1, "c_ctx")):
                act.activation(sg[:, v, :], c["vec"][:, VEC[name]:VEC[name] + DC], ACT.Sigmoid)
            act.drain().then_inc(sig, 1)

        @block.vector
        def _(dve):
            dve.wait_ge(iot, 1)
            nc.vector.tensor_tensor(it_p[:, :], it_p[:, :], it_f[:, :], ALU.bitwise_xor)
            dve.drain()
            nc.vector.tensor_copy(xorf[:, :], it_p[:, :])
            dve.drain()
            for l, m in enumerate(LEVELS):
                nc.vector.tensor_scalar(low[:, :], xorf[:, :], float(m), None, ALU.is_ge)
                dve.drain()
                nc.vector.scalar_tensor_tensor(c["level_mask"][:, l, :], xorf[:, :], float(2 * m), low[:, :],
                                               ALU.is_lt, ALU.mult)
                dve.drain()
            nc.vector.tensor_scalar(c["level_mask"][:, NL, :], xorf[:, :], 0.0, None, ALU.is_equal)
            dve.wait_ge(ev, 3)
            lbr = c["vec"][:, VEC["lb"]:VEC["lb"] + 16]
            nc.vector.tensor_sub(l0[:, :], lbr, lbr)
            dve.drain().then_inc(vecs, 1)
            dve.wait_ge(vecs, 2)
            nc.vector.reciprocal(l1[:, :], l0[:, :])
            dve.drain()
            nc.vector.tensor_mul(l1[:, :], l0[:, :], l1[:, :])
            dve.drain()
            nc.vector.tensor_sub(c["lb"][:, :], l1[:, :], l1[:, :])
            dve.drain()
            nc.vector.tensor_scalar(c["oml"][:, :], c["lb"][:, :], -1.0, 1.0, ALU.mult, ALU.add)
            dve.wait_ge(sig, 1)
            for v, name in ((0, "c"), (1, "c_ctx")):
                nc.vector.tensor_mul(cs[:, v, :], sg[:, v, :], c["vec"][:, VEC[name]:VEC[name] + DC])
            dve.drain().then_inc(cready, 1)
            for l in range(DEPTH):
                bias = c["vec"][:, VEC["ada_b"] + 48 * l:VEC["ada_b"] + 48 * l + 48]
                for v in range(2):
                    dve.wait_ge(ada_mm, 2 + NBL * (l + 1))
                    nc.vector.tensor_add(c["mod"][:, l, :, v], pa[l][:, 0:96].rearrange("p (n v) -> p n v", v=2)[:, :, v],
                                         bias)
            dve.drain().then_inc(mod_done, 1)

        @block.scalar
        def _(act):
            act.wait_ge(vecs, 1)
            act.activation(l0[:, :], l0[:, :], ACT.Exp)
            act.drain().then_inc(vecs, 1)

        @block.tensor
        def _(pe):
            pe.sem_inc(ada_mm, 2)
            pe.wait_ge(iot, 1)
            pe.wait_ge(rows_in, 16 * nload)
            for g in range(3 + 10):
                if g >= 2:
                    pe.wait_ge(ev, g - 1)
                if g < 3:
                    last = nc.tensor.transpose(pt[g % 2][:, 0, :], rows[:, g, :], c["ident"][:, :])
                else:
                    if g == 3:
                        pe.wait_ge(x_in, 32)
                    q = g - 3
                    for k in range(4):
                        kk = 4 * (q % 2) + k
                        last = nc.tensor.transpose(pt[g % 2][:, k, :], xin[:, q // 2, kk * P:(kk + 1) * P],
                                                   c["ident"][:, :])
                last.then_inc(tr, 1)
            pe.wait_ge(cready, 1)
            for l in range(DEPTH):
                with pe.Fori(0, NBL // 2) as i:
                    for b in range(2):
                        pe.wait_ge(ada_in[b], i * 16 + (16 * (l * NBL // 2) + 16))
                        for n in range(NB // P):
                            for k in range(DC):
                                dst = pa[l][:, bass.ds(i * (4 * NB // P) + (2 * (b * NB // P + n)), 2)]
                                last = nc.tensor.matmul(dst, ada[b][:, k, n * P:(n + 1) * P], cs[:, :, k],
                                                        start=(k == 0), stop=(k == DC - 1))
                        last.then_inc(ada_mm, 1)


def norm(nc, c, h_hi, h_lo, x_sp, layer, which):
    with ExitStack() as s:
        sb = lambda n, sh, dt=F32: s.enter_context(nc.sbuf_tensor(f"{n}_n{layer}{which}", sh, dt))
        sem = stage_semaphores(nc, s, f"_n{layer}{which}")
        xT = sb("x", [P, DC, T])
        sq = [sb(f"sq{i}", [P, T]) for i in range(2)]
        rs = sb("rs", [P, T])
        y = [sb(f"y{i}", [P, T]) for i in range(2)]
        ms = [s.enter_context(nc.psum_tensor(f"ms{i}_n{layer}{which}", [P, 512], F32)) for i in range(2)]
        x_in, sq_done, summed, inv, rooted, hi_done, y_done, lo_done = (sem(n) for n in
            ("x_in", "sq_done", "summed", "inv", "rooted", "hi_done", "y_done", "lo_done"))
        block = s.enter_context(nc.Block())
        w0 = VEC["norm2" if which else "norm1"] + 8 * layer
        sh, sc = 24 * which, 24 * which + 8

        @block.sync
        def _(sp):
            sp.dma_start(xT[:, :, :], x_sp).then_inc(x_in, 16)

        @block.scalar
        def _(act):
            act.wait_ge(x_in, 16)
            for k in range(DC):
                if k >= 2:
                    act.wait_ge(summed, k - 1)
                act.activation(sq[k % 2][:, :], xT[:, k, :], ACT.Square).then_inc(sq_done, 1)
            act.wait_ge(inv, 1)
            act.activation(rs[:, :], rs[:, :], ACT.Sqrt).then_inc(rooted, 1)
            for k in range(DC):
                act.wait_ge(y_done, k + 1)
                act.activation(h_hi[:, k, :], y[k % 2][:, :], ACT.Copy).then_inc(hi_done, 1)

        @block.tensor
        def _(pe):
            for k in range(DC):
                pe.wait_ge(sq_done, k + 1)
                for i, cols in halves():
                    last = nc.tensor.matmul(ms[i][:, 0:HALF], c["ones_d"][:, :], sq[k % 2][:, cols],
                                            start=(k == 0), stop=(k == DC - 1))
                last.then_inc(summed, 1)

        @block.vector
        def _(dve):
            for v in range(2):
                nc.vector.scalar_tensor_tensor(c["scale_w"][:, :, v], c["mod"][:, layer, sc:sc + DC, v], 1.0,
                                               c["vec"][:, w0:w0 + DC], ALU.add, ALU.mult)
            dve.wait_ge(summed, DC)
            for i, cols in halves():
                nc.vector.tensor_scalar(rs[:, cols], ms[i][:, 0:HALF], EPS, None, ALU.add)
            dve.drain()
            nc.vector.reciprocal(rs[:, :], rs[:, :])
            dve.drain().then_inc(inv, 1)
            dve.wait_ge(rooted, 1)

            def modulate(k):
                nc.vector.tensor_mul(y[k % 2][:, :], xT[:, k, :], rs[:, :])
                dve.drain()
                for v, cols in parts():
                    nc.vector.tensor_scalar(y[k % 2][:, cols], y[k % 2][:, cols], c["scale_w"][:, k, v:v + 1],
                                            c["mod"][:, layer, sh + k, v:v + 1], ALU.mult, ALU.add)
                dve.drain().then_inc(y_done, 1)

            modulate(0)
            for k in range(DC):
                if k + 1 < DC:
                    modulate(k + 1)
                dve.wait_ge(hi_done, k + 1)
                nc.vector.tensor_sub(h_lo[:, k, :], y[k % 2][:, :], h_hi[:, k, :].bitcast(F32))
                dve.drain()


def split_product(nc, psum, w_hi, w_lo, x_hi, x_lo, cols):
    for k in range(DC):
        for w, x in ((w_hi, x_hi), (w_hi, x_lo), (w_lo, x_hi)):
            last = nc.tensor.matmul(psum, w[:, k, :], x[:, k, cols], start=(k == 0 and w is w_hi and x is x_hi),
                                    stop=(k == DC - 1 and w is w_lo))
    return last


def mixer(nc, a, c, mx, h_hi, h_lo, oT, og_sp, out, layer):
    NV, DV, NCH, TURNS, H = mx.nv, mx.dv, mx.nch, mx.turns, mx.heads
    w_in = a["gla_w_in" if mx.gla else "hgrn_w_in"][0].rearrange("(k p) n -> p k n", p=P)
    s0 = a["state_gla" if mx.gla else "state_hgrn"][0, 0]
    s_new = out[3 if mx.gla else 2][0, 0]
    L, E = len(mx.late), len(mx.early)
    POOL_LEVELS = 3
    DVE_LEVELS = NL - POOL_LEVELS
    NTR = 10 + NT * NV
    NG = (NTR + 7) // 8
    KVR = 4 // NV
    WITH_STATE = [(0, 0), (0, 1), (0, 2), (0, 4), (1, 3), (1, 2), (1, 1), (1, 4)]
    tag = "gla" if mx.gla else "hgrn"
    with ExitStack() as s:
        sb = lambda n, sh, dt=F32: s.enter_context(nc.sbuf_tensor(f"{n}_{tag}", sh, dt))
        sem = stage_semaphores(nc, s, f"_{tag}")
        ps = lambda n, sh: s.enter_context(nc.psum_tensor(f"{n}_{tag}", sh, F32))
        w_raw = [sb(f"w_raw{i}", [P, DC, P]) for i in range(2)]
        w_hi = [sb(f"w_hi{i}", [P, DC, P], F32R) for i in range(2)]
        w_lo = [sb(f"w_lo{i}", [P, DC, P], F32R) for i in range(2)]
        zc = sb("zc", [P, 2, T])
        q = sb("q", [P, T])
        k2 = sb("k2", [P, 2, T])
        g2 = sb("g2", [P, 2, T])
        t2 = sb("t2", [P, 2, T])
        b2 = sb("b2", [P, 2, T])
        e2 = sb("e2", [P, 2, T])
        kd = sb("kdiag", [P, T])
        v = sb("v", [P, NV, T])
        og = sb("og", [P, NV, T])
        ex = sb("ex", [P, 2, NL, T])
        am = [sb(f"am{i}", [P, NL + 1, P]) for i in range(2)]
        tt = sb("tt", [P, NTR, P])
        S = sb("S", [P, 2, NT, DV])
        ebl = sb("ebl", [P, 2, NT])
        pp = [ps(f"pp{i}", [P, 512]) for i in range(2)]
        pA = [ps(f"pA{i}", [P, NL + 1, P]) for i in range(2)]
        pX = ps("pX", [P, 4, P])
        pO = ps("pO", [P, 4, P])
        (w_hi_done, w_lo_done, proj, copied, f_ready, ln_done, b_ready, pool_diff, e_ready, exp_done, qk_ready,
         ex_ready, turned, turned_out, kv, s_done, att, masked, o_done, o_out, s_in, s_out, og_done, og_out) = (
            sem(n) for n in ("w_hi_done", "w_lo_done", "proj", "copied", "f_ready", "ln_done", "b_ready",
                             "pool_diff", "e_ready", "exp_done", "qk_ready", "ex_ready", "turned", "turned_out",
                             "kv", "s_done", "att", "masked", "o_done", "o_out", "s_in", "s_out", "og_done",
                             "og_out"))
        weighted, dve_diff, sig_done, q_sig_done, sp_passed, act_passed = (sem(n) for n in
            ("weighted", "dve_diff", "sig_done", "q_sig_done", "sp_passed", "act_passed"))
        w_loaded = [sem(f"w_loaded{i}") for i in range(2)]
        if mx.gla:
            wg = sb("wg", [P, 2, P])
            lowT = sb("lowT", [P, T])
            wg_in, wg_zero, conv_done = (sem(n) for n in ("wg_in", "wg_zero", "conv_done"))
        block = s.enter_context(nc.Block())
        PRE = 1 if mx.gla else 0
        per_buf = [len([j for j in range(NCH) if j % 2 == b]) for b in range(2)]
        early_buf = [len([j for j in range(L, NCH) if j % 2 == b]) for b in range(2)]

        def column(h, j):
            _, col0, step = mx.chunks[j]
            return h * step + (col0 + (step if j >= L else 0))

        def loaded_value(h, j):
            b = j % 2
            low = PRE if b == 0 else 0
            return h * (16 * per_buf[b]) + 16 * (low + early_buf[b] + j // 2 + 1)

        def chunks_done(h, j):
            return h * NCH + (PRE + E + j + 1)

        def turn_of(j):
            return j

        def halves_done(h, turn, i):
            return h * (2 * TURNS) + (2 * (PRE + TURNS - L + turn) + i + 1)

        def before(h, j):
            if j >= 2 and not (isinstance(h, int) and h == -1 and j - 2 < L):
                return 0, j - 2
            if isinstance(h, int) and h == -1:
                return "low" if PRE and j % 2 == 0 else None
            return -1, NCH - 1 if (NCH - 1) % 2 == j else NCH - 2

        def split_free(h, j):
            last = before(h, j)
            return last if last is None else 1 if last == "low" else chunks_done(h, last[0] * NCH + last[1])

        def used(h, j):
            last = before(h, j)
            return last if last is None else 2 if last == "low" else \
                halves_done(h, last[0] * TURNS + turn_of(last[1]), 1)

        def exponents(tensor_tensor, l):
            m = LEVELS[l]
            nb = T // (2 * m)
            bf, bb, qs, ks = (x.rearrange("p (n h m) -> p n h m", h=2, m=m) for x in
                              (b2[:, 0, :], b2[:, 1, :], ex[:, 0, l, :], ex[:, 1, l, :]))
            rf = bf[:, :, 0, m - 1:m].to_broadcast([P, nb, m])
            rb = bb[:, :, 1, 0:1].to_broadcast([P, nb, m])
            tensor_tensor(qs[:, :, 1, :], bf[:, :, 1, :], rf, ALU.subtract)
            tensor_tensor(ks[:, :, 0, :], rf, bf[:, :, 0, :], ALU.subtract)
            tensor_tensor(qs[:, :, 0, :], bb[:, :, 0, :], rb, ALU.subtract)
            tensor_tensor(ks[:, :, 1, :], rb, bb[:, :, 1, :], ALU.subtract)

        @block.sync
        def _(sp):
            def load(h, j):
                if split_free(h, j) is not None:
                    sp.wait_ge(w_lo_done, split_free(h, j))
                    alone(sp, sp_passed)
                sp.dma_start(w_raw[j % 2][:, :, :], w_in[:, :, bass.ds(column(h, j), P)]) \
                    .then_inc(w_loaded[j % 2], 16)

            def load_gates(h):
                for d in range(2):
                    sp.dma_start(wg[96 + 16 * d:112 + 16 * d, d, :],
                                 a["gla_w_gate"][0, d][:, bass.ds(h * P, P)]).then_inc(wg_in, 16)

            def head(h, final):
                sp.wait_ge(o_done, h * NT + 1)
                alone(sp, sp_passed)
                sp.wait_ge(s_out, h * 32 + 32)
                sp.dma_start(S[:, 0, 0, :], s0[0][bass.ds(h, 1)].rearrange("o p v -> p (o v)")).then_inc(s_in, 16)
                sp.dma_start(S[:, 1, 3, :], s0[1][bass.ds(h, 1)].rearrange("o p v -> p (o v)")).then_inc(s_in, 16)
                for j in range(2, NCH):
                    if j < L or not final:
                        load(h, j)
                if mx.gla and not final:
                    sp.wait_ge(proj, halves_done(h, -1, 1))
                    alone(sp, sp_passed)
                    load_gates(h + 1)
                sp.wait_ge(og_done, h + 1)
                sp.dma_start(og_sp[bass.ds(h * NV, NV)].rearrange("n p t -> p n t"), og[:, :, :]).then_inc(og_out, 16)
                if not final:
                    load(h + 1, 0)
                    load(h + 1, 1)
                sp.wait_ge(s_done, h * 8 + 8)
                for d in range(2):
                    sp.dma_start(s_new[d][bass.ds(h, 1)].rearrange("o p v -> p (o v)"), S[:, d, 4, :]) \
                        .then_inc(s_out, 16)

            sp.sem_inc(s_out, 32)
            sp.sem_inc(og_out, 16)
            if mx.gla:
                sp.dma_start(w_raw[0][:, :, :], w_in[:, :, 3104 - P:3104]).then_inc(w_loaded[0], 16)
                sp.wait_ge(wg_zero, 1)
                load_gates(0)
            for j in range(L, NCH):
                load(-1, j)
            load(0, 0)
            load(0, 1)
            with sp.Fori(0, H - 1) as h:
                head(h, False)
            head(H - 1, True)
            sp.wait_ge(s_out, 32 * H + 32)
            sp.wait_ge(og_out, 16 * H + 16)

        @block.gpsimd
        def _(pool):
            def lo(h, j):
                pool.wait_ge(w_hi_done, chunks_done(h, j))
                b = j % 2
                pool.tensor_tensor(w_lo[b][:, :, :], w_raw[b][:, :, :], w_hi[b][:, :, :].bitcast(F32),
                                   ALU.subtract).then_inc(w_lo_done, 1)

            def head(h, final):
                for j in range(2, min(4, NCH)):
                    if j < L or not final:
                        lo(h, j)
                pool.wait_ge(b_ready, h + 1)
                for l in range(POOL_LEVELS):
                    exponents(pool.tensor_tensor, l)
                    pool.drain().then_inc(pool_diff, 1)
                if not final:
                    for j in range(4, NCH):
                        lo(h, j)
                    lo(h + 1, 0)
                    lo(h + 1, 1)

            if mx.gla:
                pool.memset(wg[:, :, :], 0.0)
                pool.drain().then_inc(wg_zero, 1)
                pool.wait_ge(w_hi_done, 1)
                pool.tensor_tensor(w_lo[0][:, :, :], w_raw[0][:, :, :], w_hi[0][:, :, :].bitcast(F32),
                                   ALU.subtract).then_inc(w_lo_done, 1)
            for j in range(L, NCH):
                lo(-1, j)
            lo(0, 0)
            lo(0, 1)
            with pool.Fori(0, H - 1) as h:
                head(h, False)
            head(H - 1, True)

        @block.scalar
        def _(act):
            def hi(h, j):
                b = j % 2
                act.wait_ge(w_loaded[b], loaded_value(h, j))
                if used(h, j) is not None:
                    act.wait_ge(proj, used(h, j))
                act.activation(w_hi[b][:, :, :], w_raw[b][:, :, :], ACT.Copy).then_inc(w_hi_done, 1)

            def next_hi(h, j, final):
                if j + 2 < NCH:
                    if j + 2 < L or not final:
                        hi(h, j + 2)
                elif not final:
                    if NCH % 2 == 0:
                        hi(h + 1, j + 2 - NCH)
                    elif j == NCH - 1:
                        hi(h + 1, 0)
                        hi(h + 1, 1)

            def copy(dst, turn, h, func=ACT.Copy, bias=None):
                for i, cols in halves():
                    act.wait_ge(proj, halves_done(h, turn, i))
                    if bias is not None:
                        alone(act, act_passed)
                    kw = {"bias": bias} if bias is not None else {}
                    act.activation(dst[:, cols], pp[i][:, 0:HALF], func, **kw).then_inc(copied, 1)

            def early(h, n):
                if mx.gla and n >= E:
                    d = n - E
                    bg = VEC["b_gate"] + 4 * d
                    copy(g2[:, d, :], L + n, h, ACT.Identity, bias=c["vec"][:, bass.ds(h + (bg + 1), 1)])
                    return
                if mx.gla:
                    copy(zc[:, n, :], L + n, h)
                elif n < 2:
                    copy(g2[:, n, :], L + n, h)
                else:
                    copy(zc[:, 0, :], L + n, h)
                next_hi(h, L + n, False)

            def output_gates(h, n, final):
                if n == 0:
                    act.wait_ge(og_out, h * 16 + 16)
                copy(og[:, n, :], NV + n, h)
                next_hi(h, NV + n, final)

            def head(h, final):
                if mx.gla:
                    act.drain()
                    act.activation(b2[:, :, :], g2[:, :, :], ACT.Abs)
                    act.drain()
                    act.activation(b2[:, :, :], b2[:, :, :], ACT.Exp, scale=-1.0)
                    act.drain()
                    act.activation(b2[:, :, :], b2[:, :, :], ACT.Ln, bias=c["one"][:, 0:1])
                    act.drain().then_inc(ln_done, 1)
                    dests = [k2[:, 0, :], q[:, :], v[:, 0, :], v[:, 1, :]]

                    def sig(j):
                        act.wait_ge(conv_done, h * 4 + (j + 1))
                        act.activation(t2[:, j % 2, :], dests[j], ACT.Sigmoid).then_inc(sig_done, 1)

                    for j in range(2):
                        sig(j)
                        copy(zc[:, j, :], j, h)
                        next_hi(h, j, final)
                    output_gates(h, 0, final)
                    sig(2)
                    output_gates(h, 1, final)
                    act.drain().then_inc(og_done, 1)
                    sig(3)
                else:
                    act.drain()
                    act.activation(k2[:, :, :], g2[:, :, :], ACT.Sigmoid, scale=-1.0)
                    act.drain()
                    act.activation(g2[:, :, :], g2[:, :, :], ACT.Sigmoid)
                    act.drain().then_inc(sig_done, 1)
                    act.activation(zc[:, 1, :], zc[:, 0, :], ACT.Sigmoid).then_inc(q_sig_done, 1)
                    copy(v[:, 0, :], 0, h)
                    next_hi(h, 0, final)
                    act.wait_ge(f_ready, h + 1)
                    act.activation(t2[:, :, :], t2[:, :, :], ACT.Ln).then_inc(ln_done, 1)
                    output_gates(h, 0, final)
                    act.drain().then_inc(og_done, 1)
                act.wait_ge(e_ready, h + 1)
                act.activation(e2[:, :, :], b2[:, :, :], ACT.Exp)
                act.activation(t2[:, :, :], t2[:, :, :], ACT.Exp)
                act.drain().then_inc(exp_done, 1)
                if not final:
                    early(h, 0)
                for g in range(NG):
                    n = min(8, NTR - 8 * g)
                    act.wait_ge(turned, h * NG + (g + 1))
                    act.activation(tt[:, 8 * g:8 * g + n, :], pA[g % 2][:, 0:n, :], ACT.Copy).then_inc(turned_out, 1)
                for n, levels in ((1, (0, 1, 2)), (2, (3, 4, 5, 6)), (3, ())):
                    for l in levels:
                        if l < POOL_LEVELS:
                            act.wait_ge(pool_diff, h * POOL_LEVELS + (l + 1))
                        else:
                            act.wait_ge(dve_diff, h * DVE_LEVELS + (l - POOL_LEVELS + 1))
                        act.activation(ex[:, :, l, :], ex[:, :, l, :], ACT.Exp).then_inc(ex_ready, 1)
                    if n < E + mx.extra and not final:
                        early(h, n)
                for t in range(NT):
                    act.wait_ge(o_done, h * NT + (1 + t + 1))
                    act.activation(oT[:, bass.ds(h * NV, NV), t * P:(t + 1) * P],
                                   pO[:, 0:NV, :], ACT.Copy).then_inc(o_out, 1)

            act.sem_inc(o_out, 1)
            if mx.gla:
                act.wait_ge(w_loaded[0], 16)
                act.activation(w_hi[0][:, :, :], w_raw[0][:, :, :], ACT.Copy).then_inc(w_hi_done, 1)
                for i, cols in halves():
                    act.wait_ge(proj, i + 1)
                    act.activation(lowT[:, cols], pp[i][:, 0:HALF], ACT.Copy).then_inc(copied, 1)
            hi(-1, L)
            hi(-1, L + 1)
            for n in range(E + mx.extra):
                early(-1, n)
            with act.Fori(0, H - 1) as h:
                head(h, False)
            head(H - 1, True)

        @block.vector
        def _(dve):
            def conv(h, j, dst, tap0, zsl):
                nc.vector.tensor_scalar(dst, zsl, tap_ap(h, 1, 1, tap0), None, ALU.mult)
                dve.drain()
                gz = zsl[:, 0:TS].rearrange("p (r w) -> p r w", w=GRID_W)
                gd = dst[:, 0:TS].rearrange("p (r w) -> p r w", w=GRID_W)
                for y in range(3):
                    for x in range(3):
                        if (y, x) == (1, 1):
                            continue
                        r0, r1 = max(0, 1 - y), min(ROWS, ROWS + 1 - y)
                        w0, w1 = max(0, 1 - x), min(GRID_W, GRID_W + 1 - x)
                        if y == 1:
                            u0, u1 = TS + max(0, 1 - x), TS + min(TC, TC + 1 - x)
                            nc.vector.scalar_tensor_tensor(dst[:, u0:u1], zsl[:, u0 + x - 1:u1 + x - 1],
                                                           tap_ap(h, y, x, tap0), dst[:, u0:u1], ALU.mult, ALU.add)
                        nc.vector.scalar_tensor_tensor(
                            gd[:, r0:r1, w0:w1], gz[:, r0 + y - 1:r1 + y - 1, w0 + x - 1:w1 + x - 1],
                            tap_ap(h, y, x, tap0), gd[:, r0:r1, w0:w1], ALU.mult, ALU.add)
                        dve.drain()

            def scan(h):
                nc.vector.tensor_tensor_scan(b2[:, 0, :], c["scan_f"][:, :], g2[:, 0, :], 0.0, ALU.mult, ALU.add)
                nc.vector.tensor_tensor_scan(b2[:, 1, ::-1], c["scan_b"][:, ::-1], g2[:, 1, ::-1], 0.0,
                                             ALU.mult, ALU.add)
                dve.drain().then_inc(b_ready, 1)

            def tap_ap(h, y, x, tap0):
                n = 3 * y + x
                first = (VEC["conv"] + 16 * n if n < 8 else VEC["conv8"]) + tap0[0]
                return c["vec"][:, bass.ds(h * tap0[1] + first, 1)]

            dve.sem_inc(masked, 1)

            def head(h, final):
                if mx.gla:
                    dests = [k2[:, 0, :], q[:, :], v[:, 0, :], v[:, 1, :]]
                    where = [(4, 1), (0, 1), (8, 2), (9, 2)]
                    scales = [1.0, float(P) ** -0.5, 1.0, 1.0]

                    def silu(j):
                        dve.wait_ge(sig_done, h * 4 + (j + 1))
                        nc.vector.scalar_tensor_tensor(dests[j], dests[j], scales[j], t2[:, j % 2, :],
                                                       ALU.mult, ALU.mult)

                    for j in range(4):
                        dve.wait_ge(copied, halves_done(h, L + j - TURNS if j < 2 else j - 2, 1))
                        conv(h, j, dests[j], where[j], zc[:, j % 2, :])
                        dve.drain().then_inc(conv_done, 1)
                        if j == 0:
                            dve.wait_ge(ln_done, h + 1)
                            nc.vector.scalar_tensor_tensor(g2[:, :, :], g2[:, :, :], 0.0, b2[:, :, :],
                                                           ALU.min, ALU.subtract)
                            dve.drain()
                            nc.vector.tensor_scalar(g2[:, :, :], g2[:, :, :], 1.0 / 16.0, None, ALU.mult)
                            dve.drain()
                        if j == 1:
                            scan(h)
                        if j >= 1:
                            silu(j - 1)
                            dve.drain()
                    silu(3)
                    dve.drain()
                    nc.vector.tensor_scalar(kd[:, :], k2[:, 0, :], 2.0, None, ALU.mult)
                    nc.vector.tensor_copy(k2[:, 1, :], k2[:, 0, :])
                    dve.drain()
                else:
                    dve.wait_ge(sig_done, h + 1)
                    for d in range(2):
                        oml = c["oml"][:, bass.ds(h + 8 * d, 1)]
                        nc.vector.tensor_scalar(t2[:, d, :], g2[:, d, :], oml, c["lb"][:, bass.ds(h + 8 * d, 1)],
                                                ALU.mult, ALU.add)
                        nc.vector.tensor_scalar(k2[:, d, :], k2[:, d, :], oml, None, ALU.mult)
                    dve.drain()
                    nc.vector.tensor_scalar(t2[:, :, :], t2[:, :, :], F_MIN, None, ALU.max)
                    dve.drain()
                    nc.vector.tensor_scalar(g2[:, :, :], t2[:, :, :], LN_LOW, LN_UP, ALU.is_lt, ALU.mult)
                    dve.drain()
                    nc.vector.scalar_tensor_tensor(t2[:, :, :], g2[:, :, :], 1.0, t2[:, :, :], ALU.add, ALU.mult)
                    dve.drain().then_inc(f_ready, 1)
                    nc.vector.tensor_add(kd[:, :], k2[:, 0, :], k2[:, 1, :])
                    dve.wait_ge(q_sig_done, h + 1)
                    nc.vector.tensor_mul(q[:, :], zc[:, 0, :], zc[:, 1, :])
                    dve.wait_ge(ln_done, h + 1)
                    nc.vector.scalar_tensor_tensor(g2[:, :, :], g2[:, :, :], LN_FIX, t2[:, :, :], ALU.mult, ALU.add)
                    dve.drain()
                    scan(h)
                for d, e in ((0, P - 1), (1, 0)):
                    bv = b2[:, d, :].rearrange("p (n t) -> p n t", t=P)
                    nc.vector.tensor_tensor(t2[:, d, :].rearrange("p (n t) -> p n t", t=P),
                                            bv[:, :, e:e + 1].to_broadcast([P, NT, P]), bv, ALU.subtract)
                dve.drain().then_inc(e_ready, 1)
                dve.wait_ge(exp_done, h + 1)
                for d, e in ((0, P - 1), (1, 0)):
                    nc.vector.tensor_copy(ebl[:, d, :], e2[:, d, :].rearrange("p (n t) -> p n t", t=P)[:, :, e])
                dve.drain()
                for d in range(2):
                    nc.vector.tensor_mul(e2[:, d, :], e2[:, d, :], q[:, :])
                    nc.vector.tensor_mul(t2[:, d, :], t2[:, d, :], k2[:, d, :])
                dve.drain().then_inc(qk_ready, 1)
                for l in range(POOL_LEVELS, NL):
                    exponents(nc.vector.tensor_tensor, l)
                    dve.drain().then_inc(dve_diff, 1)
                dve.wait_ge(s_in, h * 32 + 32)
                for i, (d, t) in enumerate(WITH_STATE):
                    dve.wait_ge(kv, h * 8 + (i // KVR + 1) * KVR)
                    r = (i % KVR) * NV
                    update = (pX, pO)[i // KVR % 2][:, r:r + NV, :].rearrange("p a b -> p (a b)")
                    if t == NT - 1:
                        nc.vector.tensor_copy(S[:, d, t, :], update)
                    else:
                        nxt = t + 1 if d == 0 else t - 1
                        nc.vector.scalar_tensor_tensor(S[:, d, nxt, :], S[:, d, t, :], ebl[:, d, t:t + 1],
                                                       update, ALU.mult, ALU.add)
                    dve.drain().then_inc(s_done, 1)
                for l, m in enumerate(LEVELS):
                    dve.wait_ge(ex_ready, h * NL + (l + 1))
                    nc.vector.tensor_mul(ex[:, 0, l, :], ex[:, 0, l, :], q[:, :])
                    for d in range(2):
                        kv_ = k2[:, d, :].rearrange("p (n h m) -> p n h m", h=2, m=m)[:, :, d, :]
                        ks = ex[:, 1, l, :].rearrange("p (n h m) -> p n h m", h=2, m=m)[:, :, d, :]
                        nc.vector.tensor_mul(ks, ks, kv_)
                dve.drain().then_inc(weighted, 1)
                for t in range(NT):
                    dve.wait_ge(att, h * NT + (t + 1))
                    dve.wait_ge(o_done, h * NT + (1 + (t - 1 if t >= 2 else 0)))
                    nc.vector.tensor_mul(am[t % 2][:, :, :], pA[t % 2][:, :, :], c["level_mask"][:, :, :]) \
                        .then_inc(masked, 1)

            with dve.Fori(0, H - 1) as h:
                head(h, False)
            head(H - 1, True)

        @block.tensor
        def _(pe):
            pe.sem_inc(o_done, 1)

            def free(h, turn, i):
                if not (isinstance(h, int) and h == -1 and PRE == 0 and turn == L):
                    pe.wait_ge(copied, halves_done(h, turn - 1, i))

            def project(h, j):
                pe.wait_ge(w_lo_done, chunks_done(h, j))
                for i, cols in halves():
                    free(h, j, i)
                    split_product(nc, pp[i][:, 0:HALF], w_hi[j % 2], w_lo[j % 2], h_hi, h_lo, cols).then_inc(proj, 1)

            def project_early(h):
                for j in range(L + 1, NCH):
                    project(h, j)
                if mx.gla:
                    pe.wait_ge(wg_in, h * 32 + 64)
                    for d in range(2):
                        for i, cols in halves():
                            free(h, NCH + d, i)
                            nc.tensor.matmul(pp[i][:, 0:HALF], wg[96:128, d, :], lowT[96:128, cols],
                                             start=True, stop=True).then_inc(proj, 1)

            def head(h, final):
                for j in range(L):
                    project(h, j)
                if not final:
                    project(h, L)
                pe.wait_ge(qk_ready, h + 1)
                for g in range(NG):
                    if g >= 2:
                        pe.wait_ge(turned_out, h * NG + (g - 1))
                    for r in range(min(8, NTR - 8 * g)):
                        n = 8 * g + r
                        if n < 10:
                            src = t2[:, n // NT, (n % NT) * P:(n % NT + 1) * P]
                        else:
                            t, vv = (n - 10) // NV, (n - 10) % NV
                            src = v[:, vv, t * P:(t + 1) * P]
                        last = nc.tensor.transpose(pA[g % 2][:, r, :], src, c["ident"][:, :])
                    last.then_inc(turned, 1)
                pe.wait_ge(turned_out, h * NG + NG)
                pe.wait_ge(o_out, h * NT + 1)
                for i, (d, t) in enumerate(WITH_STATE):
                    if i >= 2 * KVR and i % KVR == 0:
                        pe.wait_ge(s_done, h * 8 + (i - KVR))
                    r = (i % KVR) * NV
                    nc.tensor.matmul((pX, pO)[i // KVR % 2][:, r:r + NV, :], tt[:, d * NT + t, :],
                                     tt[:, 10 + t * NV:10 + t * NV + NV, :], start=True, stop=True).then_inc(kv, 1)
                if not final:
                    project_early(h)
                pe.wait_ge(weighted, h + 1)
                pe.wait_ge(s_done, h * 8 + 8)

                def scores(t):
                    pe.wait_ge(masked, h * NT + (1 + (t - 1 if t >= 2 else 0)))
                    tok = slice(t * P, (t + 1) * P)
                    for l in range(NL):
                        nc.tensor.matmul(pA[t % 2][:, l, :], ex[:, 1, l, tok], ex[:, 0, l, tok], start=True, stop=True)
                    nc.tensor.matmul(pA[t % 2][:, NL, :], kd[:, tok], q[:, tok], start=True, stop=True) \
                        .then_inc(att, 1)

                scores(0)
                for t in range(NT):
                    if t + 1 < NT:
                        scores(t + 1)
                    pe.wait_ge(masked, h * NT + (1 + t + 1))
                    pe.wait_ge(o_out, h * NT + (1 + t))
                    tok = slice(t * P, (t + 1) * P)
                    for vv in range(NV):
                        dst = pO[:, vv, :]
                        terms = [(tt[:, 10 + t * NV + vv, :], am[t % 2][:, l, :]) for l in range(NL + 1)]
                        if t < NT - 1:
                            terms += [(S[:, d, t, vv * P:(vv + 1) * P], e2[:, d, tok]) for d in range(2)]
                        for n, (lhsT, rhs) in enumerate(terms):
                            last = nc.tensor.matmul(dst, lhsT, rhs, start=(n == 0), stop=(n == len(terms) - 1))
                    last.then_inc(o_done, 1)

            if mx.gla:
                pe.wait_ge(w_lo_done, 1)
                for i, cols in halves():
                    split_product(nc, pp[i][:, 0:HALF], w_hi[0], w_lo[0], h_hi, h_lo, cols).then_inc(proj, 1)
            project(-1, L)
            project_early(-1)
            with pe.Fori(0, H - 1) as h:
                head(h, False)
            head(H - 1, True)


def mix_out(nc, a, c, mx, h_hi, h_lo, oT, og_sp, x_sp, layer):
    NV, H = mx.nv, mx.heads
    w_out = a["gla_w_out" if mx.gla else "hgrn_w_out"][0].rearrange("(k p) n -> p k n", p=P)
    gw = VEC["gla_g" if mx.gla else "hgrn_g"]
    with ExitStack() as s:
        sb = lambda n, sh, dt=F32: s.enter_context(nc.sbuf_tensor(f"{n}_mo{layer}", sh, dt))
        sem = stage_semaphores(nc, s, f"_mo{layer}")
        ps = lambda n, sh: s.enter_context(nc.psum_tensor(f"{n}_mo{layer}", sh, F32))
        xT = sb("x", [P, DC, T])
        og = sb("og", [P, DC, T])
        sg = [sb(f"sg{i}", [P, T]) for i in range(2)]
        sq = [sb(f"sq{i}", [P, T]) for i in range(2)]
        rs = sb("rs", [P, T])
        y = [sb(f"y{i}", [P, T]) for i in range(2)]
        w_raw = [sb(f"w_raw{i}", [P, DC, P]) for i in range(2)]
        w_hi = [sb(f"w_hi{i}", [P, DC, P], F32R) for i in range(2)]
        w_lo = [sb(f"w_lo{i}", [P, DC, P], F32R) for i in range(2)]
        ms = [ps(f"ms{i}", [P, 512]) for i in range(2)]
        pp = [ps(f"pp{i}", [P, 512]) for i in range(4)]
        (x_in, og_in, sig_done, silu_done, sq_done, summed, ms_out, inv, rooted, y_done, hi_done, lo_done,
         w_hi_done, w_lo_done, proj, added, x_out) = (sem(n) for n in (
            "x_in", "og_in", "sig_done", "silu_done", "sq_done", "summed", "ms_out", "inv", "rooted", "y_done",
            "hi_done", "lo_done", "w_hi_done", "w_lo_done", "proj", "added", "x_out"))
        w_loaded = [sem(f"w_loaded{i}") for i in range(2)]
        block = s.enter_context(nc.Block())

        @block.sync
        def _(sp):
            sp.dma_start(og[:, :, :], og_sp.rearrange("k p t -> p k t")).then_inc(og_in, 16)
            sp.dma_start(xT[:, :, :], x_sp).then_inc(x_in, 16)
            with sp.Fori(0, DC // 2) as i:
                for b in range(2):
                    sp.wait_ge(w_lo_done, i * 2 + (b + 1))
                    sp.dma_start(w_raw[b][:, :, :], w_out[:, :, bass.ds(i * (2 * P) + b * P, P)]) \
                        .then_inc(w_loaded[b], 16)
            sp.wait_ge(added, 4 + 2 * DC)
            sp.dma_start(x_sp, xT[:, :, :]).then_inc(x_out, 16)
            sp.wait_ge(x_out, 16)

        @block.gpsimd
        def _(pool):
            pool.sem_inc(w_lo_done, 2)
            with pool.Fori(0, DC // 2) as i:
                for b in range(2):
                    pool.wait_ge(w_hi_done, i * 2 + (b + 1))
                    pool.tensor_tensor(w_lo[b][:, :, :], w_raw[b][:, :, :], w_hi[b][:, :, :].bitcast(F32),
                                       ALU.subtract).then_inc(w_lo_done, 1)

        @block.scalar
        def _(act):
            def hi(b, i):
                act.wait_ge(w_loaded[b], i * 16 + 16)
                act.wait_ge(proj, i * 4 + (2 * b + 2))
                act.activation(w_hi[b][:, :, :], w_raw[b][:, :, :], ACT.Copy).then_inc(w_hi_done, 1)

            act.wait_ge(og_in, 16)
            for k in range(DC):
                if k >= 2:
                    act.wait_ge(silu_done, k - 1)
                act.activation(sg[k % 2][:, :], og[:, k, :], ACT.Sigmoid).then_inc(sig_done, 1)
            for g in range(H):
                for k in range(g * NV, (g + 1) * NV):
                    if k >= 2:
                        act.wait_ge(summed, k - 1)
                    act.activation(sq[k % 2][:, :], oT[:, k, :], ACT.Square).then_inc(sq_done, 1)
                act.wait_ge(inv, g + 1)
                act.activation(rs[:, :], rs[:, :], ACT.Sqrt).then_inc(rooted, 1)
                for k in range(g * NV, (g + 1) * NV):
                    act.wait_ge(y_done, k + 1)
                    act.activation(h_hi[:, k, :], y[k % 2][:, :], ACT.Copy).then_inc(hi_done, 1)
            with act.Fori(0, DC // 2) as i:
                hi(0, i)
                hi(1, i)

        @block.tensor
        def _(pe):
            pe.sem_inc(proj, 4)
            for k in range(DC):
                pe.wait_ge(sq_done, k + 1)
                if k % NV == 0 and k:
                    pe.wait_ge(ms_out, k // NV)
                for i, cols in halves():
                    last = nc.tensor.matmul(ms[i][:, 0:HALF], c["ones_d"][:, :], sq[k % 2][:, cols],
                                            start=(k % NV == 0), stop=(k % NV == NV - 1))
                last.then_inc(summed, 1)
            pe.wait_ge(lo_done, DC)
            with pe.Fori(0, DC // 2) as n:
                for b in range(2):
                    pe.wait_ge(w_lo_done, n * 2 + (2 + b + 1))
                    for i, cols in halves():
                        pe.wait_ge(added, n * 4 + (2 * b + i + 1))
                        split_product(nc, pp[2 * b + i][:, 0:HALF], w_hi[b], w_lo[b], h_hi, h_lo, cols) \
                            .then_inc(proj, 1)

        @block.vector
        def _(dve):
            dve.sem_inc(added, 4)
            for k in range(DC):
                dve.wait_ge(sig_done, k + 1)
                nc.vector.tensor_mul(og[:, k, :], og[:, k, :], sg[k % 2][:, :]).then_inc(silu_done, 1)

            for g in range(H):
                dve.wait_ge(summed, (g + 1) * NV)
                for i, cols in halves():
                    nc.vector.tensor_scalar(rs[:, cols], ms[i][:, 0:HALF], float(D / mx.dv), EPS, ALU.mult, ALU.add)
                dve.drain().then_inc(ms_out, 1)
                nc.vector.reciprocal(rs[:, :], rs[:, :])
                dve.drain().then_inc(inv, 1)
                dve.wait_ge(rooted, g + 1)
                for k in range(g * NV, (g + 1) * NV):
                    nc.vector.scalar_tensor_tensor(y[k % 2][:, :], oT[:, k, :],
                                                   c["vec"][:, gw + k % NV:gw + k % NV + 1], rs[:, :],
                                                   ALU.mult, ALU.mult)
                    dve.drain()
                    nc.vector.tensor_mul(y[k % 2][:, :], y[k % 2][:, :], og[:, k, :])
                    dve.drain().then_inc(y_done, 1)
                    dve.wait_ge(hi_done, k + 1)
                    nc.vector.tensor_sub(h_lo[:, k, :], y[k % 2][:, :], h_hi[:, k, :].bitcast(F32)) \
                        .then_inc(lo_done, 1)
            dve.wait_ge(x_in, 16)
            with dve.Fori(0, DC // 2) as n:
                for b in range(2):
                    for i in range(2):
                        dve.wait_ge(proj, n * 4 + (4 + 2 * b + i + 1))
                        src = pp[2 * b + i]
                        k = n * 2 + b
                        for vec, c0, c1 in ((0, 0, HALF),) if i == 0 else ((0, HALF, TS), (1, TS, T)):
                            xs = xT[:, bass.ds(k, 1), c0:c1].rearrange("p o t -> p (o t)")
                            nc.vector.scalar_tensor_tensor(
                                xs, src[:, c0 - i * HALF:c1 - i * HALF],
                                c["mod"][:, layer, bass.ds(k + 16, 1), vec], xs, ALU.mult, ALU.add)
                        dve.drain().then_inc(added, 1)


def retrieve(nc, a, c, h_hi, h_lo, chosen, layer):
    w_q = a["peer_w_q"][layer].rearrange("(k p) n -> p k n", p=P)
    keys = a["peer_keys"][layer]
    NCAND = 88
    LOWEST = -3.0e38
    with ExitStack() as s:
        sb = lambda n, sh, dt=F32: s.enter_context(nc.sbuf_tensor(f"{n}_re{layer}", sh, dt))
        sem = stage_semaphores(nc, s, f"_re{layer}")
        ps = lambda n, sh: s.enter_context(nc.psum_tensor(f"{n}_re{layer}", sh, F32))
        w_raw = [sb(f"w_raw{i}", [P, DC, P]) for i in range(2)]
        w_hi = [sb(f"w_hi{i}", [P, DC, P], F32R) for i in range(2)]
        w_lo = [sb(f"w_lo{i}", [P, DC, P], F32R) for i in range(2)]
        kraw = [sb(f"kraw{i}", [P, P]) for i in range(2)]
        kT = [sb(f"kT{i}", [P, P]) for i in range(2)]
        qT = [sb(f"qT{i}", [P, T]) for i in range(2)]
        top = sb("top", [P, 2, NT, TOPK])
        idx = sb("idx", [P, 2, NT, TOPK], U32)
        rest = sb("rest", [P, NT, P])
        cand = sb("cand", [P, NT, NCAND])
        crest = sb("crest", [P, NT, NCAND])
        ctop = sb("ctop", [P, NT, TOPK])
        cpos = sb("cpos", [P, NT, TOPK], U32)
        pq = [ps(f"pq{i}", [P, 512]) for i in range(2)]
        pk = ps("pk", [P, P])
        pS = [ps(f"pS{i}", [P, 8, P]) for i in range(2)]
        w_hi_done, w_lo_done, proj, q_out, k_turned, k_out, scored, read = (sem(n) for n in
            ("w_hi_done", "w_lo_done", "proj", "q_out", "k_turned", "k_out", "scored", "read"))
        w_loaded = [sem(f"w_loaded{i}") for i in range(2)]
        k_loaded = [sem(f"k_loaded{i}") for i in range(2)]
        dve_passed = sem("dve_passed")
        block = s.enter_context(nc.Block())

        @block.sync
        def _(sp):
            with sp.Fori(0, PH) as h:
                for b in range(2):
                    sp.wait_ge(w_lo_done, h * 2 + (b + 1))
                    sp.dma_start(w_raw[b][:, :, :], w_q[:, :, bass.ds(h * (2 * P) + b * P, P)]) \
                        .then_inc(w_loaded[b], 16)
                    sp.wait_ge(k_turned, h * 2 + (b + 1))
                    sp.dma_start(kraw[b][:, :], keys[bass.ds(h, 1), b].rearrange("o n k -> (o n) k")) \
                        .then_inc(k_loaded[b], 16)

        @block.gpsimd
        def _(pool):
            pool.sem_inc(w_lo_done, 2)
            with pool.Fori(0, PH) as h:
                for b in range(2):
                    pool.wait_ge(w_hi_done, h * 2 + (b + 1))
                    pool.tensor_tensor(w_lo[b][:, :, :], w_raw[b][:, :, :], w_hi[b][:, :, :].bitcast(F32),
                                       ALU.subtract).then_inc(w_lo_done, 1)

        @block.scalar
        def _(act):
            act.sem_inc(k_out, 1)
            act.sem_inc(q_out, 1)
            with act.Fori(0, PH) as h:
                for b in range(2):
                    act.wait_ge(w_loaded[b], h * 16 + 16)
                    act.wait_ge(proj, h * 4 + (2 * b + 2))
                    act.activation(w_hi[b][:, :, :], w_raw[b][:, :, :], ACT.Copy).then_inc(w_hi_done, 1)
                for b in range(2):
                    act.wait_ge(scored, h * 2 + (b + 1))
                    act.wait_ge(k_turned, h * 2 + (2 + b + 1))
                    act.activation(kT[b][:, :], pk[:, :], ACT.Copy).then_inc(k_out, 1)
                    for i, cols in halves():
                        act.wait_ge(proj, h * 4 + (4 + 2 * b + i + 1))
                        act.activation(qT[b][:, cols], pq[i][:, 0:HALF], ACT.Copy).then_inc(q_out, 1)

        @block.tensor
        def _(pe):
            pe.sem_inc(proj, 4)
            pe.sem_inc(k_turned, 2)
            pe.sem_inc(scored, 2)
            with pe.Fori(0, PH) as h:
                for b in range(2):
                    pe.wait_ge(k_loaded[b], h * 16 + 16)
                    pe.wait_ge(k_out, h * 2 + (1 + b))
                    nc.tensor.transpose(pk[:, :], kraw[b][:, :], c["ident"][:, :]).then_inc(k_turned, 1)
                    pe.wait_ge(w_lo_done, h * 2 + (2 + b + 1))
                    for i, cols in halves():
                        pe.wait_ge(q_out, h * 4 + (1 + (2 * b - 1 + i if b else 0)))
                        split_product(nc, pq[i][:, 0:HALF], w_hi[b], w_lo[b], h_hi, h_lo, cols).then_inc(proj, 1)
                    pe.wait_ge(q_out, h * 4 + (1 + 2 * b + 2))
                    pe.wait_ge(k_out, h * 2 + (1 + b + 1))
                    pe.wait_ge(read, h * 2 + (b + 1))
                    for t in range(NT):
                        last = nc.tensor.matmul(pS[b][:, t, :], qT[b][:, t * P:(t + 1) * P], kT[b][:, :],
                                                start=True, stop=True)
                    last.then_inc(scored, 1)

        @block.vector
        def _(dve):
            def best16(values, left, top_, idx_):
                for t in range(NT):
                    nc.vector.max(top_[:, t, 0:8], values(t))
                dve.drain()
                for t in range(NT):
                    nc.vector.max_index(idx_[:, t, 0:8], top_[:, t, 0:8], values(t))
                    nc.vector.match_replace(left[:, t, :], top_[:, t, 0:8], values(t), LOWEST)
                dve.drain()
                for t in range(NT):
                    nc.vector.max(top_[:, t, 8:16], left[:, t, :])
                dve.drain()
                for t in range(NT):
                    nc.vector.max_index(idx_[:, t, 8:16], top_[:, t, 8:16], left[:, t, :])

            dve.sem_inc(read, 2)
            with dve.Fori(0, PH) as h:
                for b in range(2):
                    dve.wait_ge(scored, h * 2 + (2 + b + 1))
                    alone(dve, dve_passed)
                    best16(lambda t: pS[b][:, t, :], rest, top[:, b], idx[:, b])
                    dve.drain().then_inc(read, 1)
                for rows, n, at in ((slice(0, 4), 16, 0), (slice(4, 8), 4, 64), (slice(8, 16), 1, 80)):
                    r = rows.stop - rows.start
                    first = top[:, 0, :, rows].unsqueeze(3).to_broadcast([P, NT, r, n])
                    second = top[:, 1, :, 0:n].unsqueeze(2).to_broadcast([P, NT, r, n])
                    nc.vector.tensor_tensor(cand[:, :, at:at + r * n].rearrange("p t (r n) -> p t r n", n=n),
                                            first, second, ALU.add)
                for f, b in ((2, 0), (3, 1)):
                    nc.vector.tensor_copy(chosen[:, f, bass.ds(h, 1)].rearrange("p o t k -> p (o t k)"),
                                          idx[:, b].rearrange("p t k -> p (t k)"))
                dve.drain()
                best16(lambda t: cand[:, t, :], crest, ctop, cpos)
                dve.drain()
                nc.vector.tensor_copy(chosen[:, 0, bass.ds(h, 1)].rearrange("p o t k -> p (o t k)"),
                                      ctop[:, :, :].rearrange("p t k -> p (t k)"))
                nc.vector.tensor_copy(chosen[:, 1, bass.ds(h, 1)].rearrange("p o t k -> p (o t k)").bitcast(U32),
                                      cpos[:, :, :].rearrange("p t k -> p (t k)"))


def route(nc, c, chosen, gates_dram, layer):
    NCH_ = PH * TOPK
    UNIT = 8
    PER = P // UNIT
    PER_STORE = STORE // UNIT
    with ExitStack() as s:
        sb = lambda n, sh, dt=F32: s.enter_context(nc.sbuf_tensor(f"{n}_ro{layer}", sh, dt))
        sem = stage_semaphores(nc, s, f"_ro{layer}")
        ps = lambda n, sh: s.enter_context(nc.psum_tensor(f"{n}_ro{layer}", sh, F32))
        ALLC = [P, PH, NT, TOPK]
        e = sb("e", ALLC)
        esum = sb("esum", [P, PH, NT])
        s4 = sb("s4", ALLC, U32)
        s2 = sb("s2", ALLC, U32)
        posf = sb("posf", ALLC)
        m = sb("m", ALLC)
        rank = [sb(f"rank{i}", [P, NT, PH, TOPK]) for i in range(2)]
        gt = sb("gt", [P, NT, PH, TOPK])
        found = [sb(f"found{i}", [P, NT, NCH_]) for i in range(2)]
        iota16 = sb("iota16", [P, TOPK])
        iota128 = sb("iota128", [P, P])
        eq = [sb(f"eq{i}", [P, NCH_, TOPK]) for i in range(2)]
        turned = sb("turned", [P, 3, T])
        first = [sb(f"first{i}", [P, UNIT, P]) for i in range(2)]
        second = [sb(f"second{i}", [P, UNIT, P]) for i in range(2)]
        stage = [sb(f"stage{i}", [P, KEYS, STORE]) for i in range(2)]
        pt = ps("pt", [P, 4, P])
        pg = [ps(f"pg{i}", [P, UNIT, P]) for i in range(2)]
        iot, sub_done, exp_done, compared, eqd, summed, gated, tr, tr_out, first_hot, second_hot, weighed, mm, staged = (sem(n) for n in
            ("iot", "sub_done", "exp_done", "compared", "eqd", "summed", "gated", "tr", "tr_out", "first_hot",
             "second_hot", "weighed", "mm", "staged"))
        stored = [sem(f"stored{i}") for i in range(2)]
        block = s.enter_context(nc.Block())

        @block.gpsimd
        def _(pool):
            pool.iota(iota16[:, :], [[1, TOPK]], base=0, channel_multiplier=0, allow_small_or_imprecise_dtypes=True)
            pool.iota(iota128[:, :], [[1, P]], base=0, channel_multiplier=0, allow_small_or_imprecise_dtypes=True)
            pool.drain().then_inc(iot, 1)

            def weigh(t):
                for b in range(2):
                    pool.wait_ge(compared, 2 * t + b + 1)
                    ev = eq[b][:, :, :].rearrange("p (h k) r -> p h k r", k=TOPK)
                    pool.tensor_tensor(ev, ev, chosen[:, 2 + b, :, t, :].unsqueeze(2).to_broadcast([P, PH, TOPK, TOPK]),
                                       ALU.mult)
                    pool.drain().then_inc(eqd, 1)

            weigh(0)
            for t in range(NT):
                if t + 1 < NT:
                    weigh(t + 1)
                with pool.Fori(0, PER // 2) as i:
                    for b in range(2):
                        pool.wait_ge(first_hot, i * 2 + (t * PER + b + 1))
                        gate = turned[:, 2, bass.ds(i * (2 * UNIT) + (t * P + b * UNIT), UNIT)]
                        pool.tensor_tensor(first[b][:, :, :], first[b][:, :, :],
                                           gate.unsqueeze(2).to_broadcast([P, UNIT, P]), ALU.mult).then_inc(weighed, 1)

        @block.vector
        def _(dve):
            pos = chosen[:, 1].bitcast(U32)
            nc.vector.tensor_tensor(e[:, :, :, :], chosen[:, 0], chosen[:, 0, :, :, 0:1].to_broadcast(ALLC), ALU.subtract)
            dve.drain().then_inc(sub_done, 1)
            nc.vector.tensor_scalar(s4[:, :, :, :], pos, 4, None, ALU.logical_shift_right)
            nc.vector.tensor_scalar(s2[:, :, :, :], pos, 2, None, ALU.logical_shift_right)
            nc.vector.tensor_copy(posf[:, :, :, :], pos)
            dve.drain()
            f = lambda x: x[:, :, :, :].rearrange("p h t k -> p (h t k)")
            nc.vector.scalar_tensor_tensor(f(m), f(s2), 12.0, f(s4), ALU.subtract, ALU.max)
            dve.drain()
            nc.vector.scalar_tensor_tensor(f(m), f(posf), 72.0, f(m), ALU.subtract, ALU.max)
            dve.drain()
            for t in range(NT):
                nc.vector.tensor_copy(rank[0][:, t], m[:, :, t, :])
            nc.vector.tensor_scalar(e2v(s4), f(m), 4.0, 48.0, ALU.mult, ALU.add)
            dve.drain()
            nc.vector.scalar_tensor_tensor(e2v(s4), f(m), 16.0, e2v(s4), ALU.mult, ALU.min)
            dve.drain()
            nc.vector.scalar_tensor_tensor(e2v(s4), f(m), 72.0, e2v(s4), ALU.add, ALU.min)
            dve.drain()
            nc.vector.tensor_sub(f(posf), f(posf), e2v(s4))
            dve.drain()
            for t in range(NT):
                nc.vector.tensor_copy(rank[1][:, t], posf[:, :, t, :])
            dve.wait_ge(iot, 1)
            dve.drain()
            dve.wait_ge(exp_done, 1)
            nc.vector.tensor_reduce(esum[:, :, :], e[:, :, :, :], AX.X, ALU.add)
            dve.drain()
            nc.vector.reciprocal(esum[:, :, :], esum[:, :, :])
            dve.drain()
            for t in range(NT):
                nc.vector.tensor_mul(gt[:, t], e[:, :, t, :], esum[:, :, t:t + 1].to_broadcast([P, PH, TOPK]))
            dve.drain().then_inc(gated, 1)

            def compare(t):
                for b in range(2):
                    r = rank[b][:, t].rearrange("p h k -> p (h k)").unsqueeze(2).to_broadcast([P, NCH_, TOPK])
                    nc.vector.tensor_tensor(eq[b][:, :, :], r,
                                            iota16[:, :].unsqueeze(1).to_broadcast([P, NCH_, TOPK]), ALU.is_equal) \
                        .then_inc(compared, 1)

            def sums(t):
                for b in range(2):
                    dve.wait_ge(eqd, 2 * t + b + 1)
                    nc.vector.tensor_reduce(found[b][:, t, :], eq[b][:, :, :], AX.X, ALU.add).then_inc(summed, 1)

            compare(0)
            sums(0)
            for t in range(NT):
                if t + 1 < NT:
                    dve.drain()
                    compare(t + 1)
                dve.wait_ge(tr_out, t + 1)
                with dve.Fori(0, PER // 2) as i:
                    for b in range(2):
                        dve.wait_ge(mm, i * 2 + (t * PER + b + 1))
                        for f, dst, done in ((0, first[b], first_hot), (1, second[b], second_hot)):
                            index = turned[:, f, bass.ds(i * (2 * UNIT) + (t * P + b * UNIT), UNIT)]
                            nc.vector.tensor_tensor(dst[:, :, :], iota128[:, :].unsqueeze(1).to_broadcast([P, UNIT, P]),
                                                    index.unsqueeze(2).to_broadcast([P, UNIT, P]), ALU.is_equal) \
                                .then_inc(done, 1)
                if t + 1 < NT:
                    sums(t + 1)

        @block.tensor
        def _(pe):
            pe.sem_inc(mm, 2)

            def turn(t):
                pe.wait_ge(summed, 2 * t + 2)
                pe.wait_ge(gated, 1)
                if t:
                    pe.wait_ge(tr_out, t)
                for n, src in enumerate((found[0][:, t, :], found[1][:, t, :], gt[:, t].rearrange("p h k -> p (h k)"))):
                    last = nc.tensor.transpose(pt[:, n, :], src, c["ident"][:, :])
                last.then_inc(tr, 1)

            for t in range(NT):
                turn(t)
                with pe.Fori(0, PER // 2) as i:
                    for b in range(2):
                        pe.wait_ge(second_hot, i * 2 + (t * PER + b + 1))
                        pe.wait_ge(weighed, i * 2 + (t * PER + b + 1))
                        pe.wait_ge(staged, i * 2 + (t * PER + b + 1))
                        for u in range(UNIT):
                            last = nc.tensor.matmul(pg[b][:, u, :], second[b][:, u, :], first[b][:, u, :],
                                                    start=True, stop=True)
                        last.then_inc(mm, 1)

        @block.scalar
        def _(act):
            act.sem_inc(staged, 2)
            act.wait_ge(sub_done, 1)
            act.activation(e[:, :, :, :], e[:, :, :, :], ACT.Exp).then_inc(exp_done, 1)

            def turn_out(t):
                act.wait_ge(tr, t + 1)
                act.activation(turned[:, :, t * P:(t + 1) * P], pt[:, 0:3, :], ACT.Copy).then_inc(tr_out, 1)

            for t in range(NT):
                turn_out(t)
                for half in range(2):
                    if t:
                        act.wait_ge(stored[half], 16 * t)
                    first_step = t * PER + half * PER_STORE
                    with act.Fori(0, PER_STORE // 2) as i:
                        for b in range(2):
                            act.wait_ge(mm, i * 2 + (2 + first_step + b + 1))
                            act.activation(stage[half][:, :, bass.ds(i * (2 * UNIT) + b * UNIT, UNIT)],
                                           pg[b][:, :, :].rearrange("p t i -> p i t"), ACT.Copy).then_inc(staged, 1)

        @block.sync
        def _(sp):
            for n in range(T // STORE):
                sp.wait_ge(staged, 2 + (n + 1) * PER_STORE)
                sp.dma_start(gates_dram[n], stage[n % 2][:, :, :]).then_inc(stored[n % 2], 16)
            for half in range(2):
                sp.wait_ge(stored[half], 16 * NT)


def e2v(x):
    return x[:, :, :, :].rearrange("p h t k -> p (h t k)").bitcast(F32)


def experts(nc, a, c, h_hi, h_lo, x_sp, gates_dram, layer):
    NE = KEYS
    K = 2
    u_tab = a["peer_u"][layer].rearrange("(n p) d -> n p d", p=P)
    v_tab = a["peer_v"][layer].rearrange("(n p) d -> n p d", p=P)
    with ExitStack() as s:
        sb = lambda n, sh, dt=F32: s.enter_context(nc.sbuf_tensor(f"{n}_ex{layer}", sh, dt))
        sem = stage_semaphores(nc, s, f"_ex{layer}")
        ps = lambda n, sh: s.enter_context(nc.psum_tensor(f"{n}_ex{layer}", sh, F32))
        acc = sb("acc", [P, DC, T])
        u_raw = [sb(f"u_raw{i}", [P, D]) for i in range(2)]
        v_raw = [sb(f"v_raw{i}", [P, D]) for i in range(2)]
        g_raw = [sb(f"g_raw{i}", [P, T]) for i in range(2)]
        uT_hi = [sb(f"uT_hi{i}", [P, DC, P], F32R) for i in range(2)]
        uT_lo = [sb(f"uT_lo{i}", [P, DC, P], F32R) for i in range(2)]
        v_hi = [sb(f"v_hi{i}", [P, D], F32R) for i in range(4)]
        v_lo = [sb(f"v_lo{i}", [P, D], F32R) for i in range(4)]
        c_hi = [sb(f"c_hi{i}", [P, T], F32R) for i in range(4)]
        c_lo = [sb(f"c_lo{i}", [P, T], F32R) for i in range(4)]
        coef = [sb(f"coef{i}", [P, T]) for i in range(2)]
        pT = [ps(f"pT{i}", [P, 4, P]) for i in range(2)]
        pu = [ps(f"pu{i}", [P, 512]) for i in range(2)]
        pv = [ps(f"pv{i}", [P, 512]) for i in range(4)]
        (turned, u_hi_done, u_lo_done, dotted, gelu_done, coef_done, c_hi_done, c_lo_done, v_hi_done, v_lo_done,
         v_mm, added, x_in, x_out, x_added) = (sem(n) for n in (
            "turned", "u_hi_done", "u_lo_done", "dotted", "gelu_done", "coef_done", "c_hi_done", "c_lo_done",
            "v_hi_done", "v_lo_done", "v_mm", "added", "x_in", "x_out", "x_added"))
        u_in, v_in, g_in = ([sem(f"{n}{i}") for i in range(2)] for n in ("u_in", "v_in", "g_in"))
        block = s.enter_context(nc.Block())
        xT = [buf[:, 0:T] for buf in (*u_raw, *v_raw, *g_raw, *coef)]
        REG = 2 * DC
        BANKS = 4

        def half16(n, r):
            if isinstance(n, int):
                return 16 * (n // 2 + 1)
            return n * 8 + (16 - 8 * (r % 2))

        def chunk_of(n, r, scale):
            if isinstance(n, int):
                return scale * (n // 2)
            return n * (scale // 2) - (scale // 2) * (r % 2)

        def schedule(eng, first, step, last):
            first(0)
            step(0, 0, None)
            step(1, 1, None)
            with eng.Fori(0, (NE - 4) // 4) as i:
                for r in range(4):
                    n = i * 4 + (2 + r)
                    step(n, 2 + r, i * 2 + (r // 2) if r % 2 else None)
            step(NE - 2, 2, None)
            step(NE - 1, 3, NE // 2 - 2)
            last(NE // 2 - 1)

        @block.sync
        def _(sp):
            with sp.Fori(0, NE // 2) as i:
                for b in range(2):
                    n = i * 2 + b
                    sp.wait_ge(turned, n + 1)
                    sp.dma_start(u_raw[b][:, :], u_tab[bass.ds(n, 1)].rearrange("o p d -> (o p) d")).then_inc(u_in[b], 16)
                    sp.wait_ge(v_lo_done, n + 1)
                    sp.dma_start(v_raw[b][:, :], v_tab[bass.ds(n, 1)].rearrange("o p d -> (o p) d")).then_inc(v_in[b], 16)
                    sp.wait_ge(coef_done, n + 1)
                    sp.dma_start(g_raw[b][:, :].rearrange("p (s t) -> p s t", t=STORE),
                                 gates_dram[:, :, bass.ds(n, 1), :].rearrange("s p o t -> p s (o t)")) \
                        .then_inc(g_in[b], 16)
            sp.wait_ge(added, BANKS + REG * NE // K)
            for k in range(DC):
                sp.dma_start(xT[k], x_sp[:, k, :]).then_inc(x_in, 16)
            sp.wait_ge(x_added, 1)
            for k in range(DC):
                sp.dma_start(x_sp[:, k, :], xT[k]).then_inc(x_out, 16)
            sp.wait_ge(x_out, 16 * DC)

        @block.gpsimd
        def _(pool):
            pool.sem_inc(v_lo_done, 2)
            with pool.Fori(0, NE // 4) as i:
                for r in range(4):
                    n = i * 4 + r
                    pool.wait_ge(v_hi_done, n + 1)
                    pool.tensor_tensor(v_lo[r][:, :], v_raw[r % 2][:, :], v_hi[r][:, :].bitcast(F32), ALU.subtract) \
                        .then_inc(v_lo_done, 1)

        @block.scalar
        def _(act):
            def turn_hi(n, r):
                act.wait_ge(turned, n + 3)
                act.wait_ge(dotted, n * 2 + 2)
                for i in range(2):
                    last_ = act.activation(uT_hi[r % 2][:, 4 * i:4 * i + 4, :], pT[i][:, :, :], ACT.Copy)
                last_.then_inc(u_hi_done, 1)

            def step(n, r, chunk):
                b = r % 2
                if not (isinstance(n, int) and n == NE - 1):
                    turn_hi(n + 1, r + 1)
                act.wait_ge(v_in[b], half16(n, r))
                act.wait_ge(v_mm, chunk_of(n, r, REG) + REG)
                act.activation(v_hi[r % 4][:, :], v_raw[b][:, :], ACT.Copy).then_inc(v_hi_done, 1)
                for i, cols in halves():
                    act.wait_ge(dotted, n * 2 + (4 + i + 1))
                    if i == 0:
                        act.wait_ge(c_lo_done, n + 1)
                    act.activation(coef[b][:, cols], pu[i][:, 0:HALF], ACT.Gelu).then_inc(gelu_done, 1)
                act.wait_ge(coef_done, n + 3)
                act.activation(c_hi[r % 4][:, :], coef[b][:, :], ACT.Copy).then_inc(c_hi_done, 1)

            schedule(act, lambda n: turn_hi(0, 0), step, lambda ch: None)

        @block.vector
        def _(dve):
            dve.sem_inc(coef_done, 2)
            dve.sem_inc(c_lo_done, 2)
            dve.sem_inc(added, BANKS)
            nc.vector.memset(acc[:, :, :], 0.0)
            dve.drain()

            def turn_lo(n, r):
                dve.wait_ge(u_hi_done, n + 1)
                for i in range(2):
                    last_ = nc.vector.tensor_sub(uT_lo[r % 2][:, 4 * i:4 * i + 4, :], pT[i][:, :, :],
                                                 uT_hi[r % 2][:, 4 * i:4 * i + 4, :].bitcast(F32))
                last_.then_inc(u_lo_done, 1)

            def accumulate(chunk):
                for g in range(REG):
                    k, i = g // 2, g % 2
                    dve.wait_ge(v_mm, chunk * REG + (2 * REG + g + 1))
                    dst = acc[:, k, i * HALF:(i + 1) * HALF]
                    nc.vector.tensor_add(dst, dst, pv[g % BANKS][:, 0:HALF]).then_inc(added, 1)

            def step(n, r, chunk):
                b = r % 2
                if not (isinstance(n, int) and n == NE - 1):
                    turn_lo(n + 1, r + 1)
                dve.wait_ge(g_in[b], half16(n, r))
                dve.wait_ge(gelu_done, n * 2 + 2)
                nc.vector.tensor_mul(coef[b][:, :], coef[b][:, :], g_raw[b][:, :]).then_inc(coef_done, 1)
                dve.wait_ge(c_hi_done, n + 1)
                nc.vector.tensor_sub(c_lo[r % 4][:, :], coef[b][:, :], c_hi[r % 4][:, :].bitcast(F32)) \
                    .then_inc(c_lo_done, 1)
                if chunk is not None:
                    accumulate(chunk)

            schedule(dve, lambda n: turn_lo(0, 0), step, accumulate)
            dve.drain()
            dve.wait_ge(x_in, 16 * DC)
            for k in range(DC):
                for v, cols in parts():
                    nc.vector.scalar_tensor_tensor(xT[k][:, cols], acc[:, k, cols],
                                                   c["mod"][:, layer, 40 + k, v:v + 1], xT[k][:, cols],
                                                   ALU.mult, ALU.add)
            dve.drain().then_inc(x_added, 1)

        @block.tensor
        def _(pe):
            pe.sem_inc(turned, 2)
            pe.sem_inc(dotted, 4)
            pe.sem_inc(v_mm, 2 * REG)

            def turn(n, r):
                pe.wait_ge(u_in[r % 2], half16(n, r))
                if not (isinstance(n, int) and n == 0):
                    pe.wait_ge(u_lo_done, n)
                for k in range(DC):
                    last_ = nc.tensor.transpose(pT[k // 4][:, k % 4, :], u_raw[r % 2][:, k * P:(k + 1) * P],
                                                c["ident"][:, :])
                last_.then_inc(turned, 1)

            def products(chunk, odd):
                for g in range(REG):
                    k, i = g // 2, g % 2
                    pe.wait_ge(added, chunk * REG + (g + 1))
                    terms = []
                    for t in range(K):
                        slot = 2 * odd + t
                        for w, x in ((v_hi, c_hi), (v_hi, c_lo), (v_lo, c_hi)):
                            terms.append((w[slot][:, k * P:(k + 1) * P], x[slot][:, i * HALF:(i + 1) * HALF]))
                    for m, (w, x) in enumerate(terms):
                        last_ = nc.tensor.matmul(pv[g % BANKS][:, 0:HALF], w, x, start=(m == 0),
                                                 stop=(m == len(terms) - 1))
                    last_.then_inc(v_mm, 1)

            def step(n, r, chunk):
                b = r % 2
                if not (isinstance(n, int) and n == NE - 1):
                    turn(n + 1, r + 1)
                pe.wait_ge(u_lo_done, n + 1)
                pe.wait_ge(gelu_done, n * 2)
                for i, cols in halves():
                    split_product(nc, pu[i][:, 0:HALF], uT_hi[b], uT_lo[b], h_hi, h_lo, cols).then_inc(dotted, 1)
                if chunk is not None:
                    pe.wait_ge(v_lo_done, chunk * 2 + 4)
                    pe.wait_ge(c_lo_done, chunk * 2 + 4)
                    products(chunk, slot_pair(r))

            def slot_pair(r):
                return 0 if r % 4 == 3 else 1

            def last(chunk):
                pe.wait_ge(v_lo_done, chunk * 2 + 4)
                pe.wait_ge(c_lo_done, chunk * 2 + 4)
                products(chunk, 1)

            schedule(pe, lambda n: turn(0, 0), step, last)


def finish(nc, c, x_sp, out):
    with ExitStack() as s:
        sb = lambda n, sh, dt=F32: s.enter_context(nc.sbuf_tensor(f"{n}_fi", sh, dt))
        sem = stage_semaphores(nc, s, f"_fi")
        ps = lambda n, sh: s.enter_context(nc.psum_tensor(f"{n}_fi", sh, F32))
        xT = sb("x", [P, DC, T])
        sq = [sb(f"sq{i}", [P, T]) for i in range(2)]
        rs = sb("rs", [P, T])
        y = sb("y", [P, NT, D])
        ms = [ps(f"ms{i}", [P, 512]) for i in range(2)]
        pt = [ps(f"pt{i}", [P, 4, P]) for i in range(2)]
        x_in, sq_done, summed, inv, rooted, scaled, tr, tr_out, stored = (sem(n) for n in
            ("x_in", "sq_done", "summed", "inv", "rooted", "scaled", "tr", "tr_out", "stored"))
        block = s.enter_context(nc.Block())

        @block.sync
        def _(sp):
            sp.dma_start(xT[:, :, :], x_sp).then_inc(x_in, 16)
            sp.wait_ge(tr_out, 2 * (NT - 1))
            sp.dma_start(out[1].rearrange("o (n p) d -> p (o n) d", p=P), y[:, 0:NT - 1, :]).then_inc(stored, 16)
            sp.wait_ge(tr_out, 2 * NT)
            sp.dma_start(out[0].rearrange("o p d -> (o p) d"), y[:, NT - 1, :]).then_inc(stored, 16)
            sp.wait_ge(stored, 32)

        @block.scalar
        def _(act):
            act.wait_ge(x_in, 16)
            for k in range(DC):
                if k >= 2:
                    act.wait_ge(summed, k - 1)
                act.activation(sq[k % 2][:, :], xT[:, k, :], ACT.Square).then_inc(sq_done, 1)
            act.wait_ge(inv, 1)
            act.activation(rs[:, :], rs[:, :], ACT.Sqrt).then_inc(rooted, 1)
            for n in range(2 * NT):
                act.wait_ge(tr, n + 1)
                act.activation(y[:, n // 2, (n % 2) * 512:(n % 2 + 1) * 512],
                               pt[n % 2][:, :, :].rearrange("p a b -> p (a b)"), ACT.Copy).then_inc(tr_out, 1)

        @block.tensor
        def _(pe):
            for k in range(DC):
                pe.wait_ge(sq_done, k + 1)
                for i, cols in halves():
                    last = nc.tensor.matmul(ms[i][:, 0:HALF], c["ones_d"][:, :], sq[k % 2][:, cols],
                                            start=(k == 0), stop=(k == DC - 1))
                last.then_inc(summed, 1)
            pe.wait_ge(scaled, 1)
            for n in range(2 * NT):
                if n >= 2:
                    pe.wait_ge(tr_out, n - 1)
                for k in range(4):
                    last = nc.tensor.transpose(pt[n % 2][:, k, :],
                                               xT[:, 4 * (n % 2) + k, (n // 2) * P:(n // 2 + 1) * P], c["ident"][:, :])
                last.then_inc(tr, 1)

        @block.vector
        def _(dve):
            dve.wait_ge(summed, DC)
            for i, cols in halves():
                nc.vector.tensor_scalar(rs[:, cols], ms[i][:, 0:HALF], EPS, None, ALU.add)
            dve.drain()
            nc.vector.reciprocal(rs[:, :], rs[:, :])
            dve.drain().then_inc(inv, 1)
            dve.wait_ge(rooted, 1)
            for k in range(DC):
                w = VEC["final"] + k
                nc.vector.scalar_tensor_tensor(xT[:, k, :], xT[:, k, :], c["vec"][:, w:w + 1], rs[:, :],
                                               ALU.mult, ALU.mult)
            dve.drain().then_inc(scaled, 1)


_INS = ["x_prompt", "x_sample", "state_hgrn", "state_gla", "c", "c_ctx", "ada_w", "ada_b", "norm1_w", "norm2_w",
        "final_norm_w", "hgrn_w_in", "hgrn_lb", "hgrn_gnorm_w", "hgrn_w_out", "gla_w_in", "gla_conv_w",
        "gla_w_gate", "gla_b_gate", "gla_gnorm_w", "gla_w_out", "peer_w_q", "peer_keys", "peer_u", "peer_v"]
_OUTS = [(1, TC, D), (1, TS, D), (1, 1, 2, 8, P, P), (1, 1, 2, 4, P, 2 * P)]


def kernel(**inputs):
    import concourse.bacc as bacc
    from concourse.bass_utils import run_bass_kernel_spmd

    nc = bacc.Bacc("TRN2", target_bir_lowering=False, num_devices=1)
    arrays, args = {}, {}
    for name in _INS:
        x = np.ascontiguousarray(inputs[name])
        arrays[f"in_{name}"] = x
        args[name] = nc.dram_tensor(f"in_{name}", x.shape, mybir.dt.from_np(x.dtype), kind="ExternalInput").ap()
    outs = [nc.dram_tensor(f"out_{i}", shape, F32, kind="ExternalOutput").ap() for i, shape in enumerate(_OUTS)]
    build_program(nc, args, outs)
    r = run_bass_kernel_spmd(nc, [arrays], core_ids=[0])
    return tuple(r.results[0][f"out_{i}"] for i in range(len(_OUTS)))
```

```python
import numpy as np
from contextlib import ExitStack

import concourse.bass as bass
from concourse import mybir

F32 = mybir.dt.float32
F32R = mybir.dt.float32r
BF16 = mybir.dt.bfloat16
U32 = mybir.dt.uint32
I32 = mybir.dt.int32
ALU = mybir.AluOpType
ACT = mybir.ActivationFunctionType
AX = mybir.AxisListType

P = 128
D = 1024
DC = D // P
TS, TC = 512, 128
T = TS + TC
NT = T // P
HALF = T // 2
GRID_W = 64
ROWS = TS // GRID_W
EPS = 1e-6
F_MIN = 1e-20
LEVELS = [64, 32, 16, 8, 4, 2, 1]
NL = len(LEVELS)
DEPTH = 2
KEYS = 128
TOPK = 16
PH = 8
STORE = 64
GATHERS = 4
LN2 = float(np.log(2.0))
LN_LOW = 2.0 ** -40
LN_UP = 2.0 ** 40 - 1.0
LN_FIX = -40.0 * LN2 / LN_UP

VEC = {}


def stage_semaphores(nc, stack, suffix):
    made = []

    def sem(name):
        made.append(nc.alloc_semaphore(f"{name}{suffix}"))
        return made[-1]

    def leave():
        nc.clear_and_free_semaphores(made)
        nc.all_engine_barrier()

    stack.callback(leave)
    return sem


def alone(eng, passed):
    eng.sem_inc(passed, 1)


def halves():
    return [(0, slice(0, HALF)), (1, slice(HALF, T))]


def parts():
    return [(0, slice(0, TS)), (1, slice(TS, T))]


class Mixer:

    def __init__(self, kind):
        self.gla = kind == "gla"
        self.heads = 4 if self.gla else 8
        self.dv = D // self.heads
        self.nv = self.dv // P
        if self.gla:
            self.late = [("v0", 1024, 2 * P), ("v1", 1024 + P, 2 * P), ("og0", 2048, 2 * P), ("og1", 2048 + P, 2 * P)]
            self.early = [("k", 512, P), ("q", 0, P)]
            self.extra = 2
        else:
            self.late = [("v0", 1024, P), ("og0", 4096, P)]
            self.early = [("ff", 2048, P), ("fb", 3072, P), ("q", 0, P)]
            self.extra = 0
        self.chunks = self.late + self.early
        self.nch = len(self.chunks)
        self.turns = self.nch + self.extra


def build_program(nc, a, out, upto=99):
    x_sp = nc.dram_tensor("xT_spill", [P, DC, T], F32, kind="Internal").ap()
    og_sp = nc.dram_tensor("og_spill", [DC, P, T], F32, kind="Internal").ap()
    gates_dram = nc.dram_tensor("gates", [TS // STORE, KEYS, KEYS, STORE], F32, kind="Internal").ap()

    ctx = ExitStack()
    with ctx:
        c = {}
        for name, shape, dt in [
            ("ident", [P, P], F32), ("ones_d", [P, P], F32), ("ones_h", [P, P], F32),
            ("level_mask", [P, (NL + 1), P], BF16), ("scan_f", [P, T], BF16), ("scan_b", [P, T], BF16),
            ("vec", [P, 3 * P], F32), ("mod", [P, DEPTH, 48, 2], F32), ("one", [P, 1], F32),
            ("scale_w", [P, DC, 2], F32), ("lb", [P, 16], F32), ("oml", [P, 16], F32),
        ]:
            c[name] = ctx.enter_context(nc.sbuf_tensor(name, shape, dt))
        with nc.sbuf_tensor("xT", [P, DC, T], F32) as xT:
            setup(nc, a, c, xT, x_sp)
        if upto < 1:
            return
        for layer in range(DEPTH):
            mx = Mixer("gla" if layer % 2 else "hgrn")
            with nc.sbuf_tensor(f"h_hi{layer}", [P, DC, T], F32R) as h_hi, \
                    nc.sbuf_tensor(f"h_lo{layer}", [P, DC, T], F32R) as h_lo:
                norm(nc, c, h_hi, h_lo, x_sp, layer, 0)
                with nc.sbuf_tensor(f"oT{layer}", [P, DC, T], F32) as oT:
                    mixer(nc, a, c, mx, h_hi, h_lo, oT, og_sp, out, layer)
                    mix_out(nc, a, c, mx, h_hi, h_lo, oT, og_sp, x_sp, layer)
                if upto < 2 + 2 * layer:
                    return
                norm(nc, c, h_hi, h_lo, x_sp, layer, 1)
                with nc.sbuf_tensor(f"ctx_index{layer}", [P, 2 * PH * TOPK + GATHERS], I32) as ctx_index, \
                        nc.sbuf_tensor(f"ctx_gate{layer}", [P, PH * TOPK], F32) as ctx_gate:
                    with nc.sbuf_tensor(f"chosen{layer}", [P, 4, PH, NT, TOPK], F32) as chosen:
                        retrieve(nc, a, c, h_hi, h_lo, chosen, layer)
                        route(nc, c, chosen, gates_dram, ctx_index, ctx_gate, layer)
                    experts(nc, a, c, h_hi, h_lo, x_sp, gates_dram, ctx_index, ctx_gate, layer)
                if upto < 3 + 2 * layer:
                    return
        finish(nc, c, x_sp, out)



def vec_rows(a):
    r = lambda ap: ap.rearrange("(n p) -> n p", p=P)
    return [
        ("norm1", a["norm1_w"].rearrange("l (n p) -> (l n) p", p=P), 16),
        ("norm2", a["norm2_w"].rearrange("l (n p) -> (l n) p", p=P), 16),
        ("final", r(a["final_norm_w"]), 8),
        ("lb", a["hgrn_lb"].rearrange("o d (n p) -> (o d n) p", p=P), 16),
        ("hgrn_g", a["hgrn_gnorm_w"].rearrange("o (n p) -> (o n) p", p=P), 1),
        ("gla_g", a["gla_gnorm_w"].rearrange("o (n p) -> (o n) p", p=P), 2),
        ("b_gate", a["gla_b_gate"].rearrange("o d (n p) -> (o d n) p", p=P), 8),
        ("c", a["c"].rearrange("o (n p) -> (o n) p", p=P), 8),
        ("c_ctx", r(a["c_ctx"]), 8),
        ("pad", None, P - 83),
        ("ada_b", a["ada_b"].rearrange("l (n p) -> (l n) p", p=P), 96),
        ("conv8", a["gla_conv_w"].rearrange("o y x (n p) -> (o y x n) p", p=P)[P:P + 16, :], 16),
        ("pad2", None, 16),
        ("conv", a["gla_conv_w"].rearrange("o y x (n p) -> (o y x n) p", p=P)[0:P, :], P),
    ]


def setup(nc, a, c, xT, x_sp):
    NB = 512
    NBL = 6 * D // NB
    with ExitStack() as s:
        sb = lambda n, sh, dt=F32: s.enter_context(nc.sbuf_tensor(n, sh, dt))
        sem = stage_semaphores(nc, s, "")
        rows = sb("param_rows", [P, 3, P])
        xin = sb("xin", [P, NT, D])
        ada = [sb(f"ada{i}", [P, DC, NB]) for i in range(2)]
        cs = sb("cs", [P, 2, DC])
        sg = sb("sg", [P, 2, DC])
        it_p = sb("it_p", [P, P], I32)
        it_f = sb("it_f", [P, P], I32)
        xorf = sb("xorf", [P, P])
        low = sb("low", [P, P])
        l0 = sb("l0", [P, 16])
        l1 = sb("l1", [P, 16])
        pt = [s.enter_context(nc.psum_tensor(f"pt{i}", [P, 4, P], F32)) for i in range(2)]
        mod_row = [sb(f"mod_row{i}", [P, NB]) for i in range(2)]
        pc = [s.enter_context(nc.psum_tensor(f"pc{i}", [P, NB // P, 2], F32)) for i in range(2)]
        pa = [s.enter_context(nc.psum_tensor(f"pa{i}", [P, 512], F32)) for i in range(2)]
        rows_in, x_in, tr, ev, vecs, cready = (sem(n) for n in
            ("rows_in", "x_in", "tr", "ev", "vecs", "cready"))
        ada_in = [sem(f"ada_in{i}") for i in range(2)]
        pe_passed = sem("pe_passed")
        ada_mm, row_out, row_turned, mod_done, x_out, iot, sig, rows_z = (sem(n) for n in
            ("ada_mm", "row_out", "row_turned", "mod_done", "x_out", "iot", "sig", "rows_z"))
        col = 0
        loads = []
        for name, view, n in vec_rows(a):
            VEC[name] = col
            if view is not None:
                loads.append((view, col, n))
            col += n
        block = s.enter_context(nc.Block())
        nload = len(loads)

        @block.sync
        def _(sp):
            sp.wait_ge(rows_z, 1)
            for view, col0, n in loads:
                sp.dma_start(rows[col0 % P:col0 % P + n, col0 // P, :], view).then_inc(rows_in, 16)
            for l in range(DEPTH):
                w = a["ada_w"][l].rearrange("(k p) n -> p k n", p=P)
                with sp.Fori(0, NBL // 2) as i:
                    for b in range(2):
                        sp.wait_ge(ada_mm, i * 2 + (l * NBL + b + 1))
                        sp.dma_start(ada[b][:, :, :], w[:, :, bass.ds(i * (2 * NB) + b * NB, NB)]) \
                            .then_inc(ada_in[b], 16)
            sp.wait_ge(ev, 3 + 40 // 4)
            sp.dma_start(x_sp, xT[:, :, :]).then_inc(x_out, 16)
            sp.wait_ge(x_out, 16)

        @block.gpsimd
        def _(pool):
            pool.memset(rows[:, :, :], 0.0)
            pool.drain().then_inc(rows_z, 1)
            pool.iota(it_p[:, :], [[0, P]], base=0, channel_multiplier=1)
            pool.iota(it_f[:, :], [[1, P]], base=0, channel_multiplier=0)
            pool.memset(c["ident"][:, :], 0.0)
            pool.memset(c["ones_d"][:, :], 1.0 / D)
            pool.memset(c["one"][:, :], 1.0)
            pool.memset(c["scan_f"][:, :], 1.0)
            pool.memset(c["scan_b"][:, :], 1.0)
            pool.drain()
            pool.affine_select(out=c["ident"][:, :], in_=c["ident"][:, :], compare_op=ALU.not_equal,
                               fill=1.0, base=0, pattern=[[-1, P]], channel_multiplier=1)
            pool.memset(c["scan_f"][:, :].rearrange("p (n t) -> p n t", t=P)[:, :, 0:1], 0.0)
            pool.memset(c["scan_b"][:, :].rearrange("p (n t) -> p n t", t=P)[:, :, P - 1:P], 0.0)
            pool.drain().then_inc(iot, 1)

        @block.scalar
        def _(act):
            act.dma_start(xin[:, 0:NT - 1, :], a["x_sample"].rearrange("o (n p) d -> p (o n) d", p=P)) \
                .then_inc(x_in, 16)
            act.dma_start(xin[:, NT - 1, :], a["x_prompt"].rearrange("o p d -> (o p) d")).then_inc(x_in, 16)
            for g in range(3 + 10):
                act.wait_ge(tr, g + 1)
                if g < 3:
                    act.activation(c["vec"][:, g * P:(g + 1) * P], pt[g % 2][:, 0, :], ACT.Copy).then_inc(ev, 1)
                else:
                    q = g - 3
                    t, k = q // 2, 4 * (q % 2)
                    act.activation(xT[:, k:k + 4, t * P:(t + 1) * P], pt[g % 2][:, :, :], ACT.Copy).then_inc(ev, 1)
        @block.vector
        def _(dve):
            dve.wait_ge(iot, 1)
            nc.vector.tensor_tensor(it_p[:, :], it_p[:, :], it_f[:, :], ALU.bitwise_xor)
            dve.drain()
            nc.vector.tensor_copy(xorf[:, :], it_p[:, :])
            dve.drain()
            for l, m in enumerate(LEVELS):
                nc.vector.tensor_scalar(low[:, :], xorf[:, :], float(m), None, ALU.is_ge)
                dve.drain()
                nc.vector.scalar_tensor_tensor(c["level_mask"][:, l, :], xorf[:, :], float(2 * m), low[:, :],
                                               ALU.is_lt, ALU.mult)
                dve.drain()
            nc.vector.tensor_scalar(c["level_mask"][:, NL, :], xorf[:, :], 0.0, None, ALU.is_equal)
            dve.wait_ge(ev, 3)
            lbr = c["vec"][:, VEC["lb"]:VEC["lb"] + 16]
            nc.vector.tensor_sub(l0[:, :], lbr, lbr)
            dve.drain().then_inc(vecs, 1)
            dve.wait_ge(vecs, 2)
            nc.vector.reciprocal(l1[:, :], l0[:, :])
            dve.drain()
            nc.vector.tensor_mul(l1[:, :], l0[:, :], l1[:, :])
            dve.drain()
            nc.vector.tensor_sub(c["lb"][:, :], l1[:, :], l1[:, :])
            dve.drain()
            nc.vector.tensor_scalar(c["oml"][:, :], c["lb"][:, :], -1.0, 1.0, ALU.mult, ALU.add)
            dve.wait_ge(sig, 1)
            for v, name in ((0, "c"), (1, "c_ctx")):
                nc.vector.tensor_mul(cs[:, v, :], sg[:, v, :], c["vec"][:, VEC[name]:VEC[name] + DC])
            dve.drain().then_inc(cready, 1)
            dve.sem_inc(mod_done, 2)
            NCB = NB // P
            for l in range(DEPTH):
                with dve.Fori(0, NBL // 2) as i:
                    for b in range(2):
                        dve.wait_ge(row_turned, i * 2 + (2 + l * NBL + b + 1))
                        bias = c["vec"][:, bass.ds(i * (2 * NCB) + (VEC["ada_b"] + 48 * l + b * NCB), NCB)]
                        nc.vector.tensor_tensor(c["mod"][:, l, bass.ds(i * (2 * NCB) + b * NCB, NCB), :], pc[b][:, :, :],
                                                bias.unsqueeze(2).to_broadcast([P, NCB, 2]), ALU.add) \
                            .then_inc(mod_done, 1)
            dve.drain()

        @block.scalar
        def _(act):
            act.wait_ge(vecs, 1)
            act.activation(l0[:, :], l0[:, :], ACT.Exp)
            act.drain().then_inc(vecs, 1)
            act.wait_ge(ev, 3)
            for v, name in ((0, "c"), (1, "c_ctx")):
                act.activation(sg[:, v, :], c["vec"][:, VEC[name]:VEC[name] + DC], ACT.Sigmoid)
            act.drain().then_inc(sig, 1)
            act.sem_inc(row_out, 2)
            with act.Fori(0, DEPTH * NBL // 2) as i:
                for b in range(2):
                    act.wait_ge(ada_mm, i * 2 + (2 + b + 1))
                    act.wait_ge(row_turned, i * 2 + (b + 1))
                    act.activation(mod_row[b][0:2, :], pa[b][0:2, :], ACT.Copy).then_inc(row_out, 1)


        @block.tensor
        def _(pe):
            pe.sem_inc(ada_mm, 2)
            pe.wait_ge(iot, 1)
            pe.wait_ge(rows_in, 16 * nload)
            for g in range(3 + 10):
                if g >= 2:
                    pe.wait_ge(ev, g - 1)
                if g < 3:
                    last = nc.tensor.transpose(pt[g % 2][:, 0, :], rows[:, g, :], c["ident"][:, :])
                else:
                    if g == 3:
                        pe.wait_ge(x_in, 32)
                    q = g - 3
                    for k in range(4):
                        kk = 4 * (q % 2) + k
                        last = nc.tensor.transpose(pt[g % 2][:, k, :], xin[:, q // 2, kk * P:(kk + 1) * P],
                                                   c["ident"][:, :])
                last.then_inc(tr, 1)
            pe.wait_ge(cready, 1)
            pe.sem_inc(row_turned, 2)
            with pe.Fori(0, DEPTH * NBL // 2) as i:
                for b in range(2):
                    pe.wait_ge(ada_in[b], i * 16 + 16)
                    pe.wait_ge(row_out, i * 2 + (b + 1))
                    for k in range(DC):
                        last = nc.tensor.matmul(pa[b][0:2, :], cs[:, :, k], ada[b][:, k, :],
                                                start=(k == 0), stop=(k == DC - 1))
                    last.then_inc(ada_mm, 1)
                for b in range(2):
                    pe.wait_ge(row_out, i * 2 + (2 + b + 1))
                    pe.wait_ge(mod_done, i * 2 + (b + 1))
                    alone(pe, pe_passed)
                    for n in range(NB // P):
                        last = nc.tensor.transpose(pc[b][:, n, :], mod_row[b][0:2, n * P:(n + 1) * P],
                                                   c["ident"][0:2, 0:2])
                    last.then_inc(row_turned, 1)


def norm(nc, c, h_hi, h_lo, x_sp, layer, which):
    with ExitStack() as s:
        sb = lambda n, sh, dt=F32: s.enter_context(nc.sbuf_tensor(f"{n}_n{layer}{which}", sh, dt))
        sem = stage_semaphores(nc, s, f"_n{layer}{which}")
        xT = sb("x", [P, DC, T])
        sq = [sb(f"sq{i}", [P, T]) for i in range(2)]
        rs = sb("rs", [P, T])
        y = [sb(f"y{i}", [P, T]) for i in range(2)]
        z = [sb(f"z{i}", [P, T]) for i in range(2)]
        ms = [s.enter_context(nc.psum_tensor(f"ms{i}_n{layer}{which}", [P, 512], F32)) for i in range(2)]
        sq_done, summed, inv, rooted, scaled, hi_done, y_done, lo_done = (sem(n) for n in
            ("sq_done", "summed", "inv", "rooted", "scaled", "hi_done", "y_done", "lo_done"))
        x_in = [sem(f"x_in{i}") for i in range(4)]
        block = s.enter_context(nc.Block())
        w0 = VEC["norm2" if which else "norm1"] + 8 * layer
        sh, sc = 24 * which, 24 * which + 8

        @block.sync
        def _(sp):
            for i in range(4):
                sp.dma_start(xT[:, 2 * i:2 * i + 2, :], x_sp[:, 2 * i:2 * i + 2, :]).then_inc(x_in[i], 16)

        @block.scalar
        def _(act):
            for k in range(DC):
                if k % 2 == 0:
                    act.wait_ge(x_in[k // 2], 16)
                if k >= 2:
                    act.wait_ge(summed, k - 1)
                act.activation(sq[k % 2][:, :], xT[:, k, :], ACT.Square).then_inc(sq_done, 1)
            act.wait_ge(inv, 1)
            act.activation(rs[:, :], rs[:, :], ACT.Sqrt).then_inc(rooted, 1)
            act.wait_ge(scaled, 1)
            for k in range(DC):
                act.wait_ge(y_done, k + 1)
                if k >= 2:
                    act.wait_ge(lo_done, k - 1)
                for v, cols in parts():
                    act.activation(z[k % 2][:, cols], y[k % 2][:, cols], ACT.Identity,
                                   bias=c["mod"][:, layer, sh + k, v:v + 1], scale=c["scale_w"][:, k, v:v + 1])
                act.drain()
                act.activation(h_hi[:, k, :], z[k % 2][:, :], ACT.Copy).then_inc(hi_done, 1)

        @block.tensor
        def _(pe):
            for k in range(DC):
                pe.wait_ge(sq_done, k + 1)
                for i, cols in halves():
                    last = nc.tensor.matmul(ms[i][:, 0:HALF], c["ones_d"][:, :], sq[k % 2][:, cols],
                                            start=(k == 0), stop=(k == DC - 1))
                last.then_inc(summed, 1)

        @block.vector
        def _(dve):
            for v in range(2):
                nc.vector.scalar_tensor_tensor(c["scale_w"][:, :, v], c["mod"][:, layer, sc:sc + DC, v], 1.0,
                                               c["vec"][:, w0:w0 + DC], ALU.add, ALU.mult)
            dve.drain().then_inc(scaled, 1)
            dve.wait_ge(summed, DC)
            for i, cols in halves():
                nc.vector.tensor_scalar(rs[:, cols], ms[i][:, 0:HALF], EPS, None, ALU.add)
            dve.drain()
            nc.vector.reciprocal(rs[:, :], rs[:, :])
            dve.drain().then_inc(inv, 1)
            dve.wait_ge(rooted, 1)

            for i in range(4):
                dve.wait_ge(x_in[i], 16)

            def normalise(k):
                if k >= 2:
                    dve.wait_ge(hi_done, k - 1)
                nc.vector.tensor_mul(y[k % 2][:, :], xT[:, k, :], rs[:, :]).then_inc(y_done, 1)

            normalise(0)
            for k in range(DC):
                if k + 1 < DC:
                    normalise(k + 1)
                dve.wait_ge(hi_done, k + 1)
                nc.vector.tensor_sub(h_lo[:, k, :], z[k % 2][:, :], h_hi[:, k, :].bitcast(F32)).then_inc(lo_done, 1)
            dve.drain()


def split_product(nc, psum, w_hi, w_lo, x_hi, x_lo, cols):
    for k in range(DC):
        for w, x in ((w_hi, x_hi), (w_hi, x_lo), (w_lo, x_hi)):
            last = nc.tensor.matmul(psum, w[:, k, :], x[:, k, cols], start=(k == 0 and w is w_hi and x is x_hi),
                                    stop=(k == DC - 1 and w is w_lo))
    return last


def mixer(nc, a, c, mx, h_hi, h_lo, oT, og_sp, out, layer):
    NV, DV, NCH, TURNS, H = mx.nv, mx.dv, mx.nch, mx.turns, mx.heads
    w_in = a["gla_w_in" if mx.gla else "hgrn_w_in"][0].rearrange("(k p) n -> p k n", p=P)
    s0 = a["state_gla" if mx.gla else "state_hgrn"][0, 0]
    s_new = out[3 if mx.gla else 2][0, 0]
    L, E = len(mx.late), len(mx.early)
    POOL_LEVELS = 3
    DVE_LEVELS = NL - POOL_LEVELS
    NTR = 10 + NT * NV
    NG = (NTR + 7) // 8
    KVR = 4 // NV
    WITH_STATE = [(0, 0), (0, 1), (0, 2), (0, 4), (1, 3), (1, 2), (1, 1), (1, 4)]
    tag = "gla" if mx.gla else "hgrn"
    with ExitStack() as s:
        sb = lambda n, sh, dt=F32: s.enter_context(nc.sbuf_tensor(f"{n}_{tag}", sh, dt))
        sem = stage_semaphores(nc, s, f"_{tag}")
        ps = lambda n, sh: s.enter_context(nc.psum_tensor(f"{n}_{tag}", sh, F32))
        w_raw = [sb(f"w_raw{i}", [P, DC, P]) for i in range(2)]
        w_hi = [sb(f"w_hi{i}", [P, DC, P], F32R) for i in range(2)]
        w_lo = [sb(f"w_lo{i}", [P, DC, P], F32R) for i in range(2)]
        zc = sb("zc", [P, 2, T])
        q = sb("q", [P, T])
        k2 = sb("k2", [P, 2, T])
        g2 = sb("g2", [P, 2, T])
        t2 = sb("t2", [P, 2, T])
        b2 = sb("b2", [P, 2, T])
        e2 = sb("e2", [P, 2, T])
        kd = sb("kdiag", [P, T])
        v = sb("v", [P, NV, T])
        og = sb("og", [P, NV, T])
        ex = sb("ex", [P, 2, NL, T])
        am = [sb(f"am{i}", [P, NL + 1, P]) for i in range(2)]
        tt = sb("tt", [P, NTR, P])
        S = sb("S", [P, 2, NT, DV])
        ebl = sb("ebl", [P, 2, NT])
        pp = [ps(f"pp{i}", [P, 512]) for i in range(2)]
        pA = [ps(f"pA{i}", [P, NL + 1, P]) for i in range(2)]
        pX = ps("pX", [P, 4, P])
        pO = ps("pO", [P, 4, P])
        (w_hi_done, w_lo_done, proj, copied, f_ready, ln_done, b_ready, pool_diff, e_ready, exp_done, qk_ready,
         ex_ready, turned, turned_out, kv, s_done, att, masked, o_done, o_out, s_in, s_out, og_done, og_out) = (
            sem(n) for n in ("w_hi_done", "w_lo_done", "proj", "copied", "f_ready", "ln_done", "b_ready",
                             "pool_diff", "e_ready", "exp_done", "qk_ready", "ex_ready", "turned", "turned_out",
                             "kv", "s_done", "att", "masked", "o_done", "o_out", "s_in", "s_out", "og_done",
                             "og_out"))
        weighted, dve_diff, sig_done, q_sig_done, sp_passed, act_passed = (sem(n) for n in
            ("weighted", "dve_diff", "sig_done", "q_sig_done", "sp_passed", "act_passed"))
        w_loaded = [sem(f"w_loaded{i}") for i in range(2)]
        if mx.gla:
            wg = sb("wg", [P, 2, P])
            lowT = sb("lowT", [P, T])
            wg_in, wg_zero, conv_done = (sem(n) for n in ("wg_in", "wg_zero", "conv_done"))
        block = s.enter_context(nc.Block())
        PRE = 1 if mx.gla else 0
        per_buf = [len([j for j in range(NCH) if j % 2 == b]) for b in range(2)]
        early_buf = [len([j for j in range(L, NCH) if j % 2 == b]) for b in range(2)]

        def column(h, j):
            _, col0, step = mx.chunks[j]
            return h * step + (col0 + (step if j >= L else 0))

        def loaded_value(h, j):
            b = j % 2
            low = PRE if b == 0 else 0
            return h * (16 * per_buf[b]) + 16 * (low + early_buf[b] + j // 2 + 1)

        def chunks_done(h, j):
            return h * NCH + (PRE + E + j + 1)

        def halves_done(h, turn, i):
            return h * (2 * TURNS) + (2 * (PRE + TURNS - L + turn) + i + 1)

        def before(h, j):
            if j >= 2 and not (isinstance(h, int) and h == -1 and j - 2 < L):
                return 0, j - 2
            if isinstance(h, int) and h == -1:
                return "low" if PRE and j % 2 == 0 else None
            return -1, NCH - 1 if (NCH - 1) % 2 == j else NCH - 2

        def split_free(h, j):
            last = before(h, j)
            return last if last is None else 1 if last == "low" else chunks_done(h, last[0] * NCH + last[1])

        def used(h, j):
            last = before(h, j)
            return last if last is None else 2 if last == "low" else \
                halves_done(h, last[0] * TURNS + last[1], 1)

        def exponents(tensor_tensor, l):
            m = LEVELS[l]
            nb = T // (2 * m)
            bf, bb, qs, ks = (x.rearrange("p (n h m) -> p n h m", h=2, m=m) for x in
                              (b2[:, 0, :], b2[:, 1, :], ex[:, 0, l, :], ex[:, 1, l, :]))
            rf = bf[:, :, 0, m - 1:m].to_broadcast([P, nb, m])
            rb = bb[:, :, 1, 0:1].to_broadcast([P, nb, m])
            tensor_tensor(qs[:, :, 1, :], bf[:, :, 1, :], rf, ALU.subtract)
            tensor_tensor(ks[:, :, 0, :], rf, bf[:, :, 0, :], ALU.subtract)
            tensor_tensor(qs[:, :, 0, :], bb[:, :, 0, :], rb, ALU.subtract)
            tensor_tensor(ks[:, :, 1, :], rb, bb[:, :, 1, :], ALU.subtract)

        @block.sync
        def _(sp):
            def load(h, j):
                if split_free(h, j) is not None:
                    sp.wait_ge(w_lo_done, split_free(h, j))
                    alone(sp, sp_passed)
                sp.dma_start(w_raw[j % 2][:, :, :], w_in[:, :, bass.ds(column(h, j), P)]) \
                    .then_inc(w_loaded[j % 2], 16)

            def load_gates(h):
                for d in range(2):
                    sp.dma_start(wg[96 + 16 * d:112 + 16 * d, d, :],
                                 a["gla_w_gate"][0, d][:, bass.ds(h * P, P)]).then_inc(wg_in, 16)

            def head(h, final):
                sp.wait_ge(o_done, h * NT + 1)
                alone(sp, sp_passed)
                sp.wait_ge(s_out, h * 32 + 32)
                sp.dma_start(S[:, 0, 0, :], s0[0][bass.ds(h, 1)].rearrange("o p v -> p (o v)")).then_inc(s_in, 16)
                sp.dma_start(S[:, 1, 3, :], s0[1][bass.ds(h, 1)].rearrange("o p v -> p (o v)")).then_inc(s_in, 16)
                for j in range(2, NCH):
                    if j < L or not final:
                        load(h, j)
                if mx.gla and not final:
                    sp.wait_ge(proj, halves_done(h, -1, 1))
                    alone(sp, sp_passed)
                    load_gates(h + 1)
                sp.wait_ge(og_done, h + 1)
                sp.dma_start(og_sp[bass.ds(h * NV, NV)].rearrange("n p t -> p n t"), og[:, :, :]).then_inc(og_out, 16)
                if not final:
                    load(h + 1, 0)
                    load(h + 1, 1)
                sp.wait_ge(s_done, h * 8 + 8)
                for d in range(2):
                    sp.dma_start(s_new[d][bass.ds(h, 1)].rearrange("o p v -> p (o v)"), S[:, d, 4, :]) \
                        .then_inc(s_out, 16)

            sp.sem_inc(s_out, 32)
            sp.sem_inc(og_out, 16)
            if mx.gla:
                sp.dma_start(w_raw[0][:, :, :], w_in[:, :, 3104 - P:3104]).then_inc(w_loaded[0], 16)
                sp.wait_ge(wg_zero, 1)
                load_gates(0)
            for j in range(L, NCH):
                load(-1, j)
            load(0, 0)
            load(0, 1)
            with sp.Fori(0, H - 1) as h:
                head(h, False)
            head(H - 1, True)
            sp.wait_ge(s_out, 32 * H + 32)
            sp.wait_ge(og_out, 16 * H + 16)

        @block.gpsimd
        def _(pool):
            def lo(h, j):
                pool.wait_ge(w_hi_done, chunks_done(h, j))
                b = j % 2
                pool.tensor_tensor(w_lo[b][:, :, :], w_raw[b][:, :, :], w_hi[b][:, :, :].bitcast(F32),
                                   ALU.subtract).then_inc(w_lo_done, 1)

            def head(h, final):
                for j in range(2, min(4, NCH)):
                    if j < L or not final:
                        lo(h, j)
                pool.wait_ge(b_ready, h + 1)
                for l in range(POOL_LEVELS):
                    exponents(pool.tensor_tensor, l)
                    pool.drain().then_inc(pool_diff, 1)
                if not final:
                    for j in range(4, NCH):
                        lo(h, j)
                    lo(h + 1, 0)
                    lo(h + 1, 1)

            if mx.gla:
                pool.memset(wg[:, :, :], 0.0)
                pool.drain().then_inc(wg_zero, 1)
                pool.wait_ge(w_hi_done, 1)
                pool.tensor_tensor(w_lo[0][:, :, :], w_raw[0][:, :, :], w_hi[0][:, :, :].bitcast(F32),
                                   ALU.subtract).then_inc(w_lo_done, 1)
            for j in range(L, NCH):
                lo(-1, j)
            lo(0, 0)
            lo(0, 1)
            with pool.Fori(0, H - 1) as h:
                head(h, False)
            head(H - 1, True)

        @block.scalar
        def _(act):
            def hi(h, j):
                b = j % 2
                act.wait_ge(w_loaded[b], loaded_value(h, j))
                if used(h, j) is not None:
                    act.wait_ge(proj, used(h, j))
                act.activation(w_hi[b][:, :, :], w_raw[b][:, :, :], ACT.Copy).then_inc(w_hi_done, 1)

            def next_hi(h, j, final):
                if j + 2 < NCH:
                    if j + 2 < L or not final:
                        hi(h, j + 2)
                elif not final:
                    if NCH % 2 == 0:
                        hi(h + 1, j + 2 - NCH)
                    elif j == NCH - 1:
                        hi(h + 1, 0)
                        hi(h + 1, 1)

            def copy(dst, turn, h, func=ACT.Copy, bias=None):
                for i, cols in halves():
                    act.wait_ge(proj, halves_done(h, turn, i))
                    if bias is not None:
                        alone(act, act_passed)
                    kw = {"bias": bias} if bias is not None else {}
                    act.activation(dst[:, cols], pp[i][:, 0:HALF], func, **kw).then_inc(copied, 1)

            def early(h, n):
                if mx.gla and n >= E:
                    d = n - E
                    bg = VEC["b_gate"] + 4 * d
                    copy(g2[:, d, :], L + n, h, ACT.Identity, bias=c["vec"][:, bass.ds(h + (bg + 1), 1)])
                    return
                if mx.gla:
                    copy(zc[:, n, :], L + n, h)
                elif n < 2:
                    copy(g2[:, n, :], L + n, h)
                else:
                    copy(zc[:, 0, :], L + n, h)
                next_hi(h, L + n, False)

            def output_gates(h, n, final):
                if n == 0:
                    act.wait_ge(og_out, h * 16 + 16)
                copy(og[:, n, :], NV + n, h)
                next_hi(h, NV + n, final)

            def head(h, final):
                if mx.gla:
                    act.drain()
                    act.activation(b2[:, :, :], g2[:, :, :], ACT.Abs)
                    act.drain()
                    act.activation(b2[:, :, :], b2[:, :, :], ACT.Exp, scale=-1.0)
                    act.drain()
                    act.activation(b2[:, :, :], b2[:, :, :], ACT.Ln, bias=c["one"][:, 0:1])
                    act.drain().then_inc(ln_done, 1)
                    convolved = [k2[:, 0, :], k2[:, 1, :], v[:, 0, :], v[:, 1, :]]

                    def sig(j):
                        act.wait_ge(conv_done, h * 4 + (j + 1))
                        act.activation(t2[:, j % 2, :], convolved[j], ACT.Sigmoid).then_inc(sig_done, 1)

                    for j in range(2):
                        sig(j)
                        copy(zc[:, j, :], j, h)
                        next_hi(h, j, final)
                    output_gates(h, 0, final)
                    sig(2)
                    output_gates(h, 1, final)
                    act.drain().then_inc(og_done, 1)
                    sig(3)
                else:
                    act.drain()
                    act.activation(k2[:, :, :], g2[:, :, :], ACT.Sigmoid, scale=-1.0)
                    act.drain()
                    act.activation(g2[:, :, :], g2[:, :, :], ACT.Sigmoid)
                    act.drain().then_inc(sig_done, 1)
                    act.activation(zc[:, 1, :], zc[:, 0, :], ACT.Sigmoid).then_inc(q_sig_done, 1)
                    copy(v[:, 0, :], 0, h)
                    next_hi(h, 0, final)
                    act.wait_ge(f_ready, h + 1)
                    act.activation(t2[:, :, :], t2[:, :, :], ACT.Ln).then_inc(ln_done, 1)
                    output_gates(h, 0, final)
                    act.drain().then_inc(og_done, 1)
                act.wait_ge(e_ready, h + 1)
                act.activation(e2[:, :, :], b2[:, :, :], ACT.Exp)
                act.activation(t2[:, :, :], t2[:, :, :], ACT.Exp)
                act.drain().then_inc(exp_done, 1)
                if not final:
                    early(h, 0)
                for g in range(NG):
                    n = min(8, NTR - 8 * g)
                    act.wait_ge(turned, h * NG + (g + 1))
                    act.activation(tt[:, 8 * g:8 * g + n, :], pA[g % 2][:, 0:n, :], ACT.Copy).then_inc(turned_out, 1)
                for n, levels in ((1, (0, 1, 2)), (2, (3, 4, 5, 6)), (3, ())):
                    for l in levels:
                        if l < POOL_LEVELS:
                            act.wait_ge(pool_diff, h * POOL_LEVELS + (l + 1))
                        else:
                            act.wait_ge(dve_diff, h * DVE_LEVELS + (l - POOL_LEVELS + 1))
                        act.activation(ex[:, :, l, :], ex[:, :, l, :], ACT.Exp).then_inc(ex_ready, 1)
                    if n < E + mx.extra and not final:
                        early(h, n)
                for t in range(NT):
                    act.wait_ge(o_done, h * NT + (1 + t + 1))
                    act.activation(oT[:, bass.ds(h * NV, NV), t * P:(t + 1) * P],
                                   pO[:, 0:NV, :], ACT.Copy).then_inc(o_out, 1)

            act.sem_inc(o_out, 1)
            if mx.gla:
                act.wait_ge(w_loaded[0], 16)
                act.activation(w_hi[0][:, :, :], w_raw[0][:, :, :], ACT.Copy).then_inc(w_hi_done, 1)
                for i, cols in halves():
                    act.wait_ge(proj, i + 1)
                    act.activation(lowT[:, cols], pp[i][:, 0:HALF], ACT.Copy).then_inc(copied, 1)
            hi(-1, L)
            hi(-1, L + 1)
            for n in range(E + mx.extra):
                early(-1, n)
            with act.Fori(0, H - 1) as h:
                head(h, False)
            head(H - 1, True)

        @block.vector
        def _(dve):
            if mx.gla:
                convolved = [k2[:, 0, :], k2[:, 1, :], v[:, 0, :], v[:, 1, :]]
                dests = [k2[:, 0, :], q[:, :], v[:, 0, :], v[:, 1, :]]
                where = [(4, 1), (0, 1), (8, 2), (9, 2)]
                scales = [1.0, float(P) ** -0.5, 1.0, 1.0]

            def conv(h, j, half):
                dst, tap0, zsl = convolved[j], where[j], zc[:, j % 2, :]
                taps = [(y, x) for y in range(3) for x in range(3) if (y, x) != (1, 1)]
                if half == 0:
                    nc.vector.tensor_scalar(dst, zsl, tap_ap(h, 1, 1, tap0), None, ALU.mult)
                    dve.drain()
                gz = zsl[:, 0:TS].rearrange("p (r w) -> p r w", w=GRID_W)
                gd = dst[:, 0:TS].rearrange("p (r w) -> p r w", w=GRID_W)
                for y, x in taps[4 * half:4 * half + 4]:
                    r0, r1 = max(0, 1 - y), min(ROWS, ROWS + 1 - y)
                    w0, w1 = max(0, 1 - x), min(GRID_W, GRID_W + 1 - x)
                    if y == 1:
                        u0, u1 = TS + max(0, 1 - x), TS + min(TC, TC + 1 - x)
                        nc.vector.scalar_tensor_tensor(dst[:, u0:u1], zsl[:, u0 + x - 1:u1 + x - 1],
                                                       tap_ap(h, y, x, tap0), dst[:, u0:u1], ALU.mult, ALU.add)
                    nc.vector.scalar_tensor_tensor(
                        gd[:, r0:r1, w0:w1], gz[:, r0 + y - 1:r1 + y - 1, w0 + x - 1:w1 + x - 1],
                        tap_ap(h, y, x, tap0), gd[:, r0:r1, w0:w1], ALU.mult, ALU.add)
                    dve.drain()
                if half:
                    dve.drain().then_inc(conv_done, 1)

            def scan(h):
                nc.vector.tensor_tensor_scan(b2[:, 0, :], c["scan_f"][:, :], g2[:, 0, :], 0.0, ALU.mult, ALU.add)
                nc.vector.tensor_tensor_scan(b2[:, 1, ::-1], c["scan_b"][:, ::-1], g2[:, 1, ::-1], 0.0,
                                             ALU.mult, ALU.add)
                dve.drain().then_inc(b_ready, 1)

            def tap_ap(h, y, x, tap0):
                n = 3 * y + x
                first = (VEC["conv"] + 16 * n if n < 8 else VEC["conv8"]) + tap0[0]
                return c["vec"][:, bass.ds(h * tap0[1] + first, 1)]

            dve.sem_inc(masked, 1)
            def head(h, final):
                if mx.gla:
                    def silu(j):
                        dve.wait_ge(sig_done, h * 4 + (j + 1))
                        nc.vector.scalar_tensor_tensor(dests[j], convolved[j], scales[j], t2[:, j % 2, :],
                                                       ALU.mult, ALU.mult)
                        dve.drain()

                    dve.wait_ge(ln_done, h + 1)
                    nc.vector.scalar_tensor_tensor(g2[:, :, :], g2[:, :, :], 0.0, b2[:, :, :],
                                                   ALU.min, ALU.subtract)
                    dve.drain()
                    nc.vector.tensor_scalar(g2[:, :, :], g2[:, :, :], 1.0 / 16.0, None, ALU.mult)
                    dve.drain()
                    scan(h)
                    silu(0)
                    silu(1)
                    for j in (2, 3):
                        dve.wait_ge(copied, halves_done(h, j - 2, 1))
                        conv(h, j, 0)
                        conv(h, j, 1)
                    silu(2)
                    silu(3)
                    nc.vector.tensor_scalar(kd[:, :], k2[:, 0, :], 2.0, None, ALU.mult)
                    nc.vector.tensor_copy(k2[:, 1, :], k2[:, 0, :])
                    dve.drain()
                else:
                    dve.wait_ge(sig_done, h + 1)
                    for d in range(2):
                        oml = c["oml"][:, bass.ds(h + 8 * d, 1)]
                        nc.vector.tensor_scalar(t2[:, d, :], g2[:, d, :], oml, c["lb"][:, bass.ds(h + 8 * d, 1)],
                                                ALU.mult, ALU.add)
                        nc.vector.tensor_scalar(k2[:, d, :], k2[:, d, :], oml, None, ALU.mult)
                    dve.drain()
                    nc.vector.tensor_scalar(t2[:, :, :], t2[:, :, :], F_MIN, None, ALU.max)
                    dve.drain()
                    nc.vector.tensor_scalar(g2[:, :, :], t2[:, :, :], LN_LOW, LN_UP, ALU.is_lt, ALU.mult)
                    dve.drain()
                    nc.vector.scalar_tensor_tensor(t2[:, :, :], g2[:, :, :], 1.0, t2[:, :, :], ALU.add, ALU.mult)
                    dve.drain().then_inc(f_ready, 1)
                    nc.vector.tensor_add(kd[:, :], k2[:, 0, :], k2[:, 1, :])
                    dve.wait_ge(q_sig_done, h + 1)
                    nc.vector.tensor_mul(q[:, :], zc[:, 0, :], zc[:, 1, :])
                    dve.wait_ge(ln_done, h + 1)
                    nc.vector.scalar_tensor_tensor(g2[:, :, :], g2[:, :, :], LN_FIX, t2[:, :, :], ALU.mult, ALU.add)
                    dve.drain()
                    scan(h)
                for d, e in ((0, P - 1), (1, 0)):
                    bv = b2[:, d, :].rearrange("p (n t) -> p n t", t=P)
                    nc.vector.tensor_tensor(t2[:, d, :].rearrange("p (n t) -> p n t", t=P),
                                            bv[:, :, e:e + 1].to_broadcast([P, NT, P]), bv, ALU.subtract)
                dve.drain().then_inc(e_ready, 1)
                dve.wait_ge(exp_done, h + 1)
                for d, e in ((0, P - 1), (1, 0)):
                    nc.vector.tensor_copy(ebl[:, d, :], e2[:, d, :].rearrange("p (n t) -> p n t", t=P)[:, :, e])
                dve.drain()
                for d in range(2):
                    nc.vector.tensor_mul(e2[:, d, :], e2[:, d, :], q[:, :])
                    nc.vector.tensor_mul(t2[:, d, :], t2[:, d, :], k2[:, d, :])
                dve.drain().then_inc(qk_ready, 1)
                for l in range(POOL_LEVELS, NL):
                    exponents(nc.vector.tensor_tensor, l)
                    dve.drain().then_inc(dve_diff, 1)
                dve.wait_ge(s_in, h * 32 + 32)
                for i, (d, t) in enumerate(WITH_STATE):
                    dve.wait_ge(kv, h * 8 + (i // KVR + 1) * KVR)
                    r = (i % KVR) * NV
                    update = (pX, pO)[i // KVR % 2][:, r:r + NV, :].rearrange("p a b -> p (a b)")
                    if t == NT - 1:
                        nc.vector.tensor_copy(S[:, d, t, :], update)
                    else:
                        nxt = t + 1 if d == 0 else t - 1
                        nc.vector.scalar_tensor_tensor(S[:, d, nxt, :], S[:, d, t, :], ebl[:, d, t:t + 1],
                                                       update, ALU.mult, ALU.add)
                    dve.drain().then_inc(s_done, 1)
                for l, m in enumerate(LEVELS):
                    dve.wait_ge(ex_ready, h * NL + (l + 1))
                    nc.vector.tensor_mul(ex[:, 0, l, :], ex[:, 0, l, :], q[:, :])
                    for d in range(2):
                        kv_ = k2[:, d, :].rearrange("p (n h m) -> p n h m", h=2, m=m)[:, :, d, :]
                        ks = ex[:, 1, l, :].rearrange("p (n h m) -> p n h m", h=2, m=m)[:, :, d, :]
                        nc.vector.tensor_mul(ks, ks, kv_)
                dve.drain().then_inc(weighted, 1)
                for t in range(NT):
                    dve.wait_ge(att, h * NT + (t + 1))
                    dve.wait_ge(o_done, h * NT + (1 + (t - 1 if t >= 2 else 0)))
                    nc.vector.tensor_mul(am[t % 2][:, :, :], pA[t % 2][:, :, :], c["level_mask"][:, :, :]) \
                        .then_inc(masked, 1)
                    if mx.gla and not final and t < 4:
                        dve.wait_ge(copied, halves_done(h, L + t // 2, 1))
                        conv(h + 1, t // 2, t % 2)

            if mx.gla:
                for j in range(2):
                    dve.wait_ge(copied, halves_done(-1, L + j, 1))
                    conv(0, j, 0)
                    conv(0, j, 1)
            with dve.Fori(0, H - 1) as h:
                head(h, False)
            head(H - 1, True)

        @block.tensor
        def _(pe):
            pe.sem_inc(o_done, 1)

            def free(h, turn, i):
                if not (isinstance(h, int) and h == -1 and PRE == 0 and turn == L):
                    pe.wait_ge(copied, halves_done(h, turn - 1, i))

            def project(h, j):
                pe.wait_ge(w_lo_done, chunks_done(h, j))
                for i, cols in halves():
                    free(h, j, i)
                    split_product(nc, pp[i][:, 0:HALF], w_hi[j % 2], w_lo[j % 2], h_hi, h_lo, cols).then_inc(proj, 1)

            def project_early(h):
                for j in range(L + 1, NCH):
                    project(h, j)
                if mx.gla:
                    pe.wait_ge(wg_in, h * 32 + 64)
                    for d in range(2):
                        for i, cols in halves():
                            free(h, NCH + d, i)
                            nc.tensor.matmul(pp[i][:, 0:HALF], wg[96:128, d, :], lowT[96:128, cols],
                                             start=True, stop=True).then_inc(proj, 1)

            def head(h, final):
                for j in range(L):
                    project(h, j)
                if not final:
                    project(h, L)
                pe.wait_ge(qk_ready, h + 1)
                for g in range(NG):
                    if g >= 2:
                        pe.wait_ge(turned_out, h * NG + (g - 1))
                    for r in range(min(8, NTR - 8 * g)):
                        n = 8 * g + r
                        if n < 10:
                            src = t2[:, n // NT, (n % NT) * P:(n % NT + 1) * P]
                        else:
                            t, vv = (n - 10) // NV, (n - 10) % NV
                            src = v[:, vv, t * P:(t + 1) * P]
                        last = nc.tensor.transpose(pA[g % 2][:, r, :], src, c["ident"][:, :])
                    last.then_inc(turned, 1)
                pe.wait_ge(turned_out, h * NG + NG)
                pe.wait_ge(o_out, h * NT + 1)
                for i, (d, t) in enumerate(WITH_STATE):
                    if i >= 2 * KVR and i % KVR == 0:
                        pe.wait_ge(s_done, h * 8 + (i - KVR))
                    r = (i % KVR) * NV
                    nc.tensor.matmul((pX, pO)[i // KVR % 2][:, r:r + NV, :], tt[:, d * NT + t, :],
                                     tt[:, 10 + t * NV:10 + t * NV + NV, :], start=True, stop=True).then_inc(kv, 1)
                if not final:
                    project_early(h)
                pe.wait_ge(weighted, h + 1)
                pe.wait_ge(s_done, h * 8 + 8)

                def scores(t):
                    pe.wait_ge(masked, h * NT + (1 + (t - 1 if t >= 2 else 0)))
                    tok = slice(t * P, (t + 1) * P)
                    for l in range(NL):
                        nc.tensor.matmul(pA[t % 2][:, l, :], ex[:, 1, l, tok], ex[:, 0, l, tok], start=True, stop=True)
                    nc.tensor.matmul(pA[t % 2][:, NL, :], kd[:, tok], q[:, tok], start=True, stop=True) \
                        .then_inc(att, 1)

                scores(0)
                for t in range(NT):
                    if t + 1 < NT:
                        scores(t + 1)
                    pe.wait_ge(masked, h * NT + (1 + t + 1))
                    pe.wait_ge(o_out, h * NT + (1 + t))
                    tok = slice(t * P, (t + 1) * P)
                    for vv in range(NV):
                        dst = pO[:, vv, :]
                        terms = [(tt[:, 10 + t * NV + vv, :], am[t % 2][:, l, :]) for l in range(NL + 1)]
                        if t < NT - 1:
                            terms += [(S[:, d, t, vv * P:(vv + 1) * P], e2[:, d, tok]) for d in range(2)]
                        for n, (lhsT, rhs) in enumerate(terms):
                            last = nc.tensor.matmul(dst, lhsT, rhs, start=(n == 0), stop=(n == len(terms) - 1))
                    last.then_inc(o_done, 1)

            if mx.gla:
                pe.wait_ge(w_lo_done, 1)
                for i, cols in halves():
                    split_product(nc, pp[i][:, 0:HALF], w_hi[0], w_lo[0], h_hi, h_lo, cols).then_inc(proj, 1)
            project(-1, L)
            project_early(-1)
            with pe.Fori(0, H - 1) as h:
                head(h, False)
            head(H - 1, True)


def mix_out(nc, a, c, mx, h_hi, h_lo, oT, og_sp, x_sp, layer):
    NV, H = mx.nv, mx.heads
    w_out = a["gla_w_out" if mx.gla else "hgrn_w_out"][0].rearrange("(k p) n -> p k n", p=P)
    gw = VEC["gla_g" if mx.gla else "hgrn_g"]
    with ExitStack() as s:
        sb = lambda n, sh, dt=F32: s.enter_context(nc.sbuf_tensor(f"{n}_mo{layer}", sh, dt))
        sem = stage_semaphores(nc, s, f"_mo{layer}")
        ps = lambda n, sh: s.enter_context(nc.psum_tensor(f"{n}_mo{layer}", sh, F32))
        xT = sb("x", [P, DC, T])
        og = sb("og", [P, DC, T])
        sg = [sb(f"sg{i}", [P, T]) for i in range(2)]
        sq = [sb(f"sq{i}", [P, T]) for i in range(2)]
        rs = [sb(f"rs{i}", [P, T]) for i in range(2)]
        y = [sb(f"y{i}", [P, T]) for i in range(2)]
        w_raw = [sb(f"w_raw{i}", [P, DC, P]) for i in range(2)]
        w_hi = [sb(f"w_hi{i}", [P, DC, P], F32R) for i in range(2)]
        w_lo = [sb(f"w_lo{i}", [P, DC, P], F32R) for i in range(2)]
        ms = [[ps(f"ms{g}_{i}", [P, 512]) for i in range(2)] for g in range(2)]
        pp = [ps(f"pp{i}", [P, 512]) for i in range(4)]
        (x_in, sig_done, silu_done, sq_done, summed, ms_out, inv, rooted, y_done, hi_done, lo_done,
         w_hi_done, w_lo_done, proj, added, x_out) = (sem(n) for n in (
            "x_in", "sig_done", "silu_done", "sq_done", "summed", "ms_out", "inv", "rooted", "y_done",
            "hi_done", "lo_done", "w_hi_done", "w_lo_done", "proj", "added", "x_out"))
        og_in = [sem(f"og_in{i}") for i in range(4)]
        w_loaded = [sem(f"w_loaded{i}") for i in range(2)]
        block = s.enter_context(nc.Block())

        @block.sync
        def _(sp):
            for i in range(4):
                sp.dma_start(og[:, 2 * i:2 * i + 2, :], og_sp[2 * i:2 * i + 2].rearrange("k p t -> p k t")) \
                    .then_inc(og_in[i], 16)
            sp.dma_start(xT[:, :, :], x_sp).then_inc(x_in, 16)
            with sp.Fori(0, DC // 2) as i:
                for b in range(2):
                    sp.wait_ge(w_lo_done, i * 2 + (b + 1))
                    sp.dma_start(w_raw[b][:, :, :], w_out[:, :, bass.ds(i * (2 * P) + b * P, P)]) \
                        .then_inc(w_loaded[b], 16)
            for k in range(0, DC, 2):
                sp.wait_ge(added, 4 + 2 * (k + 2))
                sp.dma_start(x_sp[:, k:k + 2, :], xT[:, k:k + 2, :]).then_inc(x_out, 16)
            sp.wait_ge(x_out, 16 * DC // 2)

        @block.gpsimd
        def _(pool):
            pool.sem_inc(w_lo_done, 2)
            for k in range(DC):
                pool.wait_ge(sig_done, k + 1)
                pool.tensor_tensor(og[:, k, :], og[:, k, :], sg[k % 2][:, :], ALU.mult).then_inc(silu_done, 1)
            with pool.Fori(0, DC // 2) as i:
                for b in range(2):
                    pool.wait_ge(w_hi_done, i * 2 + (b + 1))
                    pool.tensor_tensor(w_lo[b][:, :, :], w_raw[b][:, :, :], w_hi[b][:, :, :].bitcast(F32),
                                       ALU.subtract).then_inc(w_lo_done, 1)

        @block.scalar
        def _(act):
            def hi(b, i):
                act.wait_ge(w_loaded[b], i * 16 + 16)
                act.wait_ge(proj, i * 4 + (2 * b + 2))
                act.activation(w_hi[b][:, :, :], w_raw[b][:, :, :], ACT.Copy).then_inc(w_hi_done, 1)

            def square(k):
                if k >= 2:
                    act.wait_ge(summed, k - 1)
                act.activation(sq[k % 2][:, :], oT[:, k, :], ACT.Square).then_inc(sq_done, 1)

            def gate(k):
                if k % 2 == 0:
                    act.wait_ge(og_in[k // 2], 16)
                if k >= 2:
                    act.wait_ge(silu_done, k - 1)
                act.activation(sg[k % 2][:, :], og[:, k, :], ACT.Sigmoid).then_inc(sig_done, 1)

            def root(g):
                act.wait_ge(inv, g + 1)
                act.activation(rs[g % 2][:, :], rs[g % 2][:, :], ACT.Sqrt).then_inc(rooted, 1)

            for k in range(2 * NV):
                square(k)
            for k in range(DC):
                gate(k)
            root(0)
            for g in range(H):
                for k in range((g + 2) * NV, min((g + 3) * NV, DC)):
                    square(k)
                if g + 1 < H:
                    root(g + 1)
                for k in range(g * NV, (g + 1) * NV):
                    act.wait_ge(y_done, k + 1)
                    act.activation(h_hi[:, k, :], y[k % 2][:, :], ACT.Copy).then_inc(hi_done, 1)
            with act.Fori(0, DC // 2) as i:
                hi(0, i)
                hi(1, i)

        @block.tensor
        def _(pe):
            pe.sem_inc(proj, 4)
            for k in range(DC):
                pe.wait_ge(sq_done, k + 1)
                if k % NV == 0 and k // NV >= 2:
                    pe.wait_ge(ms_out, k // NV - 1)
                for i, cols in halves():
                    last = nc.tensor.matmul(ms[k // NV % 2][i][:, 0:HALF], c["ones_d"][:, :], sq[k % 2][:, cols],
                                            start=(k % NV == 0), stop=(k % NV == NV - 1))
                last.then_inc(summed, 1)
            pe.wait_ge(lo_done, DC)
            with pe.Fori(0, DC // 2) as n:
                for b in range(2):
                    pe.wait_ge(w_lo_done, n * 2 + (2 + b + 1))
                    for i, cols in halves():
                        pe.wait_ge(added, n * 4 + (2 * b + i + 1))
                        split_product(nc, pp[2 * b + i][:, 0:HALF], w_hi[b], w_lo[b], h_hi, h_lo, cols) \
                            .then_inc(proj, 1)

        @block.vector
        def _(dve):
            dve.sem_inc(added, 4)
            def inverse(g):
                dve.wait_ge(summed, (g + 1) * NV)
                for i, cols in halves():
                    nc.vector.tensor_scalar(rs[g % 2][:, cols], ms[g % 2][i][:, 0:HALF], float(D / mx.dv), EPS,
                                            ALU.mult, ALU.add)
                dve.drain().then_inc(ms_out, 1)
                nc.vector.reciprocal(rs[g % 2][:, :], rs[g % 2][:, :])
                dve.drain().then_inc(inv, 1)

            def split(k):
                dve.wait_ge(hi_done, k + 1)
                nc.vector.tensor_sub(h_lo[:, k, :], y[k % 2][:, :], h_hi[:, k, :].bitcast(F32))
                dve.drain().then_inc(lo_done, 1)

            inverse(0)
            for g in range(H):
                if g + 1 < H:
                    inverse(g + 1)
                dve.wait_ge(rooted, g + 1)
                for k in range(g * NV, (g + 1) * NV):
                    nc.vector.scalar_tensor_tensor(y[k % 2][:, :], oT[:, k, :],
                                                   c["vec"][:, gw + k % NV:gw + k % NV + 1], rs[g % 2][:, :],
                                                   ALU.mult, ALU.mult)
                    dve.wait_ge(silu_done, k + 1)
                    dve.drain()
                    nc.vector.tensor_mul(y[k % 2][:, :], y[k % 2][:, :], og[:, k, :])
                    dve.drain().then_inc(y_done, 1)
                    if k >= 1:
                        split(k - 1)
            split(DC - 1)
            dve.wait_ge(x_in, 16)
            with dve.Fori(0, DC // 2) as n:
                for b in range(2):
                    for i in range(2):
                        dve.wait_ge(proj, n * 4 + (4 + 2 * b + i + 1))
                        src = pp[2 * b + i]
                        k = n * 2 + b
                        for vec, c0, c1 in ((0, 0, HALF),) if i == 0 else ((0, HALF, TS), (1, TS, T)):
                            xs = xT[:, bass.ds(k, 1), c0:c1].rearrange("p o t -> p (o t)")
                            nc.vector.scalar_tensor_tensor(
                                xs, src[:, c0 - i * HALF:c1 - i * HALF],
                                c["mod"][:, layer, bass.ds(k + 16, 1), vec], xs, ALU.mult, ALU.add)
                        dve.drain().then_inc(added, 1)


def retrieve(nc, a, c, h_hi, h_lo, chosen, layer):
    w_q = a["peer_w_q"][layer].rearrange("(k p) n -> p k n", p=P)
    keys = a["peer_keys"][layer]
    NCAND = 88
    LOWEST = -3.0e38
    with ExitStack() as s:
        sb = lambda n, sh, dt=F32: s.enter_context(nc.sbuf_tensor(f"{n}_re{layer}", sh, dt))
        sem = stage_semaphores(nc, s, f"_re{layer}")
        ps = lambda n, sh: s.enter_context(nc.psum_tensor(f"{n}_re{layer}", sh, F32))
        w_raw = [sb(f"w_raw{i}", [P, DC, P]) for i in range(2)]
        w_hi = [sb(f"w_hi{i}", [P, DC, P], F32R) for i in range(2)]
        w_lo = [sb(f"w_lo{i}", [P, DC, P], F32R) for i in range(2)]
        kraw = [sb(f"kraw{i}", [P, P]) for i in range(2)]
        kT = [sb(f"kT{i}", [P, P]) for i in range(2)]
        qT = [sb(f"qT{i}", [P, T]) for i in range(2)]
        top = sb("top", [P, 2, NT, TOPK])
        idx = sb("idx", [P, 2, NT, TOPK], U32)
        rest = sb("rest", [P, NT, P])
        cand = sb("cand", [P, NT, NCAND])
        crest = sb("crest", [P, NT, NCAND])
        ctop = sb("ctop", [P, NT, TOPK])
        cpos = sb("cpos", [P, NT, TOPK], U32)
        pq = [ps(f"pq{i}", [P, 512]) for i in range(2)]
        pk = ps("pk", [P, P])
        pS = [ps(f"pS{i}", [P, 8, P]) for i in range(2)]
        w_hi_done, w_lo_done, proj, q_out, k_turned, k_out, scored, read = (sem(n) for n in
            ("w_hi_done", "w_lo_done", "proj", "q_out", "k_turned", "k_out", "scored", "read"))
        w_loaded = [sem(f"w_loaded{i}") for i in range(2)]
        k_loaded = [sem(f"k_loaded{i}") for i in range(2)]
        dve_passed = sem("dve_passed")
        block = s.enter_context(nc.Block())

        @block.sync
        def _(sp):
            with sp.Fori(0, PH) as h:
                for b in range(2):
                    sp.wait_ge(w_lo_done, h * 2 + (b + 1))
                    sp.dma_start(w_raw[b][:, :, :], w_q[:, :, bass.ds(h * (2 * P) + b * P, P)]) \
                        .then_inc(w_loaded[b], 16)
                    sp.wait_ge(k_turned, h * 2 + (b + 1))
                    sp.dma_start(kraw[b][:, :], keys[bass.ds(h, 1), b].rearrange("o n k -> (o n) k")) \
                        .then_inc(k_loaded[b], 16)

        @block.gpsimd
        def _(pool):
            pool.sem_inc(w_lo_done, 2)
            with pool.Fori(0, PH) as h:
                for b in range(2):
                    pool.wait_ge(w_hi_done, h * 2 + (b + 1))
                    pool.tensor_tensor(w_lo[b][:, :, :], w_raw[b][:, :, :], w_hi[b][:, :, :].bitcast(F32),
                                       ALU.subtract).then_inc(w_lo_done, 1)

        @block.scalar
        def _(act):
            act.sem_inc(k_out, 1)
            act.sem_inc(q_out, 2)

            def hi(h, b):
                act.wait_ge(w_loaded[b], h * 16 + 16)
                act.wait_ge(proj, h * 4 + (2 * b + 2))
                act.activation(w_hi[b][:, :, :], w_raw[b][:, :, :], ACT.Copy).then_inc(w_hi_done, 1)

            def copies(h, b):
                act.wait_ge(scored, h * 2 + (b + 1))
                act.wait_ge(k_turned, h * 2 + (2 + b + 1))
                act.activation(kT[b][:, :], pk[:, :], ACT.Copy).then_inc(k_out, 1)
                for i, cols in halves():
                    act.wait_ge(proj, h * 4 + (4 + 2 * b + i + 1))
                    act.activation(qT[b][:, cols], pq[i][:, 0:HALF], ACT.Copy).then_inc(q_out, 1)

            hi(0, 0)
            hi(0, 1)
            with act.Fori(0, PH - 1) as h:
                for b in range(2):
                    copies(h, b)
                    hi(h + 1, b)
            copies(PH - 1, 0)
            copies(PH - 1, 1)

        @block.tensor
        def _(pe):
            pe.sem_inc(proj, 4)
            pe.sem_inc(k_turned, 2)
            pe.sem_inc(scored, 2)

            def project(h, b):
                pe.wait_ge(k_loaded[b], h * 16 + 16)
                pe.wait_ge(k_out, h * 2 + (1 + b))
                nc.tensor.transpose(pk[:, :], kraw[b][:, :], c["ident"][:, :]).then_inc(k_turned, 1)
                pe.wait_ge(w_lo_done, h * 2 + (2 + b + 1))
                for i, cols in halves():
                    pe.wait_ge(q_out, h * 4 + (1 + 2 * b + i))
                    split_product(nc, pq[i][:, 0:HALF], w_hi[b], w_lo[b], h_hi, h_lo, cols).then_inc(proj, 1)

            def scores(h, b):
                pe.wait_ge(q_out, h * 4 + (2 + 2 * b + 2))
                pe.wait_ge(k_out, h * 2 + (1 + b + 1))
                pe.wait_ge(read, h * 2 + (b + 1))
                for t in range(NT):
                    last = nc.tensor.matmul(pS[b][:, t, :], qT[b][:, t * P:(t + 1) * P], kT[b][:, :],
                                            start=True, stop=True)
                last.then_inc(scored, 1)

            project(0, 0)
            with pe.Fori(0, PH - 1) as h:
                project(h, 1)
                scores(h, 0)
                project(h + 1, 0)
                scores(h, 1)
            project(PH - 1, 1)
            scores(PH - 1, 0)
            scores(PH - 1, 1)

        @block.vector
        def _(dve):
            def best16(values, left, top_, idx_):
                for t in range(NT):
                    nc.vector.max(top_[:, t, 0:8], values(t))
                dve.drain()
                for t in range(NT):
                    nc.vector.max_index(idx_[:, t, 0:8], top_[:, t, 0:8], values(t))
                    nc.vector.match_replace(left[:, t, :], top_[:, t, 0:8], values(t), LOWEST)
                dve.drain()
                for t in range(NT):
                    nc.vector.max(top_[:, t, 8:16], left[:, t, :])
                dve.drain()
                for t in range(NT):
                    nc.vector.max_index(idx_[:, t, 8:16], top_[:, t, 8:16], left[:, t, :])

            dve.sem_inc(read, 2)
            with dve.Fori(0, PH) as h:
                for b in range(2):
                    dve.wait_ge(scored, h * 2 + (2 + b + 1))
                    alone(dve, dve_passed)
                    best16(lambda t: pS[b][:, t, :], rest, top[:, b], idx[:, b])
                    dve.drain().then_inc(read, 1)
                for rows, n, at in ((slice(0, 4), 16, 0), (slice(4, 8), 4, 64), (slice(8, 16), 1, 80)):
                    r = rows.stop - rows.start
                    first = top[:, 0, :, rows].unsqueeze(3).to_broadcast([P, NT, r, n])
                    second = top[:, 1, :, 0:n].unsqueeze(2).to_broadcast([P, NT, r, n])
                    nc.vector.tensor_tensor(cand[:, :, at:at + r * n].rearrange("p t (r n) -> p t r n", n=n),
                                            first, second, ALU.add)
                for f, b in ((2, 0), (3, 1)):
                    nc.vector.tensor_copy(chosen[:, f, bass.ds(h, 1)].rearrange("p o t k -> p (o t k)"),
                                          idx[:, b].rearrange("p t k -> p (t k)"))
                dve.drain()
                best16(lambda t: cand[:, t, :], crest, ctop, cpos)
                dve.drain()
                nc.vector.tensor_copy(chosen[:, 0, bass.ds(h, 1)].rearrange("p o t k -> p (o t k)"),
                                      ctop[:, :, :].rearrange("p t k -> p (t k)"))
                nc.vector.tensor_copy(chosen[:, 1, bass.ds(h, 1)].rearrange("p o t k -> p (o t k)").bitcast(U32),
                                      cpos[:, :, :].rearrange("p t k -> p (t k)"))


def route(nc, c, chosen, gates_dram, ctx_index, ctx_gate, layer):
    NCH_ = PH * TOPK
    UNIT = 8
    RING = 4
    NL_T = NT - 1
    PER = P // UNIT
    PER_STORE = STORE // UNIT
    with ExitStack() as s:
        sb = lambda n, sh, dt=F32: s.enter_context(nc.sbuf_tensor(f"{n}_ro{layer}", sh, dt))
        sem = stage_semaphores(nc, s, f"_ro{layer}")
        ps = lambda n, sh: s.enter_context(nc.psum_tensor(f"{n}_ro{layer}", sh, F32))
        ALLC = [P, PH, NT, TOPK]
        e = sb("e", ALLC)
        esum = sb("esum", [P, PH, NT])
        s4 = sb("s4", ALLC, U32)
        s2 = sb("s2", ALLC, U32)
        posf = sb("posf", ALLC)
        m = sb("m", ALLC)
        rank = [sb(f"rank{i}", [P, NT, PH, TOPK]) for i in range(2)]
        gt = sb("gt", [P, NT, PH, TOPK])
        found = [sb(f"found{i}", [P, NT, NCH_]) for i in range(2)]
        iota16 = sb("iota16", [P, TOPK])
        iota128 = sb("iota128", [P, P])
        eq = [sb(f"eq{i}", [P, NCH_, TOPK]) for i in range(2)]
        turned = sb("turned", [P, 3, T])
        first = [sb(f"first{i}", [P, UNIT, P]) for i in range(RING)]
        second = [sb(f"second{i}", [P, UNIT, P]) for i in range(RING)]
        stage = [sb(f"stage{i}", [P, KEYS, STORE]) for i in range(2)]
        pt = ps("pt", [P, 4, P])
        pg = [ps(f"pg{i}", [P, UNIT, P]) for i in range(2)]
        iot, sub_done, exp_done, compared, eqd, summed, gated, tr, tr_out, first_hot, second_hot, weighed, mm, staged = (sem(n) for n in
            ("iot", "sub_done", "exp_done", "compared", "eqd", "summed", "gated", "tr", "tr_out", "first_hot",
             "second_hot", "weighed", "mm", "staged"))
        stored = [sem(f"stored{i}") for i in range(2)]
        block = s.enter_context(nc.Block())

        @block.gpsimd
        def _(pool):
            pool.iota(iota16[:, :], [[1, TOPK]], base=0, channel_multiplier=0, allow_small_or_imprecise_dtypes=True)
            pool.iota(iota128[:, :], [[1, P]], base=0, channel_multiplier=0, allow_small_or_imprecise_dtypes=True)
            pool.drain().then_inc(iot, 1)

            def weigh(t):
                for b in range(2):
                    pool.wait_ge(compared, 2 * t + b + 1)
                    ev = eq[b][:, :, :].rearrange("p (h k) r -> p h k r", k=TOPK)
                    pool.tensor_tensor(ev, ev, chosen[:, 2 + b, :, t, :].unsqueeze(2).to_broadcast([P, PH, TOPK, TOPK]),
                                       ALU.mult)
                    pool.drain().then_inc(eqd, 1)

            weigh(0)
            for t in range(NT):
                if t + 1 < NT:
                    weigh(t + 1)
                if t == NL_T:
                    break
                with pool.Fori(0, PER // RING) as i:
                    for b in range(RING):
                        pool.wait_ge(first_hot, i * RING + (t * PER + b + 1))
                        gate = turned[:, 2, bass.ds(i * (RING * UNIT) + (t * P + b * UNIT), UNIT)]
                        pool.tensor_tensor(first[b][:, :, :], first[b][:, :, :],
                                           gate.unsqueeze(2).to_broadcast([P, UNIT, P]), ALU.mult).then_inc(weighed, 1)

        @block.vector
        def _(dve):
            pos = chosen[:, 1].bitcast(U32)
            nc.vector.tensor_tensor(e[:, :, :, :], chosen[:, 0], chosen[:, 0, :, :, 0:1].to_broadcast(ALLC), ALU.subtract)
            dve.drain().then_inc(sub_done, 1)
            nc.vector.tensor_scalar(s4[:, :, :, :], pos, 4, None, ALU.logical_shift_right)
            nc.vector.tensor_scalar(s2[:, :, :, :], pos, 2, None, ALU.logical_shift_right)
            nc.vector.tensor_copy(posf[:, :, :, :], pos)
            dve.drain()
            f = lambda x: x[:, :, :, :].rearrange("p h t k -> p (h t k)")
            nc.vector.scalar_tensor_tensor(f(m), f(s2), 12.0, f(s4), ALU.subtract, ALU.max)
            dve.drain()
            nc.vector.scalar_tensor_tensor(f(m), f(posf), 72.0, f(m), ALU.subtract, ALU.max)
            dve.drain()
            for t in range(NT):
                nc.vector.tensor_copy(rank[0][:, t], m[:, :, t, :])
            nc.vector.tensor_scalar(e2v(s4), f(m), 4.0, 48.0, ALU.mult, ALU.add)
            dve.drain()
            nc.vector.scalar_tensor_tensor(e2v(s4), f(m), 16.0, e2v(s4), ALU.mult, ALU.min)
            dve.drain()
            nc.vector.scalar_tensor_tensor(e2v(s4), f(m), 72.0, e2v(s4), ALU.add, ALU.min)
            dve.drain()
            nc.vector.tensor_sub(f(posf), f(posf), e2v(s4))
            dve.drain()
            for t in range(NT):
                nc.vector.tensor_copy(rank[1][:, t], posf[:, :, t, :])
            dve.wait_ge(iot, 1)
            dve.drain()
            dve.wait_ge(exp_done, 1)
            nc.vector.tensor_reduce(esum[:, :, :], e[:, :, :, :], AX.X, ALU.add)
            dve.drain()
            nc.vector.reciprocal(esum[:, :, :], esum[:, :, :])
            dve.drain()
            for t in range(NT):
                nc.vector.tensor_mul(gt[:, t], e[:, :, t, :], esum[:, :, t:t + 1].to_broadcast([P, PH, TOPK]))
            dve.drain().then_inc(gated, 1)

            def compare(t):
                for b in range(2):
                    r = rank[b][:, t].rearrange("p h k -> p (h k)").unsqueeze(2).to_broadcast([P, NCH_, TOPK])
                    nc.vector.tensor_tensor(eq[b][:, :, :], r,
                                            iota16[:, :].unsqueeze(1).to_broadcast([P, NCH_, TOPK]), ALU.is_equal) \
                        .then_inc(compared, 1)

            def sums(t):
                for b in range(2):
                    dve.wait_ge(eqd, 2 * t + b + 1)
                    nc.vector.tensor_reduce(found[b][:, t, :], eq[b][:, :, :], AX.X, ALU.add).then_inc(summed, 1)

            compare(0)
            sums(0)
            for t in range(NT):
                if t + 1 < NT:
                    dve.drain()
                    compare(t + 1)
                if t == NL_T:
                    break
                dve.wait_ge(tr_out, t + 1)
                with dve.Fori(0, PER // RING) as i:
                    for b in range(RING):
                        dve.wait_ge(mm, i * RING + (t * PER + b + 1))
                        for f, dst, done in ((0, first[b], first_hot), (1, second[b], second_hot)):
                            index = turned[:, f, bass.ds(i * (RING * UNIT) + (t * P + b * UNIT), UNIT)]
                            nc.vector.tensor_tensor(dst[:, :, :], iota128[:, :].unsqueeze(1).to_broadcast([P, UNIT, P]),
                                                    index.unsqueeze(2).to_broadcast([P, UNIT, P]), ALU.is_equal) \
                                .then_inc(done, 1)
                if t + 1 < NT:
                    sums(t + 1)

            dve.drain()
            nc.vector.tensor_scalar(found[0][:, NL_T, :], found[0][:, NL_T, :], float(KEYS),
                                    float(layer * KEYS * KEYS), ALU.mult, ALU.add)
            dve.drain()
            nc.vector.tensor_add(found[0][:, NL_T, :], found[0][:, NL_T, :], found[1][:, NL_T, :])
            nc.vector.tensor_copy(ctx_gate[:, :], gt[:, NL_T].rearrange("p h k -> p (h k)"))
            dve.drain()
            for n in range(2):
                nc.vector.tensor_copy(ctx_index[:, n * NCH_:(n + 1) * NCH_], found[0][:, NL_T, :])
            nc.vector.tensor_copy(ctx_index[:, 2 * NCH_:], found[0][:, NL_T, 0:GATHERS])
            dve.drain()

        @block.tensor
        def _(pe):
            pe.sem_inc(mm, RING)

            def turn(t):
                pe.wait_ge(summed, 2 * t + 2)
                pe.wait_ge(gated, 1)
                if t:
                    pe.wait_ge(tr_out, t)
                for n, src in enumerate((found[0][:, t, :], found[1][:, t, :], gt[:, t].rearrange("p h k -> p (h k)"))):
                    last = nc.tensor.transpose(pt[:, n, :], src, c["ident"][:, :])
                last.then_inc(tr, 1)

            for t in range(NL_T):
                turn(t)
                with pe.Fori(0, PER // RING) as i:
                    for b in range(RING):
                        pe.wait_ge(second_hot, i * RING + (t * PER + b + 1))
                        pe.wait_ge(weighed, i * RING + (t * PER + b + 1))
                        pe.wait_ge(staged, i * RING + (t * PER + b + 1))
                        for u in range(UNIT):
                            last = nc.tensor.matmul(pg[b % 2][:, u, :], second[b][:, u, :], first[b][:, u, :],
                                                    start=True, stop=True)
                        last.then_inc(mm, 1)

        @block.scalar
        def _(act):
            act.sem_inc(staged, 2)
            act.wait_ge(sub_done, 1)
            act.activation(e[:, :, :, :], e[:, :, :, :], ACT.Exp).then_inc(exp_done, 1)

            def turn_out(t):
                act.wait_ge(tr, t + 1)
                act.activation(turned[:, :, t * P:(t + 1) * P], pt[:, 0:3, :], ACT.Copy).then_inc(tr_out, 1)

            for t in range(NL_T):
                turn_out(t)
                for half in range(2):
                    if t:
                        act.wait_ge(stored[half], 16 * t)
                    first_step = t * PER + half * PER_STORE
                    with act.Fori(0, PER_STORE // 2) as i:
                        for b in range(2):
                            act.wait_ge(mm, i * 2 + (RING + first_step + b + 1))
                            act.activation(stage[half][:, :, bass.ds(i * (2 * UNIT) + b * UNIT, UNIT)],
                                           pg[b][:, :, :].rearrange("p t i -> p i t"), ACT.Copy).then_inc(staged, 1)

        @block.sync
        def _(sp):
            for n in range(TS // STORE):
                sp.wait_ge(staged, 2 + (n + 1) * PER_STORE)
                sp.dma_start(gates_dram[n], stage[n % 2][:, :, :]).then_inc(stored[n % 2], 16)
            for half in range(2):
                sp.wait_ge(stored[half], 16 * NL_T)


def e2v(x):
    return x[:, :, :, :].rearrange("p h t k -> p (h t k)").bitcast(F32)


def experts(nc, a, c, h_hi, h_lo, x_sp, gates_dram, ctx_index, ctx_gate, layer):
    NE = KEYS
    K = 2
    NC = PH * TOPK
    PAIRS = 8
    LAT = slice(0, TS)
    u_tab = a["peer_u"][layer].rearrange("(n p) d -> n p d", p=P)
    v_tab = a["peer_v"][layer].rearrange("(n p) d -> n p d", p=P)
    with ExitStack() as s:
        sb = lambda n, sh, dt=F32: s.enter_context(nc.sbuf_tensor(f"{n}_ex{layer}", sh, dt))
        sem = stage_semaphores(nc, s, f"_ex{layer}")
        ps = lambda n, sh: s.enter_context(nc.psum_tensor(f"{n}_ex{layer}", sh, F32))
        acc = sb("acc", [P, DC, TS])
        rows = [sb(f"rows{i}", [P, D]) for i in range(GATHERS)]
        now = [sb(f"now{i}", [P, 1], I32) for i in range(GATHERS)]
        h_ctx = sb("h_ctx", [P, D])
        ctx_acc = sb("ctx_acc", [P, D])
        unused = sb("unused", [P, D])
        dot = sb("dot", [P, 1])
        ctx_coef = sb("ctx_coef", [P, PH * TOPK])
        u_raw = [sb(f"u_raw{i}", [P, D]) for i in range(2)]
        v_raw = [sb(f"v_raw{i}", [P, D]) for i in range(2)]
        g_raw = [sb(f"g_raw{i}", [P, TS]) for i in range(2)]
        uT_hi = [sb(f"uT_hi{i}", [P, DC, P], F32R) for i in range(2)]
        uT_lo = [sb(f"uT_lo{i}", [P, DC, P], F32R) for i in range(2)]
        v_hi = [sb(f"v_hi{i}", [P, D], F32R) for i in range(4)]
        v_lo = [sb(f"v_lo{i}", [P, D], F32R) for i in range(4)]
        c_hi = [sb(f"c_hi{i}", [P, TS], F32R) for i in range(4)]
        c_lo = [sb(f"c_lo{i}", [P, TS], F32R) for i in range(4)]
        coef = [sb(f"coef{i}", [P, TS]) for i in range(2)]
        pT = [ps(f"pT{i}", [P, 4, P]) for i in range(2)]
        pu = [ps(f"pu{i}", [P, 512]) for i in range(2)]
        pv = [ps(f"pv{i}", [P, 512]) for i in range(4)]
        (turned, u_hi_done, u_lo_done, dotted, gelu_done, coef_done, c_hi_done, c_lo_done, v_hi_done, v_lo_done,
         v_mm, added, x_in, x_out, x_added) = (sem(n) for n in (
            "turned", "u_hi_done", "u_lo_done", "dotted", "gelu_done", "coef_done", "c_hi_done", "c_lo_done",
            "v_hi_done", "v_lo_done", "v_mm", "added", "x_in", "x_out", "x_added"))
        ctx_turned, ctx_read, index_ready, dotted_ctx, gelu_ctx, ctx_done, ctx_back, dve_passed, pool_passed = (sem(n) for n in
            ("ctx_turned", "ctx_read", "index_ready", "dotted_ctx", "gelu_ctx", "ctx_done", "ctx_back", "dve_passed",
             "pool_passed"))
        row_in = [sem(f"row_in{i}") for i in range(GATHERS)]
        u_in, v_in, g_in = ([sem(f"{n}{i}") for i in range(2)] for n in ("u_in", "v_in", "g_in"))
        block = s.enter_context(nc.Block())
        xT = [buf[:, 0:T] for buf in (*u_raw, *v_raw, *rows)]
        REG = DC
        BANKS = 4

        def half16(n, r):
            if isinstance(n, int):
                return 16 * (n // 2 + 1)
            return n * 8 + (16 - 8 * (r % 2))

        def chunk_of(n, r, scale):
            if isinstance(n, int):
                return scale * (n // 2)
            return n * (scale // 2) - (scale // 2) * (r % 2)

        def schedule(eng, first, step, middle, last):
            first(0)
            step(0, 0, None, None)
            step(1, 1, None, None)
            for turn0, turns in ((0, NC // PAIRS), (NC // PAIRS, (NE - 4) // 4 - NC // PAIRS)):
                with eng.Fori(0, turns) as i:
                    for r in range(4):
                        n = i * 4 + (4 * turn0 + 2 + r)
                        chunk = i * 2 + (2 * turn0 + r // 2) if r % 2 else None
                        step(n, 2 + r, chunk, [(i * PAIRS + (PAIRS * turn0 + 2 * r + e), 2 * r + e, turn0 > 0)
                                               for e in range(2)])
                if turn0 == 0:
                    middle()
            for t in range(2):
                step(NE - 2 + t, 2 + t, NE // 2 - 2 if t else None,
                     [(2 * NC - PAIRS + 4 * t + e, 4 * t + e, True) for e in range(4)])
            last(NE // 2 - 1)

        @block.sync
        def _(sp):
            with sp.Fori(0, NE // 2) as i:
                for b in range(2):
                    n = i * 2 + b
                    sp.wait_ge(turned, n + 1)
                    sp.dma_start(u_raw[b][:, :], u_tab[bass.ds(n, 1)].rearrange("o p d -> (o p) d")).then_inc(u_in[b], 16)
                    sp.wait_ge(v_lo_done, n + 1)
                    sp.dma_start(v_raw[b][:, :], v_tab[bass.ds(n, 1)].rearrange("o p d -> (o p) d")).then_inc(v_in[b], 16)
                    sp.wait_ge(coef_done, n + 1)
                    sp.dma_start(g_raw[b][:, :].rearrange("p (s t) -> p s t", t=STORE),
                                 gates_dram[:, :, bass.ds(n, 1), :].rearrange("s p o t -> p s (o t)")) \
                        .then_inc(g_in[b], 16)
            sp.wait_ge(added, BANKS + REG * NE // K)
            sp.wait_ge(ctx_done, 1)
            for k in range(DC):
                sp.dma_start(xT[k], x_sp[:, k, :]).then_inc(x_in, 16)
            for k in range(DC):
                sp.wait_ge(x_added, k + 1)
                sp.dma_start(x_sp[:, k, :], xT[k]).then_inc(x_out, 16)
            sp.wait_ge(x_out, 16 * DC)

        @block.gpsimd
        def _(pool):
            pool.sem_inc(v_lo_done, 2)

            def step(n, r, chunk, choices):
                pool.wait_ge(v_hi_done, n + 1)
                pool.tensor_tensor(v_lo[r % 4][:, :], v_raw[r % 2][:, :], v_hi[r % 4][:, :].bitcast(F32), ALU.subtract) \
                    .then_inc(v_lo_done, 1)
                for number, place, of_v in choices or ():
                    pool.wait_ge(index_ready, number + 1)
                    alone(pool, pool_passed)
                    slot = place % GATHERS
                    pool.indirect_dma_start(out=rows[slot][:, :], out_offset=None,
                                            in_=a["peer_v" if of_v else "peer_u"].rearrange("l n d -> (l n) d"),
                                            in_offset=bass.IndirectOffsetOnAxis(ap=now[slot][:, 0:1], axis=0)) \
                        .then_inc(row_in[slot], 16)

            schedule(pool, lambda n: None, step, lambda: None, lambda ch: None)

        @block.scalar
        def _(act):
            def turn_hi(n, r):
                act.wait_ge(turned, n + 3)
                act.wait_ge(dotted, n + 1)
                for i in range(2):
                    last_ = act.activation(uT_hi[r % 2][:, 4 * i:4 * i + 4, :], pT[i][:, :, :], ACT.Copy)
                last_.then_inc(u_hi_done, 1)

            def step(n, r, chunk, choices):
                b = r % 2
                if not (isinstance(n, int) and n == NE - 1):
                    turn_hi(n + 1, r + 1)
                act.wait_ge(v_in[b], half16(n, r))
                act.wait_ge(v_mm, chunk_of(n, r, REG) + REG)
                act.activation(v_hi[r % 4][:, :], v_raw[b][:, :], ACT.Copy).then_inc(v_hi_done, 1)
                act.wait_ge(dotted, n + 3)
                act.wait_ge(c_lo_done, n + 1)
                act.activation(coef[b][:, :], pu[b][:, :], ACT.Gelu).then_inc(gelu_done, 1)
                act.wait_ge(coef_done, n + 3)
                act.activation(c_hi[r % 4][:, :], coef[b][:, :], ACT.Copy).then_inc(c_hi_done, 1)

            def middle():
                act.wait_ge(dotted_ctx, 1)
                act.activation(ctx_coef[:, :], ctx_coef[:, :], ACT.Gelu).then_inc(gelu_ctx, 1)

            schedule(act, lambda n: turn_hi(0, 0), step, middle, lambda ch: None)

        @block.vector
        def _(dve):
            dve.sem_inc(coef_done, 2)
            dve.sem_inc(c_lo_done, 2)
            dve.sem_inc(added, BANKS)
            nc.vector.memset(acc[:, :, :], 0.0)
            nc.vector.memset(ctx_acc[:, :], 0.0)
            dve.drain()
            for slot in range(GATHERS):
                nc.vector.tensor_copy(now[slot][:, :], ctx_index[:, slot:slot + 1])
            dve.drain().then_inc(index_ready, GATHERS)
            for g in range(2):
                dve.wait_ge(ctx_turned, g + 1)
                dst = h_ctx[:, 4 * P * g:4 * P * (g + 1)].rearrange("p (k c) -> p k c", c=P)
                nc.vector.tensor_copy(dst, pT[0][:, :, :])
                dve.drain()
                nc.vector.tensor_add(dst, dst, pT[1][:, :, :]).then_inc(ctx_read, 1)
            dve.drain()

            def turn_lo(n, r):
                dve.wait_ge(u_hi_done, n + 1)
                for i in range(2):
                    last_ = nc.vector.tensor_sub(uT_lo[r % 2][:, 4 * i:4 * i + 4, :], pT[i][:, :, :],
                                                 uT_hi[r % 2][:, 4 * i:4 * i + 4, :].bitcast(F32))
                last_.then_inc(u_lo_done, 1)

            def accumulate(chunk, regions=range(REG)):
                for g in regions:
                    dve.wait_ge(v_mm, chunk * REG + (2 * REG + g + 1))
                    nc.vector.tensor_add(acc[:, g, :], acc[:, g, :], pv[g % BANKS][:, :]).then_inc(added, 1)

            def choose(number, place, of_v):
                slot = place % GATHERS
                dve.wait_ge(row_in[slot], number * (16 // GATHERS) + (16 - (16 // GATHERS) * slot))
                alone(dve, dve_passed)
                if of_v:
                    nc.vector.scalar_tensor_tensor(ctx_acc[:, :], rows[slot][:, :],
                                                   ctx_coef[:, bass.ds(number + -NC, 1)], ctx_acc[:, :],
                                                   ALU.mult, ALU.add)
                else:
                    nc.vector.tensor_tensor_reduce(unused[:, :], rows[slot][:, :], h_ctx[:, :], 1.0, 0.0,
                                                   ALU.mult, ALU.add, accum_out=dot[:, :])
                    dve.drain()
                    nc.vector.tensor_copy(ctx_coef[:, bass.ds(number, 1)], dot[:, :])
                nc.vector.tensor_copy(now[slot][:, :], ctx_index[:, bass.ds(number + GATHERS, 1)])
                dve.drain().then_inc(index_ready, 1)

            def step(n, r, chunk, choices):
                b = r % 2
                if not (isinstance(n, int) and n == NE - 1):
                    turn_lo(n + 1, r + 1)
                dve.wait_ge(g_in[b], half16(n, r))
                dve.wait_ge(gelu_done, n + 1)
                nc.vector.tensor_mul(coef[b][:, :], coef[b][:, :], g_raw[b][:, :]).then_inc(coef_done, 1)
                if chunk is not None:
                    accumulate(chunk, [0])
                dve.wait_ge(c_hi_done, n + 1)
                nc.vector.tensor_sub(c_lo[r % 4][:, :], coef[b][:, :], c_hi[r % 4][:, :].bitcast(F32)) \
                    .then_inc(c_lo_done, 1)
                choices = choices or ()
                for m in range(2):
                    if chunk is not None:
                        accumulate(chunk, range(1 + 3 * m, 4 + 3 * m))
                    for choice in choices[m:m + 1]:
                        choose(*choice)
                if chunk is not None:
                    accumulate(chunk, [REG - 1])
                for choice in choices[2:]:
                    choose(*choice)

            def middle():
                dve.drain().then_inc(dotted_ctx, 1)
                dve.wait_ge(gelu_ctx, 1)
                nc.vector.tensor_mul(ctx_coef[:, :], ctx_coef[:, :], ctx_gate[:, :])
                dve.drain()

            def last(chunk):
                dve.drain().then_inc(ctx_done, 1)
                accumulate(chunk)

            schedule(dve, lambda n: turn_lo(0, 0), step, middle, last)
            dve.drain()
            dve.wait_ge(ctx_back, 1)
            dve.wait_ge(x_in, 16 * DC)
            for k in range(DC):
                for v, cols, y in ((0, LAT, acc[:, k, :]), (1, slice(TS, T), pT[k // 4][:, k % 4, :])):
                    nc.vector.scalar_tensor_tensor(xT[k][:, cols], y, c["mod"][:, layer, 40 + k, v:v + 1],
                                                   xT[k][:, cols], ALU.mult, ALU.add)
                dve.drain().then_inc(x_added, 1)

        @block.tensor
        def _(pe):
            pe.sem_inc(turned, 2)
            pe.sem_inc(dotted, 2)
            pe.sem_inc(v_mm, 2 * REG)

            def turn(n, r):
                pe.wait_ge(u_in[r % 2], half16(n, r))
                if not (isinstance(n, int) and n == 0):
                    pe.wait_ge(u_lo_done, n)
                for k in range(DC):
                    last_ = nc.tensor.transpose(pT[k // 4][:, k % 4, :], u_raw[r % 2][:, k * P:(k + 1) * P],
                                                c["ident"][:, :])
                last_.then_inc(turned, 1)

            for g in range(2):
                if g:
                    pe.wait_ge(ctx_read, g)
                for h, part in enumerate((h_hi, h_lo)):
                    for k in range(4):
                        last_ = nc.tensor.transpose(pT[h][:, k, :], part[:, 4 * g + k, TS:T].bitcast(F32),
                                                    c["ident"][:, :])
                last_.then_inc(ctx_turned, 1)
            pe.wait_ge(ctx_read, 2)

            def products(chunk, odd):
                for g in range(REG):
                    pe.wait_ge(added, chunk * REG + (g + 1))
                    terms = []
                    for t in range(K):
                        slot = 2 * odd + t
                        for w, x in ((v_hi, c_hi), (v_hi, c_lo), (v_lo, c_hi)):
                            terms.append((w[slot][:, g * P:(g + 1) * P], x[slot][:, :]))
                    for m, (w, x) in enumerate(terms):
                        last_ = nc.tensor.matmul(pv[g % BANKS][:, :], w, x, start=(m == 0),
                                                 stop=(m == len(terms) - 1))
                    last_.then_inc(v_mm, 1)

            def step(n, r, chunk, choices):
                b = r % 2
                if not (isinstance(n, int) and n == NE - 1):
                    turn(n + 1, r + 1)
                pe.wait_ge(u_lo_done, n + 1)
                if not (isinstance(n, int) and n < 2):
                    pe.wait_ge(gelu_done, n + -1)
                split_product(nc, pu[b][:, :], uT_hi[b], uT_lo[b], h_hi, h_lo, LAT).then_inc(dotted, 1)
                if chunk is not None:
                    pe.wait_ge(v_lo_done, chunk * 2 + 4)
                    pe.wait_ge(c_lo_done, chunk * 2 + 4)
                    products(chunk, slot_pair(r))

            def slot_pair(r):
                return 0 if r % 4 == 3 else 1

            def last(chunk):
                pe.wait_ge(v_lo_done, chunk * 2 + 4)
                pe.wait_ge(c_lo_done, chunk * 2 + 4)
                products(chunk, 1)

            schedule(pe, lambda n: turn(0, 0), step, lambda: None, last)
            pe.wait_ge(ctx_done, 1)
            for k in range(DC):
                last_ = nc.tensor.transpose(pT[k // 4][:, k % 4, :], ctx_acc[:, k * P:(k + 1) * P], c["ident"][:, :])
            last_.then_inc(ctx_back, 1)


def finish(nc, c, x_sp, out):
    with ExitStack() as s:
        sb = lambda n, sh, dt=F32: s.enter_context(nc.sbuf_tensor(f"{n}_fi", sh, dt))
        sem = stage_semaphores(nc, s, f"_fi")
        ps = lambda n, sh: s.enter_context(nc.psum_tensor(f"{n}_fi", sh, F32))
        xT = sb("x", [P, DC, T])
        sq = [sb(f"sq{i}", [P, T]) for i in range(2)]
        rs = sb("rs", [P, T])
        y = sb("y", [P, NT, D])
        ms = [ps(f"ms{i}", [P, 512]) for i in range(2)]
        pt = [ps(f"pt{i}", [P, 4, P]) for i in range(2)]
        x_in, sq_done, summed, inv, rooted, scaled, tr, tr_out, stored = (sem(n) for n in
            ("x_in", "sq_done", "summed", "inv", "rooted", "scaled", "tr", "tr_out", "stored"))
        block = s.enter_context(nc.Block())

        @block.sync
        def _(sp):
            sp.dma_start(xT[:, :, :], x_sp).then_inc(x_in, 16)
            sp.wait_ge(tr_out, 2 * (NT - 1))
            sp.dma_start(out[1].rearrange("o (n p) d -> p (o n) d", p=P), y[:, 0:NT - 1, :]).then_inc(stored, 16)
            sp.wait_ge(tr_out, 2 * NT)
            sp.dma_start(out[0].rearrange("o p d -> (o p) d"), y[:, NT - 1, :]).then_inc(stored, 16)
            sp.wait_ge(stored, 32)

        @block.scalar
        def _(act):
            act.wait_ge(x_in, 16)
            for k in range(DC):
                if k >= 2:
                    act.wait_ge(summed, k - 1)
                act.activation(sq[k % 2][:, :], xT[:, k, :], ACT.Square).then_inc(sq_done, 1)
            act.wait_ge(inv, 1)
            act.activation(rs[:, :], rs[:, :], ACT.Sqrt).then_inc(rooted, 1)
            for n in range(2 * NT):
                act.wait_ge(tr, n + 1)
                act.activation(y[:, n // 2, (n % 2) * 512:(n % 2 + 1) * 512],
                               pt[n % 2][:, :, :].rearrange("p a b -> p (a b)"), ACT.Copy).then_inc(tr_out, 1)

        @block.tensor
        def _(pe):
            for k in range(DC):
                pe.wait_ge(sq_done, k + 1)
                for i, cols in halves():
                    last = nc.tensor.matmul(ms[i][:, 0:HALF], c["ones_d"][:, :], sq[k % 2][:, cols],
                                            start=(k == 0), stop=(k == DC - 1))
                last.then_inc(summed, 1)
            pe.wait_ge(scaled, 1)
            for n in range(2 * NT):
                if n >= 2:
                    pe.wait_ge(tr_out, n - 1)
                for k in range(4):
                    last = nc.tensor.transpose(pt[n % 2][:, k, :],
                                               xT[:, 4 * (n % 2) + k, (n // 2) * P:(n // 2 + 1) * P], c["ident"][:, :])
                last.then_inc(tr, 1)

        @block.vector
        def _(dve):
            dve.wait_ge(summed, DC)
            for i, cols in halves():
                nc.vector.tensor_scalar(rs[:, cols], ms[i][:, 0:HALF], EPS, None, ALU.add)
            dve.drain()
            nc.vector.reciprocal(rs[:, :], rs[:, :])
            dve.drain().then_inc(inv, 1)
            dve.wait_ge(rooted, 1)
            for k in range(DC):
                w = VEC["final"] + k
                nc.vector.scalar_tensor_tensor(xT[:, k, :], xT[:, k, :], c["vec"][:, w:w + 1], rs[:, :],
                                               ALU.mult, ALU.mult)
            dve.drain().then_inc(scaled, 1)


_INS = ["x_prompt", "x_sample", "state_hgrn", "state_gla", "c", "c_ctx", "ada_w", "ada_b", "norm1_w", "norm2_w",
        "final_norm_w", "hgrn_w_in", "hgrn_lb", "hgrn_gnorm_w", "hgrn_w_out", "gla_w_in", "gla_conv_w",
        "gla_w_gate", "gla_b_gate", "gla_gnorm_w", "gla_w_out", "peer_w_q", "peer_keys", "peer_u", "peer_v"]
_OUTS = [(1, TC, D), (1, TS, D), (1, 1, 2, 8, P, P), (1, 1, 2, 4, P, 2 * P)]


def kernel(**inputs):
    import concourse.bacc as bacc
    from concourse.bass_utils import run_bass_kernel_spmd

    nc = bacc.Bacc("TRN2", target_bir_lowering=False, num_devices=1)
    arrays, args = {}, {}
    for name in _INS:
        x = np.ascontiguousarray(inputs[name])
        arrays[f"in_{name}"] = x
        args[name] = nc.dram_tensor(f"in_{name}", x.shape, mybir.dt.from_np(x.dtype), kind="ExternalInput").ap()
    outs = [nc.dram_tensor(f"out_{i}", shape, F32, kind="ExternalOutput").ap() for i, shape in enumerate(_OUTS)]
    build_program(nc, args, outs)
    r = run_bass_kernel_spmd(nc, [arrays], core_ids=[0])
    return tuple(r.results[0][f"out_{i}"] for i in range(len(_OUTS)))
```
